# Optimizing a Trainium2 kernel written in Bass

```python
import jax, jax.numpy as jnp
from jax import lax
import numpy as np

D_MODEL = 1024
BATCH = 1
SEQ = 256
DEPTH = 1

N_MEM = 256
EPS = 1e-5
NEG = -1e30
BIG = 1e30

N_HEADS_A = 8
N_KV_A = 2
HG_A = N_HEADS_A // N_KV_A
DH_A = 64
CMP_BLOCK = 32
CMP_STRIDE = 16
SUB_PER_CMP = CMP_BLOCK // CMP_STRIDE
SLC_BLOCK = 64
SUB_PER_SLC = SLC_BLOCK // CMP_STRIDE
N_SEL = 16
WINDOW = 512
PHI_HIDDEN = 128
Q_BLOCK = 64

N_HEADS_B = 4
DH_B = 128
CONV_K = 4
CHUNK = 64

NSA_Q = N_HEADS_A * DH_A
NSA_KV = N_KV_A * DH_A
NSA_GATES = 3 * N_HEADS_A
M_INNER = N_HEADS_B * DH_B
IN_COLS = NSA_Q + 6 * NSA_KV + NSA_GATES + 2 * M_INNER + 2 * N_HEADS_B + 2 * D_MODEL

N_HEADS_X = 4
DH_X = D_MODEL // N_HEADS_X

N_EXPERTS = 32
TOP_K = 4
D_FF = D_MODEL
SWIGLU_LIMIT = 7.0
SWIGLU_ALPHA = 1.702
MOE_BLOCK = 256

kernel_name = 'hybrid_nsa_mlstm_moe_block'

def rmsnorm(x, g):
    xf = x.astype(jnp.float32)
    y = xf * lax.rsqrt(jnp.mean(xf * xf, axis=-1, keepdims=True) + EPS)
    return (y * g.astype(jnp.float32)).astype(x.dtype)

def nsa_mixer(q, k_cmp, v_cmp, k_slc, v_slc, k_win, v_win, gate_logits,
              pe_k, pe_v, w_phi1_k, w_phi2_k, w_phi1_v, w_phi2_v):
    B, T = q.shape[0], q.shape[1]
    f32 = jnp.float32
    scale = DH_A ** -0.5
    n_sub = T // CMP_STRIDE
    n_cmp = n_sub - SUB_PER_CMP + 1
    n_slc = T // SLC_BLOCK
    n_sel = min(N_SEL, n_slc)

    def compress(kv, pe, w1, w2):
        sub = kv.reshape(B, n_sub, CMP_STRIDE, N_KV_A, DH_A)
        blocks = jnp.concatenate([sub[:, r:r + n_cmp] for r in range(SUB_PER_CMP)], axis=2)
        blocks = blocks + pe[None, None, :, None, :]
        flat = blocks.transpose(0, 1, 3, 2, 4).reshape(B, n_cmp, N_KV_A, CMP_BLOCK * DH_A)
        return jax.nn.gelu(flat @ w1) @ w2

    kc = compress(k_cmp, pe_k, w_phi1_k, w_phi2_k)
    vc = compress(v_cmp, pe_v, w_phi1_v, w_phi2_v)
    cmp_end = jnp.arange(n_cmp) * CMP_STRIDE + (CMP_BLOCK - 1)
    kb = k_slc.reshape(B, n_slc, SLC_BLOCK, N_KV_A, DH_A).transpose(0, 3, 1, 2, 4)
    vb = v_slc.reshape(B, n_slc, SLC_BLOCK, N_KV_A, DH_A).transpose(0, 3, 1, 2, 4)
    kw = jnp.pad(k_win, ((0, 0), (WINDOW, 0), (0, 0), (0, 0)))
    vw = jnp.pad(v_win, ((0, 0), (WINDOW, 0), (0, 0), (0, 0)))
    b_idx = jnp.arange(B)[:, None, None, None]
    g_idx = jnp.arange(N_KV_A)[None, :, None, None]
    blk = jnp.arange(n_slc)
    in_slc = jnp.arange(SLC_BLOCK)
    in_win = jnp.arange(Q_BLOCK + WINDOW)

    def block_fn(i):
        q0 = i * Q_BLOCK
        qb = lax.dynamic_slice_in_dim(q, q0, Q_BLOCK, axis=1)
        t = q0 + jnp.arange(Q_BLOCK)
        s = jnp.einsum('bqghd,bjgd->bgqhj', qb, kc).astype(f32) * scale
        mc = (cmp_end[None, :] <= t[:, None])[None, None, :, None, :]
        p_cmp = jax.nn.softmax(jnp.where(mc, s, NEG), axis=-1) * mc
        o_cmp = jnp.einsum('bgqhj,bjgd->bqghd', p_cmp.astype(vc.dtype), vc)
        pg = jnp.pad(p_cmp.sum(axis=3), ((0, 0), (0, 0), (0, 0), (1, SUB_PER_SLC)))
        imp = sum(pg[..., 1 + m - n::SUB_PER_SLC][..., :n_slc]
                  for m in range(SUB_PER_SLC) for n in range(SUB_PER_CMP))
        cur = t // SLC_BLOCK
        valid = blk[None, :] <= cur[:, None]
        forced = (blk[None, :] == 0) | (blk[None, :] == cur[:, None]) | (blk[None, :] == cur[:, None] - 1)
        score = jnp.where(valid, jnp.where(forced, BIG, imp), NEG)
        _, idx = lax.top_k(score, n_sel)
        ks = kb[b_idx, g_idx, idx]
        vs = vb[b_idx, g_idx, idx]
        kpos = idx[..., None] * SLC_BLOCK + in_slc
        ms = (kpos <= t[None, None, :, None, None])[:, :, :, None]
        s = jnp.einsum('bqghd,bgqskd->bgqhsk', qb, ks).astype(f32) * scale
        s = jnp.where(ms, s, NEG).reshape(B, N_KV_A, Q_BLOCK, HG_A, n_sel * SLC_BLOCK)
        p = jax.nn.softmax(s, axis=-1).reshape(B, N_KV_A, Q_BLOCK, HG_A, n_sel, SLC_BLOCK)
        o_slc = jnp.einsum('bgqhsk,bgqskd->bqghd', p.astype(vs.dtype), vs)
        kwb = lax.dynamic_slice_in_dim(kw, q0, Q_BLOCK + WINDOW, axis=1)
        vwb = lax.dynamic_slice_in_dim(vw, q0, Q_BLOCK + WINDOW, axis=1)
        kp = q0 - WINDOW + in_win
        mw = ((kp[None, :] <= t[:, None]) & (kp[None, :] > t[:, None] - WINDOW)
              & (kp[None, :] >= 0))[None, None, :, None, :]
        s = jnp.einsum('bqghd,bkgd->bgqhk', qb, kwb).astype(f32) * scale
        p = jax.nn.softmax(jnp.where(mw, s, NEG), axis=-1)
        o_win = jnp.einsum('bgqhk,bkgd->bqghd', p.astype(vwb.dtype), vwb)
        return o_cmp, o_slc, o_win

    outs = lax.map(block_fn, jnp.arange(T // Q_BLOCK))

    def unblock(o):
        return o.transpose(1, 0, 2, 3, 4, 5).reshape(B, T, N_KV_A, HG_A, DH_A).astype(f32)

    o_cmp, o_slc, o_win = unblock(outs[0]), unblock(outs[1]), unblock(outs[2])
    g = jax.nn.sigmoid(gate_logits.astype(f32)).reshape(B, T, N_KV_A, HG_A, 3)
    o = g[..., 0, None] * o_cmp + g[..., 1, None] * o_slc + g[..., 2, None] * o_win
    return o.reshape(B, T, NSA_Q).astype(q.dtype)

def mlstm_mixer(x_m, o_pre, i_pre, f_pre, w_conv, b_conv, w_q, w_k, w_v, b_i, b_f, mh_gain, skip):
    B, T, _ = x_m.shape
    f32 = jnp.float32
    n_chunk = T // CHUNK
    xp = jnp.pad(x_m, ((0, 0), (CONV_K - 1, 0), (0, 0)))
    conv = sum(xp[:, r:r + T] * w_conv[r] for r in range(CONV_K)) + b_conv
    x_c = jax.nn.silu(conv)
    xc_h = x_c.reshape(B, T, N_HEADS_B, DH_B)
    xm_h = x_m.reshape(B, T, N_HEADS_B, DH_B)
    q = jnp.einsum('bthd,hde->bthe', xc_h, w_q).astype(f32)
    k = jnp.einsum('bthd,hde->bthe', xc_h, w_k).astype(f32) * (DH_B ** -0.5)
    v = jnp.einsum('bthd,hde->bthe', xm_h, w_v).astype(f32)
    log_f = jax.nn.log_sigmoid((f_pre + b_f).astype(f32))
    log_i = (i_pre + b_i).astype(f32)

    def chunks(a):
        return a.reshape(B, n_chunk, CHUNK, N_HEADS_B, -1).transpose(1, 0, 3, 2, 4)

    causal = jnp.tril(jnp.ones((CHUNK, CHUNK), dtype=bool))

    def step(carry, inp):
        C, n, m = carry
        qc, kc, vc, lf, li = inp
        b = jnp.cumsum(lf, axis=-1)
        log_d = jnp.where(causal, b[..., :, None] - b[..., None, :] + li[..., None, :], NEG)
        m_inter = b + m[..., None]
        m_t = jnp.maximum(log_d.max(axis=-1), m_inter)
        d = jnp.exp(log_d - m_t[..., None])
        s = jnp.einsum('bhtd,bhsd->bhts', qc, kc) * d
        inter = jnp.exp(m_inter - m_t)
        num = jnp.einsum('bhts,bhse->bhte', s, vc) + inter[..., None] * jnp.einsum('bhtd,bhde->bhte', qc, C)
        den = s.sum(axis=-1) + inter * jnp.einsum('bhtd,bhd->bht', qc, n)
        h = num / jnp.maximum(jnp.abs(den), jnp.exp(-m_t))[..., None]
        b_last = b[..., -1]
        log_w = b_last[..., None] - b + li
        m_new = jnp.maximum(b_last + m, log_w.max(axis=-1))
        w = jnp.exp(log_w - m_new[..., None])
        decay = jnp.exp(b_last + m - m_new)
        C_new = decay[..., None, None] * C + jnp.einsum('bhs,bhsd,bhse->bhde', w, kc, vc)
        n_new = decay[..., None] * n + jnp.einsum('bhs,bhsd->bhd', w, kc)
        return (C_new, n_new, m_new), h

    init = (jnp.zeros((B, N_HEADS_B, DH_B, DH_B), f32),
            jnp.zeros((B, N_HEADS_B, DH_B), f32),
            jnp.zeros((B, N_HEADS_B), f32))
    _, h = lax.scan(step, init, (chunks(q), chunks(k), chunks(v),
                                 chunks(log_f[..., None])[..., 0], chunks(log_i[..., None])[..., 0]))
    h = h.transpose(1, 0, 3, 2, 4).reshape(B, T, N_HEADS_B, DH_B)
    h = jax.nn.sigmoid(o_pre.astype(f32)).reshape(B, T, N_HEADS_B, DH_B) * h
    mu = h.mean(axis=-1, keepdims=True)
    var = jnp.mean((h - mu) ** 2, axis=-1, keepdims=True)
    hn = (h - mu) * lax.rsqrt(var + EPS) * mh_gain.astype(f32).reshape(N_HEADS_B, DH_B)
    y = hn.reshape(B, T, M_INNER) + skip.astype(f32) * x_c.astype(f32)
    return y.astype(x_m.dtype)

def token_mixer(h, w_in, pe_cmp_k, pe_cmp_v, w_phi1_k, w_phi2_k, w_phi1_v, w_phi2_v,
                w_conv, b_conv, w_q_m, w_k_m, w_v_m, b_i, b_f, mh_gain, skip_m,
                w_up_a, w_up_b, w_o_mix):
    B, T, _ = h.shape
    proj = h @ w_in
    sizes = [NSA_Q] + [NSA_KV] * 6 + [NSA_GATES, M_INNER, M_INNER, N_HEADS_B, N_HEADS_B, D_MODEL, D_MODEL]
    (q, k_cmp, v_cmp, k_slc, v_slc, k_win, v_win, g_nsa,
     x_m, o_pre, i_pre, f_pre, gate_a, gate_b) = jnp.split(proj, np.cumsum(sizes)[:-1].tolist(), axis=-1)

    def kv(a):
        return a.reshape(B, T, N_KV_A, DH_A)

    y_a = nsa_mixer(q.reshape(B, T, N_KV_A, HG_A, DH_A), kv(k_cmp), kv(v_cmp), kv(k_slc), kv(v_slc),
                    kv(k_win), kv(v_win), g_nsa, pe_cmp_k, pe_cmp_v, w_phi1_k, w_phi2_k, w_phi1_v, w_phi2_v)
    y_b = mlstm_mixer(x_m, o_pre, i_pre, f_pre, w_conv, b_conv, w_q_m, w_k_m, w_v_m, b_i, b_f, mh_gain, skip_m)
    merged = jax.nn.sigmoid(gate_a) * (y_a @ w_up_a) + jax.nn.sigmoid(gate_b) * (y_b @ w_up_b)
    return merged @ w_o_mix

def memory_cross_attention(h, m, w_q, w_k, w_v, w_o):
    B, T, D = h.shape
    M = m.shape[1]
    q = (h @ w_q).reshape(B, T, N_HEADS_X, DH_X)
    k = (m @ w_k).reshape(B, M, N_HEADS_X, DH_X)
    v = (m @ w_v).reshape(B, M, N_HEADS_X, DH_X)
    s = jnp.einsum('bthd,bmhd->bhtm', q, k).astype(jnp.float32) * (DH_X ** -0.5)
    p = jax.nn.softmax(s, axis=-1).astype(v.dtype)
    o = jnp.einsum('bhtm,bmhd->bthd', p, v).reshape(B, T, D)
    return o @ w_o

def moe_ffn(h, w_router, b_router, w_gu, b_gu, w_down, b_down):
    B, T, D = h.shape
    f32 = jnp.float32
    n_tok = B * T
    hf = h.reshape(n_tok, D)
    logits = (hf @ w_router + b_router).astype(f32)
    top_val, top_idx = lax.top_k(logits, TOP_K)
    gate = jax.nn.softmax(top_val, axis=-1)
    n_asg = n_tok * TOP_K
    e_flat = top_idx.reshape(n_asg)
    tok_flat = jnp.repeat(jnp.arange(n_tok, dtype=jnp.int32), TOP_K)
    w_flat = gate.reshape(n_asg)
    order = jnp.argsort(e_flat)
    e_s, tok_s, w_s = e_flat[order], tok_flat[order], w_flat[order]
    counts = jnp.bincount(e_flat, length=N_EXPERTS)
    padded = (counts + MOE_BLOCK - 1) // MOE_BLOCK * MOE_BLOCK
    p_end = jnp.cumsum(padded)
    p_start = p_end - padded
    u_start = jnp.cumsum(counts) - counts
    dest = p_start[e_s] + jnp.arange(n_asg) - u_start[e_s]
    n_blk = -(-n_asg // MOE_BLOCK) + N_EXPERTS
    n_pad = n_blk * MOE_BLOCK
    buf_tok = jnp.full((n_pad,), n_tok, jnp.int32).at[dest].set(tok_s)
    buf_w = jnp.zeros((n_pad,), f32).at[dest].set(w_s)
    blk_exp = jnp.minimum(jnp.searchsorted(p_end, jnp.arange(n_blk) * MOE_BLOCK, side='right'), N_EXPERTS - 1)
    x_buf = jnp.concatenate([hf, jnp.zeros((1, D), hf.dtype)], axis=0)[buf_tok].reshape(n_blk, MOE_BLOCK, D)

    def expert_block(args):
        xb, e = args
        gu = xb @ w_gu[e] + b_gu[e]
        g, u = gu[:, :D_FF], gu[:, D_FF:]
        g = jnp.minimum(g, SWIGLU_LIMIT)
        u = jnp.clip(u, -SWIGLU_LIMIT, SWIGLU_LIMIT)
        return ((u + 1.0) * (g * jax.nn.sigmoid(SWIGLU_ALPHA * g))) @ w_down[e] + b_down[e]

    y_buf = lax.map(expert_block, (x_buf, blk_exp)).reshape(n_pad, D)
    y = jnp.zeros((n_tok + 1, D), y_buf.dtype).at[buf_tok].add(y_buf * buf_w[:, None].astype(y_buf.dtype))
    return y[:n_tok].reshape(B, T, D)

def setup_inputs(seed: int = 0) -> dict:
    key = jax.random.key(seed)
    keys = iter(jax.random.split(key, 40))
    L = DEPTH

    def nrm(shape, scale):
        return jax.random.normal(next(keys), shape, jnp.float32) * scale

    def gain(shape):
        return 1.0 + nrm(shape, 0.02)

    return {
        'x': nrm((BATCH, SEQ, D_MODEL), 1.0),
        'mem': nrm((BATCH, N_MEM, D_MODEL), 1.0),
        'g_mix': gain((L, D_MODEL)),
        'w_in': nrm((L, D_MODEL, IN_COLS), D_MODEL ** -0.5),
        'pe_cmp_k': nrm((L, CMP_BLOCK, DH_A), 0.1),
        'pe_cmp_v': nrm((L, CMP_BLOCK, DH_A), 0.1),
        'w_phi1_k': nrm((L, CMP_BLOCK * DH_A, PHI_HIDDEN), (CMP_BLOCK * DH_A) ** -0.5),
        'w_phi2_k': nrm((L, PHI_HIDDEN, DH_A), PHI_HIDDEN ** -0.5),
        'w_phi1_v': nrm((L, CMP_BLOCK * DH_A, PHI_HIDDEN), (CMP_BLOCK * DH_A) ** -0.5),
        'w_phi2_v': nrm((L, PHI_HIDDEN, DH_A), PHI_HIDDEN ** -0.5),
        'w_conv': nrm((L, CONV_K, M_INNER), CONV_K ** -0.5),
        'b_conv': nrm((L, M_INNER), 0.01),
        'w_q_m': nrm((L, N_HEADS_B, DH_B, DH_B), DH_B ** -0.5),
        'w_k_m': nrm((L, N_HEADS_B, DH_B, DH_B), DH_B ** -0.5),
        'w_v_m': nrm((L, N_HEADS_B, DH_B, DH_B), DH_B ** -0.5),
        'b_i': nrm((L, N_HEADS_B), 0.1),
        'b_f': jnp.linspace(3.0, 6.0, N_HEADS_B)[None, :] + nrm((L, N_HEADS_B), 0.1),
        'mh_gain': gain((L, M_INNER)),
        'skip_m': gain((L, M_INNER)),
        'w_up_a': nrm((L, NSA_Q, D_MODEL), NSA_Q ** -0.5),
        'w_up_b': nrm((L, M_INNER, D_MODEL), M_INNER ** -0.5),
        'w_o_mix': nrm((L, D_MODEL, D_MODEL), D_MODEL ** -0.5),
        'g_x': gain((L, D_MODEL)),
        'g_mem': gain((L, D_MODEL)),
        'w_q_x': nrm((L, D_MODEL, D_MODEL), D_MODEL ** -0.5),
        'w_k_x': nrm((L, D_MODEL, D_MODEL), D_MODEL ** -0.5),
        'w_v_x': nrm((L, D_MODEL, D_MODEL), D_MODEL ** -0.5),
        'w_o_x': nrm((L, D_MODEL, D_MODEL), D_MODEL ** -0.5),
        'g_ffn': gain((L, D_MODEL)),
        'w_router': nrm((L, D_MODEL, N_EXPERTS), D_MODEL ** -0.5),
        'b_router': nrm((L, N_EXPERTS), 0.01),
        'w_gu': nrm((L, N_EXPERTS, D_MODEL, 2 * D_FF), D_MODEL ** -0.5),
        'b_gu': nrm((L, N_EXPERTS, 2 * D_FF), 0.01),
        'w_down': nrm((L, N_EXPERTS, D_FF, D_MODEL), D_FF ** -0.5),
        'b_down': nrm((L, N_EXPERTS, D_MODEL), 0.01),
        'g_final': gain((D_MODEL,)),
    }

def reference(x, mem, g_mix, w_in, pe_cmp_k, pe_cmp_v, w_phi1_k, w_phi2_k, w_phi1_v, w_phi2_v,
              w_conv, b_conv, w_q_m, w_k_m, w_v_m, b_i, b_f, mh_gain, skip_m,
              w_up_a, w_up_b, w_o_mix, g_x, g_mem, w_q_x, w_k_x, w_v_x, w_o_x,
              g_ffn, w_router, b_router, w_gu, b_gu, w_down, b_down, g_final):
    for l in range(DEPTH):
        x = x + token_mixer(rmsnorm(x, g_mix[l]), w_in[l], pe_cmp_k[l], pe_cmp_v[l],
                            w_phi1_k[l], w_phi2_k[l], w_phi1_v[l], w_phi2_v[l],
                            w_conv[l], b_conv[l], w_q_m[l], w_k_m[l], w_v_m[l], b_i[l], b_f[l],
                            mh_gain[l], skip_m[l], w_up_a[l], w_up_b[l], w_o_mix[l])
        x = x + memory_cross_attention(rmsnorm(x, g_x[l]), rmsnorm(mem, g_mem[l]),
                                       w_q_x[l], w_k_x[l], w_v_x[l], w_o_x[l])
        x = x + moe_ffn(rmsnorm(x, g_ffn[l]), w_router[l], b_router[l], w_gu[l], b_gu[l],
                        w_down[l], b_down[l])
    return rmsnorm(x, g_final)


_drawn_inputs = setup_inputs


def setup_inputs(seed=0):
    import zlib

    import numpy as np

    out = dict(_drawn_inputs(seed))
    spreads = {}
    factors = {'pe_cmp_k': 5.581,
     'b_conv': 2.85,
     'b_i': 64.0,
     'skip_m': 2.679,
     'g_x': 5.639,
     'g_mem': 4.929,
     'b_gu': 44.13,
     'b_down': 50.953,
     'g_final': 8.653,
     'g_ffn': 4.985,
     'b_router': 8.0}
    for name, (base, spread) in spreads.items():
        noise = np.random.default_rng([zlib.crc32(name.encode()), seed]).standard_normal(out[name].shape)
        drawn = base * np.exp(spread * noise) if base else spread * noise
        out[name] = __import__('jax').numpy.asarray(drawn.astype(out[name].dtype))
    for name, factor in factors.items():
        out[name] = (out[name] * factor).astype(out[name].dtype)
    return out
```

```python
from contextlib import ExitStack

import concourse.bass as bass
from concourse import mybir

F32 = mybir.dt.float32
I32 = mybir.dt.int32
ALU = mybir.AluOpType
ACT = mybir.ActivationFunctionType
AX = mybir.AxisListType

P = 128
T = 256
TT = T // P
D = 1024
C = D // P
EPS = 1e-5
NEG = -1e30

HA, DA = 8, 64
PAIRS = HA // 2
CMP_BLOCK, CMP_STRIDE = 32, 16
NCMP = T // CMP_STRIDE - 1
CW = 16
HM, DM = 4, 128
HX = 4
NE, TOPK = 32, 4
SLOTS = 64
MORE = T // SLOTS - 1
NBLK = NE + T * TOPK // SLOTS - 1
BCOL = 48
assert NBLK < BCOL

Q0, KC0, VC0, KS0, VS0, KW0, VW0, GN0 = 0, 512, 640, 768, 896, 1024, 1152, 1280
XM0 = GN0 + 3 * HA
OP0 = XM0 + 512
IF0 = OP0 + 512
GA0 = IF0 + 2 * HM
GB0 = GA0 + D
GW = XM0 - KW0
GCOL = GW + 2 * HM

R_MIX, R_X, R_MEM, R_FFN, R_BC, R_WC, R_GAIN, R_SKIP, R_PEK, R_PEV = 0, 8, 16, 24, 32, 36, 52, 56, 64, 96

SLOT_N = 6
SLOT_W = 4096

PIECES = ["q", "kcvs", "kwg", "xm", "phik", "phiv", "op", "ga0", "ga1", "gb0", "gb1",
          "kx0", "kx1", "vx0", "vx1", "ua", "ub", "om0", "om1", "qx0", "qx1", "ox0", "ox1"]
LAST_USE = {"q": "q1", "kcvs": "ksvs", "kwg": "if", "xm": "xm1", "phik": "cmpB", "phiv": "cmpB", "op": "op1",
            "ga0": "ga1", "ga1": "ga3", "gb0": "gb1", "gb1": "gb3", "kx0": "kx1", "kx1": "kx3", "vx0": "vx1",
            "vx1": "vx3", "ua": "ub3", "ub": "ub3", "om0": "om0_1", "om1": "om1_1", "qx0": "qx1", "qx1": "qx3",
            "ox0": "ro0_1", "ox1": "ro1_1"}
DMAS = {"q": 8, "kwg": 2, "phik": 2, "phiv": 2, "ua": 2}
EXPERT_PIECES = ["gu0", "gu1", "gu2", "gu3", "dn0", "dn1"]

FILL = [("ga", n) for n in range(4)] + [("gb", n) for n in range(4)] + \
       [("kx", n) for n in range(4)] + [("vx", n) for n in range(4)]


def filler_names(step):
    return [f"{k}{n}" for k, n in FILL[2 * step:2 * step + 2]]


def group_order():
    g = ["vec", "tm0", "tm1", "tm2", "tm3", "q0", "q1", "kcvc", "ksvs", "kwvw", "gn", "if", "xm0", "xm1",
         "cmpA", "cmpB", "te0", "te1", "te2", "te3", "op0", "op1", "cmp2", "csA", "csB", "mt"]
    for h in range(HA + 1):
        if h >= 1:
            g += [f"ta{h - 1}", f"tb{h - 1}"]
        if h < HA:
            g += [f"sc{h}_0", f"sc{h}_1"] + filler_names(h)[:1]
        if h == 1:
            g += ["mv0", "mv1", "mq0", "mq1", "mq2", "mq3"]
        if 3 <= h <= 6:
            g += [f"mn{h - 3}"]
        if 2 <= h <= 5:
            g += [f"mb{h - 2}", f"ms{h - 2}"]
        if h >= 2 and h % 2 == 0:
            g += [f"pv{h // 2 - 1}"]
        if h < HA:
            g += filler_names(h)[1:]
        if h == HA:
            g += ["ty0", "ty1"]
    for n in range(4):
        g += [f"ua{n}", f"ub{n}"]
    g += ["om0_0", "om0_1", "om1_0", "om1_1"] + [f"tx{n}" for n in range(4)]
    g += [f"qx{n}" for n in range(4)] + [f"sx{h}" for h in range(HX)]
    for h in range(HX):
        g += [f"pt{h}", f"ox{h}"]
    g += ["ro0_0", "ro0_1", "ro1_0", "ro1_1"] + [f"tf{n}" for n in range(4)]
    g += ["rt", "pos", "cnt", "rank", "meta", "blk"]
    return g


GROUPS = group_order()
BANKS = 8
AT = {name: (i % BANKS, i // BANKS) for i, name in enumerate(GROUPS)}
USES = [sum(1 for b, _ in AT.values() if b == k) for k in range(BANKS)]

YB = 0
GBK, UBK, XBK, ZBK = 4, 5, 6, 7


def program(nc, A, out):
    ctx = ExitStack()
    with ctx:
        def sb(name, shape, dt=F32):
            return ctx.enter_context(nc.sbuf_tensor(name, shape, dt))

        def sem(name):
            return ctx.enter_context(nc.semaphore(name))

        ps = ctx.enter_context(nc.psum_tensor("ps", [P, BANKS, 512], F32))

        ring = sb("ring", [P, SLOT_N, SLOT_W])
        r_x = sb("r_x", [P, TT * D])
        r_mem = sb("r_mem", [P, TT * D])
        r_xs = sb("r_xs", [P, TT * D])
        r_hT = sb("r_hT", [P, C * T])
        r_memT = sb("r_memT", [P, C * T])
        r_kx = sb("r_kx", [P, C * T])
        r_ga = sb("r_ga", [P, C * T])
        r_gb = sb("r_gb", [P, C * T])
        r_q = sb("r_q", [P, PAIRS * T])
        r_p = sb("r_p", [P, 2 * 2 * T])
        r_so = sb("r_so", [P, TT * 512])
        r_xm = sb("r_xm", [P, HM * T])
        r_xc = sb("r_xc", [P, HM * T])
        r_tmp = sb("r_tmp", [P, HM * T])
        r_dm = sb("r_dm", [P, 2 * 2 * T])
        kcvc = sb("kcvc", [P, 2, T])
        kskw = sb("kskw", [P, 2, T])
        vsvw = sb("vsvw", [P, 2, TT, P])
        mv = sb("mv", [P, TT, HM, DM + 4])
        vrow = sb("vrow", [P, P])
        vT = sb("vT", [P, P])
        w2 = sb("w2", [P, 2, DA])
        wr = sb("wr", [P, C, NE])
        ident = sb("ident", [P, P])
        ones = sb("ones", [P, T])
        causal = sb("causal", [P, T])
        upper = sb("upper", [P, P])
        sm = sb("sm", [P, 704])
        cnt_i = sb("cnt_i", [1, 32], I32)

        small_at = [0]

        def small(n):
            small_at[0] += n
            assert small_at[0] <= 704
            return sm[:, small_at[0] - n:small_at[0]]

        ss, msq, std, rstd = small(8), small(8), small(8), small(8)
        rmaskc = small(2 * CW).rearrange("p (t j) -> p t j", t=TT)
        mmaskc = small(2 * CW).rearrange("p (t j) -> p t j", t=TT)
        gates = small(TT * 3 * HA).rearrange("p (t h b) -> p t h b", t=TT, b=3)
        hid = small(4 * CW)
        hid2 = small(4 * CW)
        gel = small(4 * CW).rearrange("p (k g j) -> p k g j", k=2, g=2)
        kcT = small(CW)
        bif = small(2)
        cmcol = small(16).rearrange("p (k t h) -> p k t h", k=2, t=TT)
        emcol = small(8).rearrange("p (t h) -> p t h", t=TT)
        nmax = small(4)
        rsum = small(4)
        rinv = small(4)
        fac = small(4)
        cst = small(16)
        den = small(4)
        hsum = small(8)
        hst = small(8)
        brow = small(NE)
        cst2 = small(16)
        lnm = small(8)
        iota_p = small(2)

        x_tok = r_x[:].rearrange("p (t d) -> p t d", t=TT)
        pT = r_x[:].rearrange("p (b k n) -> p b k n", b=2, k=2)
        mem_tok = r_mem[:].rearrange("p (t d) -> p t d", t=TT)
        vx = mem_tok
        xs = r_xs[:].rearrange("p (t d) -> p t d", t=TT)
        mqk = r_xs[:].rearrange("p (h k t) -> p h k t", h=HM, k=2)
        hT = r_hT[:].rearrange("p (c t) -> p c t", c=C)
        memT = r_memT[:].rearrange("p (c t) -> p c t", c=C)
        oxT = memT
        kx = r_kx[:].rearrange("p (c t) -> p c t", c=C)
        wm = r_kx[:, 0:3 * HM * DM].rearrange("p (k h e) -> p k h e", k=3, h=HM)
        sga = r_ga[:].rearrange("p (c t) -> p c t", c=C)
        sgb = r_gb[:].rearrange("p (c t) -> p c t", c=C)
        rows = r_gb[0:HM, :].rearrange("p (k t) -> p k t", k=8)
        qx = sgb
        qT = r_q[:].rearrange("p (c t) -> p c t", c=PAIRS)
        yaT = qT
        pr = r_p[:].rearrange("p (t b k) -> p t b k", t=2, b=2)
        pcmp = sb("pcmp", [P, TT, HA, CW])
        vc = kcvc[:, 0, 0:P].rearrange("p (g d) -> p g d", g=2)
        mrow = kcvc[0:HM, 1]
        so = r_so[:].rearrange("p (t d) -> p t d", t=TT)
        xm = r_xm[:].rearrange("p (h t) -> p h t", h=HM)
        ybT = xm
        xc = r_xc[:].rearrange("p (h t) -> p h t", h=HM)
        conv = r_tmp[:].rearrange("p (h t) -> p h t", h=HM)
        hs = r_tmp[:].rearrange("p (t h e) -> p t h e", t=TT, h=HM)
        blocks = r_dm[:, 0:2 * CMP_BLOCK * NCMP].rearrange("p (k s j) -> p k s j", k=2, s=CMP_BLOCK)
        dm = r_dm[:].rearrange("p (b s t) -> p b s t", b=2, s=2)
        px = r_p[:].rearrange("p (t m) -> p t m", t=4)
        pxT = r_dm[:].rearrange("p (b m t) -> p b m t", b=2, m=2)
        junk = {"mix": r_hT, "mem": r_memT, "x": r_hT, "ffn": r_hT}

        lg = r_gb[:, 0:64].rearrange("p (t e) -> p t e", t=TT)
        lgm = r_gb[:, 64:128].rearrange("p (t e) -> p t e", t=TT)
        top = r_gb[:, 128:144].rearrange("p (t e) -> p t e", t=TT)
        mask = r_gb[:, 144:208].rearrange("p (t e) -> p t e", t=TT)
        gexp = r_gb[:, 208:272].rearrange("p (t e) -> p t e", t=TT)
        gate = r_gb[:, 272:336].rearrange("p (t e) -> p t e", t=TT)
        gsum = r_gb[:, 336:340]
        negtop = r_gb[:, 340:342]
        posT = r_gb[0:NE, 352:608]
        gateT = r_gb[0:NE, 608:864]
        cnt = r_gb[0:NE, 864:865]
        ovf = r_gb[0:NE, 868:868 + MORE]
        ovs = r_gb[0:NE, 872:872 + MORE]
        sel3 = r_gb[0:NE, 880:880 + MORE * 16].rearrange("p (c b) -> p c b", c=MORE)
        rank = r_gb[0:NE, 928:928 + MORE]
        blksel = r_gb[0:NE, 944:944 + BCOL]
        blkoff = r_gb[0:NE, 992:992 + BCOL]
        idx16 = r_gb[:, 1040:1056]
        strict = r_gb[:, 1056:1056 + T]
        mT = r_gb[0:NE, 1312:1568]
        metas = r_gb[0:1, 1568:1568 + 32]
        eidx = r_gb[:, 1600:1602]
        lge = r_gb[:, 1608:1672].rearrange("p (t e) -> p t e", t=TT)
        pos_b = r_q[:, 0:TT * BCOL].rearrange("p (t b) -> p t b", t=TT)
        gate_b = r_q[:, TT * BCOL:2 * TT * BCOL].rearrange("p (t b) -> p t b", t=TT)
        iota_s = r_q[:, 256:256 + 2 * SLOTS]
        cur = r_q[0:NE, 400:400 + SLOTS]
        bgu_rows = r_ga[0:NE, :]
        bdn_rows = r_so[0:NE, :]
        gfin = r_xm[:]
        gffn = r_xc[:]
        xg = r_memT[:, 0:512].rearrange("p (c s) -> p c s", c=C)
        gact, uact, sig, hact = (r_memT[:, 512:1024], r_memT[:, 1024:1536], r_memT[:, 1536:2048], r_kx[:, 0:512])
        hactT = r_kx[:, 512:1024].rearrange("p (c n s) -> p c n s", c=4, n=2)
        y_slot = r_kx[:, 1024:1536]
        place = r_dm[:, 0:128].rearrange("p (t s) -> p t s", t=TT)
        placeg = r_dm[:, 128:384].rearrange("p (t s) -> p t s", t=TT)
        scat = r_dm[:, 384:640]

        loaded = [sem(f"loaded{i}") for i in range(SLOT_N)]
        freed = [sem(f"freed{i}") for i in range(SLOT_N)]
        filled = [sem(f"filled{i}") for i in range(BANKS)]
        drained = [sem(f"drained{i}") for i in range(BANKS)]
        vrow_clear, vec_loaded = sem("vrow_clear"), sem("vec_loaded")
        x_loaded, mem_loaded = sem("x_loaded"), sem("mem_loaded")
        small_loaded, wm_loaded, x_again = sem("small_loaded"), sem("wm_loaded"), sem("x_again")
        late_loaded, gfin_loaded, gffn_loaded = sem("late_loaded"), sem("gfin_loaded"), sem("gffn_loaded")
        consts, p_chain = sem("consts"), sem("p_chain")
        v_chain, a_chain = sem("v_chain"), sem("a_chain")
        sq_done, msq_ready = sem("sq_done"), sem("msq_ready")
        std_ready, xs_ready = sem("std_ready"), sem("xs_ready")
        gate_e, blk_ready, gelu_in = sem("gate_e"), sem("blk_ready"), sem("gelu_in")
        gelu_e, gelu_done = sem("gelu_e"), sem("gelu_done")
        fabs_ready, softp_ready = sem("fabs_ready"), sem("softp_ready")
        rows_ready, em_done = sem("rows_ready"), sem("em_done")
        conv_ready, silu_e, xc_ready = sem("conv_ready"), sem("silu_e"), sem("xc_ready")
        cm_in, cm_e, cm_done = sem("cm_in"), sem("cm_e"), sem("cm_done")
        s_max, s_exp = sem("s_max"), sem("s_exp")
        s_fac, s_prob = sem("s_fac"), sem("s_prob")
        dm_e, var_ready, lstd_ready = sem("dm_e"), sem("var_ready"), sem("lstd_ready")
        hn_ready, merged_ready = sem("hn_ready"), sem("merged_ready")
        cx_max, cx_inv, cx_prob = sem("cx_max"), sem("cx_inv"), sem("cx_prob")
        r_top, r_exp, r_gate = sem("r_top"), sem("r_exp"), sem("r_gate")
        r_ovf, r_sel, y_begun = sem("r_ovf"), sem("r_sel"), sem("y_begun")
        place_ready, placeg_ready = sem("place_ready"), sem("placeg_ready")
        gathered, xg_ready = sem("gathered"), sem("xg_ready")
        g_limited, sig_done, h_ready = sem("g_limited"), sem("sig_done"), sem("h_ready")
        cur_ready, ht_done, hT_ready, g_chain = sem("cur_ready"), sem("ht_done"), sem("hT_ready"), sem("g_chain")
        pt_done, scat_ready = sem("pt_done"), sem("scat_ready")
        yslot_ready, scattered = sem("yslot_ready"), sem("scattered")
        fin_sq, fin_v, fin_std = sem("fin_sq"), sem("fin_v"), sem("fin_std")
        out_ready, out_sem = sem("out_ready"), sem("out_sem")

        slot_of, need = {}, {}
        dmas = [0] * SLOT_N
        for n, name in enumerate(PIECES):
            s = n % SLOT_N
            dmas[s] += DMAS.get(name, 1)
            slot_of[name], need[name] = s, 16 * dmas[s]
        eslot = {name: (len(PIECES) + j) % SLOT_N for j, name in enumerate(EXPERT_PIECES)}

        def bank(name):
            return ps[:, AT[name][0], :]

        def drained_of(eng, name):
            b, turn = AT[name]
            eng.wait_ge(drained[b], turn + 1)

        def filled_of(eng, name):
            b, turn = AT[name]
            eng.wait_ge(filled[b], turn + 1)

        def wslot(name, rows_, width):
            return ring[:, slot_of[name], 0:rows_ * width].rearrange("p (c n) -> p c n", c=rows_)

        w_in = A["w_in"][0].rearrange("(c p) n -> p c n", p=P)

        def cols(w, a, b):
            return w[0].rearrange("(c p) n -> p c n", p=P)[:, :, a:b]

        gu_dram = A["w_gu"].rearrange("l e (j k p) n -> (l e) j p k n", k=2, p=P)
        dn_dram = A["w_down"].rearrange("l e (j k p) n -> (l e) j p k n", k=4, p=P)

        block = ctx.enter_context(nc.Block())

        @block.sync
        def _(sp):
            x_dram = A["x"][0].rearrange("(t p) d -> p t d", p=P)
            for t in range(TT):
                sp.dma_start(x_tok[:, t], x_dram[:, t]).then_inc(x_loaded, 16)

            def piece(name):
                s = slot_of[name]
                n = PIECES.index(name)
                if n >= SLOT_N:
                    filled_of(sp, LAST_USE[PIECES[n - SLOT_N]])
                w8 = wslot(name, C, 512)
                if name == "q":
                    pairs = [(w8[:, :, c * P + g * DA:c * P + g * DA + DA],
                              w_in[:, :, Q0 + (g * PAIRS + c) * DA:Q0 + (g * PAIRS + c + 1) * DA])
                             for c in range(PAIRS) for g in range(2)]
                elif name == "kcvs":
                    pairs = [(w8, w_in[:, :, KC0:KC0 + 512])]
                elif name == "kwg":
                    w = wslot(name, C, GCOL)
                    pairs = [(w[:, :, 0:GW], w_in[:, :, KW0:XM0]), (w[:, :, GW:GCOL], w_in[:, :, IF0:GA0])]
                elif name == "xm":
                    pairs = [(w8, w_in[:, :, XM0:XM0 + 512])]
                elif name in ("phik", "phiv"):
                    w = wslot(name, CMP_BLOCK, P)
                    src = A["w_phi1_" + name[-1]][0].rearrange("(s d) n -> d s n", d=DA)
                    pairs = [(w[g * DA:(g + 1) * DA], src) for g in range(2)]
                elif name == "op":
                    pairs = [(w8, w_in[:, :, OP0:OP0 + 512])]
                elif name[:2] in ("ga", "gb"):
                    a = (GA0 if name[1] == "a" else GB0) + 512 * int(name[2])
                    pairs = [(w8, w_in[:, :, a:a + 512])]
                elif name == "ua":
                    w = wslot(name, PAIRS, D)
                    src = A["w_up_a"][0].rearrange("(g c d) n -> g d c n", g=2, d=DA)
                    pairs = [(w[g * DA:(g + 1) * DA], src[g]) for g in range(2)]
                elif name == "ub":
                    pairs = [(wslot(name, HM, D), A["w_up_b"][0].rearrange("(c p) n -> p c n", p=P))]
                else:
                    src = {"kx": "w_k_x", "vx": "w_v_x", "om": "w_o_mix", "qx": "w_q_x", "ox": "w_o_x"}[name[:2]]
                    a = 512 * int(name[2])
                    pairs = [(w8, cols(A[src], a, a + 512))]
                for dst, src in pairs:
                    sp.dma_start(dst, src).then_inc(loaded[s], 16)

            for name in PIECES:
                piece(name)

            def expert(e, i):
                for j, name in enumerate(EXPERT_PIECES):
                    s = eslot[name]
                    if i is None:
                        filled_of(sp, LAST_USE[PIECES[len(PIECES) + j - SLOT_N]])
                    else:
                        sp.wait_ge(freed[s], i)
                    if j < 4:
                        dst, src = ring[:, s].rearrange("p (k n) -> p k n", k=2), gu_dram[e, j]
                    else:
                        dst, src = ring[:, s].rearrange("p (k n) -> p k n", k=4), dn_dram[e, j - 4]
                    sp.dma_start(dst, src).then_inc(loaded[s], 16)

            expert(0, None)
            with sp.Fori(1, NE) as i:
                expert(i, i)
            drained_of(sp, "meta")
            nblk = sp.value_load(cnt_i[0:1, 0:1], min_val=NE, max_val=NBLK)
            with sp.If(nblk > NE):
                with sp.Fori(NE, nblk) as i:
                    e = sp.value_load(cnt_i[0:1, bass.ds(i - (NE - 1), 1)], min_val=0, max_val=NE - 1)
                    expert(e, i)
            sp.wait_ge(out_ready, 2)
            sp.dma_start(out[0].rearrange("(t p) d -> p t d", p=P), x_tok).then_inc(out_sem, 16)
            sp.wait_ge(out_sem, 16)

        @block.gpsimd
        def _(pool):
            count = [0]

            def link(ins):
                count[0] += 1
                ins.then_inc(p_chain, 1)
                pool.wait_ge(p_chain, count[0])

            pool.memset(vrow[:], 0.0).then_inc(vrow_clear, 1)
            link(pool.memset(ident[:], 0.0))
            pool.memset(ones[:], 1.0)
            pool.memset(sm[:], 0.0)
            pool.memset(cnt_i[:], 0)
            pool.memset(mv[:], 1.0)
            pool.memset(pcmp[:], 0.0)
            pool.memset(causal[:], 0.0)
            link(pool.affine_select(out=ident[:], in_=ident[:], compare_op=ALU.not_equal, fill=1.0, base=0,
                                    pattern=[[-1, P]], channel_multiplier=1))
            pool.affine_select(out=causal[:, P:T], in_=causal[:, P:T], compare_op=ALU.is_ge, fill=NEG, base=0,
                               pattern=[[-1, P]], channel_multiplier=1)
            pool.affine_select(out=upper[:], in_=ones[:, 0:P], compare_op=ALU.is_ge, fill=0.0, base=0,
                               pattern=[[1, P]], channel_multiplier=-1)
            for t in range(TT):
                pool.affine_select(out=rmaskc[:, t], in_=rmaskc[:, t], compare_op=ALU.is_ge, fill=NEG,
                                   base=P * t - (CMP_BLOCK - 1), pattern=[[-CMP_STRIDE, CW]], channel_multiplier=1)
                last = pool.affine_select(out=mmaskc[:, t], in_=ones[:, 0:CW], compare_op=ALU.is_ge, fill=0.0,
                                          base=P * t - (CMP_BLOCK - 1), pattern=[[-CMP_STRIDE, CW]],
                                          channel_multiplier=1)
            last.then_inc(consts, 1)
            filled_of(pool, "pv3")
            pool.dma_start(x_tok, A["x"][0].rearrange("(t p) d -> p t d", p=P)).then_inc(x_again, 16)
            filled_of(pool, "om1_1")
            pool.dma_start(bgu_rows, A["b_gu"][0]).then_inc(late_loaded, 16)
            pool.dma_start(bdn_rows, A["b_down"][0]).then_inc(late_loaded, 16)
            pool.dma_start(gfin, A["g_final"].rearrange("(a d) -> a d", a=1).partition_broadcast(P))\
                .then_inc(gfin_loaded, 16)
            pool.dma_start(gffn, A["g_ffn"].partition_broadcast(P)[:, 0]).then_inc(gffn_loaded, 16)
            filled_of(pool, "sx3")
            pool.iota(idx16, pattern=[[1, 16]], base=0, channel_multiplier=0, allow_small_or_imprecise_dtypes=True)
            pool.iota(eidx, pattern=[[0, 2]], base=0, channel_multiplier=1, allow_small_or_imprecise_dtypes=True)
            pool.iota(iota_s, pattern=[[0, 2], [1, SLOTS]], base=0, channel_multiplier=0, allow_small_or_imprecise_dtypes=True)
            link(pool.memset(blksel, 0.0))
            pool.memset(blkoff, 0.0)
            pool.affine_select(out=blksel[:, 0:NE], in_=blksel[:, 0:NE], compare_op=ALU.not_equal, fill=1.0,
                               base=0, pattern=[[-1, NE]], channel_multiplier=1)
            pool.affine_select(out=strict, in_=ones[:], compare_op=ALU.is_gt, fill=0.0, base=0,
                               pattern=[[1, T]], channel_multiplier=-1).then_inc(consts, 1)

        @block.scalar
        def _(act):
            count = [0]

            def link(ins):
                count[0] += 1
                ins.then_inc(a_chain, 1)
                act.wait_ge(a_chain, count[0])

            m_dram = A["mem"][0].rearrange("(t p) d -> p t d", p=P)
            act.wait_ge(vrow_clear, 1)
            for name, r, n in (("g_mix", R_MIX, C), ("g_x", R_X, C), ("g_mem", R_MEM, C), ("g_ffn", R_FFN, C),
                               ("b_conv", R_BC, HM), ("mh_gain", R_GAIN, HM), ("skip_m", R_SKIP, HM)):
                act.dma_start(vrow[r:r + n, :], A[name][0].rearrange("(c p) -> c p", p=P)).then_inc(vec_loaded, 16)
            act.dma_start(vrow[R_WC:R_WC + 4 * HM, :], A["w_conv"][0].rearrange("r (c p) -> (r c) p", p=P))\
                .then_inc(vec_loaded, 16)
            for r, name in ((R_PEK, "pe_cmp_k"), (R_PEV, "pe_cmp_v")):
                for g in range(2):
                    act.dma_start(vrow[r:r + CMP_BLOCK, g * DA:(g + 1) * DA], A[name][0]).then_inc(vec_loaded, 16)
            for t in range(TT):
                act.dma_start(mem_tok[:, t], m_dram[:, t]).then_inc(mem_loaded, 16)
            act.wait_ge(consts, 1)
            act.dma_start(bif[0:HM, 0:1], A["b_i"][0].rearrange("(h a) -> h a", a=1)).then_inc(small_loaded, 16)
            act.dma_start(bif[0:HM, 1:2], A["b_f"][0].rearrange("(h a) -> h a", a=1)).then_inc(small_loaded, 16)
            act.dma_start(w2[:, 0], A["w_phi2_k"][0]).then_inc(small_loaded, 16)
            act.dma_start(w2[:, 1], A["w_phi2_v"][0]).then_inc(small_loaded, 16)
            act.dma_start(wr[:], A["w_router"][0].rearrange("(c p) e -> p c e", p=P)).then_inc(small_loaded, 16)
            act.dma_start(brow, A["b_router"].partition_broadcast(P)[:, 0]).then_inc(small_loaded, 16)
            for k, name in enumerate(("w_q_m", "w_k_m", "w_v_m")):
                act.dma_start(wm[:, k], A[name][0].rearrange("h d e -> d h e")).then_inc(wm_loaded, 16)

            def squares(n, name, src):
                for t in range(TT):
                    nc.scalar.activation(junk[name][:, t * D:(t + 1) * D], src[:, t], ACT.Square,
                                         accum_out=ss[:, 2 * n + t:2 * n + t + 1]).then_inc(sq_done, 1)
                act.wait_ge(msq_ready, n + 1)
                nc.scalar.activation(std[:, 2 * n:2 * n + 2], msq[:, 2 * n:2 * n + 2], ACT.Sqrt).then_inc(std_ready, 1)

            def gained(name, dst, g0, n):
                filled_of(act, name)
                b, _ = AT[name]
                for j in range(2):
                    last = nc.scalar.activation(dst[:, 2 * n + j], bank(name)[:, j * T:(j + 1) * T], ACT.Copy,
                                                scale=vT[:, g0 + 2 * n + j:g0 + 2 * n + j + 1])
                last.then_inc(drained[b], 1)

            def copy(name, dst, src, func=ACT.Copy, **kw):
                filled_of(act, name)
                nc.scalar.activation(dst, src, func, **kw).then_inc(drained[AT[name][0]], 1)

            act.wait_ge(consts, 1)
            act.wait_ge(x_loaded, 32)
            squares(0, "mix", x_tok)
            drained_of(act, "vec")
            gained("tm0", hT, R_MIX, 0)
            gained("tm2", hT, R_MIX, 2)
            act.wait_ge(mem_loaded, 32)
            squares(1, "mem", mem_tok)
            copy("q0", qT[:, 0:2], bank("q0").rearrange("p (c t) -> p c t", c=2))
            copy("q1", qT[:, 2:4], bank("q1").rearrange("p (c t) -> p c t", c=2))
            copy("kcvc", kcvc[:], bank("kcvc").rearrange("p (c t) -> p c t", c=2))
            drained_of(act, "gn")
            nc.scalar.activation(gates[:].rearrange("p t h b -> p (t h b)"),
                                 gates[:].rearrange("p t h b -> p (t h b)"), ACT.Exp, scale=-1.0).then_inc(gate_e, 1)
            copy("xm0", xm[:, 0:2], bank("xm0").rearrange("p (c t) -> p c t", c=2))
            act.wait_ge(fabs_ready, 1)
            link(nc.scalar.activation(rows[:, 3], rows[:, 2], ACT.Exp, scale=-1.0))
            nc.scalar.activation(rows[:, 3], rows[:, 3], ACT.Ln, bias=1.0).then_inc(softp_ready, 1)
            act.wait_ge(conv_ready, 1)
            nc.scalar.activation(r_xc[:], r_tmp[:], ACT.Exp, scale=-1.0).then_inc(silu_e, 1)
            act.wait_ge(gelu_in, 1)
            nc.scalar.activation(hid2, hid2, ACT.Exp, scale=-2.0 * 0.7978845608028654).then_inc(gelu_e, 1)
            gained("te0", memT, R_MEM, 0)
            gained("te2", memT, R_MEM, 2)
            for t in range(TT):
                copy(f"op{t}", so[:, t], bank(f"op{t}"), ACT.Exp, scale=-1.0)
            act.wait_ge(cm_in, 1)
            nc.scalar.activation(pcmp[:], pcmp[:], ACT.Exp).then_inc(cm_e, 1)
            drained_of(act, "mt")
            nc.scalar.activation(emcol, cmcol[:, 1], ACT.Exp, scale=-1.0).then_inc(em_done, 1)

            def filler(name):
                kind, n = name[:2], int(name[2])
                if kind == "ga":
                    copy(name, sga[:, 2 * n:2 * n + 2], bank(name).rearrange("p (c t) -> p c t", c=2),
                         ACT.Exp, scale=-1.0)
                elif kind == "gb":
                    copy(name, sgb[:, 2 * n:2 * n + 2], bank(name).rearrange("p (c t) -> p c t", c=2),
                         ACT.Exp, scale=-1.0)
                elif kind == "kx":
                    copy(name, kx[:, 2 * n:2 * n + 2], bank(name).rearrange("p (c t) -> p c t", c=2))

            for h in range(HA + 1):
                if h >= 1:
                    copy(f"ta{h - 1}", pT[:, (h - 1) % 2, 0], bank(f"ta{h - 1}"))
                if h < HA:
                    for t in range(TT):
                        act.wait_ge(s_max, 2 * h + t + 1)
                        for b in range(2):
                            last = nc.scalar.activation(pr[:, t, b, 0:P * (t + 1)], pr[:, t, b, 0:P * (t + 1)],
                                                        ACT.Exp, bias=nmax[:, 2 * t + b:2 * t + b + 1],
                                                        accum_out=rsum[:, 2 * t + b:2 * t + b + 1])
                        last.then_inc(s_exp, 1)
                    for name in filler_names(h)[:1]:
                        filler(name)
                    for t in range(TT):
                        act.wait_ge(s_fac, 2 * h + t + 1)
                        for b in range(2):
                            last = nc.scalar.activation(pr[:, t, b, 0:P * (t + 1)], pr[:, t, b, 0:P * (t + 1)],
                                                        ACT.Copy, scale=fac[:, 2 * t + b:2 * t + b + 1])
                        last.then_inc(s_prob, 1)
                if h == 1:
                    for m in range(HM):
                        filled_of(act, f"mq{m}")
                        nc.scalar.activation(mqk[:, m, 0], bank(f"mq{m}")[:, 0:T], ACT.Copy)
                        nc.scalar.activation(mqk[:, m, 1], bank(f"mq{m}")[:, T:2 * T], ACT.Copy,
                                             scale=float(DM) ** -0.5).then_inc(drained[AT[f"mq{m}"][0]], 1)
                if 2 <= h <= 5:
                    m = h - 2
                    drained_of(act, f"mb{m}")
                    nc.scalar.activation(r_dm[:, (m % 2) * 512:(m % 2) * 512 + 384],
                                         r_dm[:, (m % 2) * 512:(m % 2) * 512 + 384], ACT.Exp,
                                         scale=-1.0).then_inc(dm_e, 1)
                if h == 7:
                    act.wait_ge(var_ready, 1)
                    nc.scalar.activation(hst, lnm, ACT.Sqrt).then_inc(lstd_ready, 1)
                if h >= 2 and h % 2 == 0:
                    c = h // 2 - 1
                    copy(f"pv{c}", yaT[:, c], bank(f"pv{c}")[:, 0:T])
                if h < HA:
                    for name in filler_names(h)[1:]:
                        filler(name)

            for n in range(4):
                drained_of(act, f"om{n // 2}_{n % 2}")
            squares(2, "x", x_tok)
            gained("tx0", hT, R_X, 0)
            gained("tx2", hT, R_X, 2)
            for n in (0, 2):
                copy(f"qx{n}", qx[:, 2 * n:2 * n + 2], bank(f"qx{n}").rearrange("p (c t) -> p c t", c=2))
            for h in range(HX):
                act.wait_ge(cx_max, h + 1)
                for t in range(TT):
                    j = 2 * (h % 2) + t
                    last = nc.scalar.activation(px[:, j], bank(f"sx{h}")[:, t * T:(t + 1) * T], ACT.Exp,
                                                bias=nmax[:, j:j + 1], scale=float(2 * P) ** -0.5,
                                                accum_out=rsum[:, j:j + 1])
                last.then_inc(drained[AT[f"sx{h}"][0]], 1)
                act.wait_ge(cx_inv, h + 1)
                for t in range(TT):
                    j = 2 * (h % 2) + t
                    last = nc.scalar.activation(px[:, j], px[:, j], ACT.Copy, scale=rinv[:, j:j + 1])
                last.then_inc(cx_prob, 1)
                if h >= 1:
                    copy(f"ox{h - 1}", oxT[:, 2 * h - 2:2 * h], bank(f"ox{h - 1}").rearrange("p (c t) -> p c t", c=2))
            copy("ox3", oxT[:, 6:8], bank("ox3").rearrange("p (c t) -> p c t", c=2))
            for n in range(4):
                drained_of(act, f"ro{n // 2}_{n % 2}")
            squares(3, "ffn", x_tok)
            for n in (0, 2):
                copy(f"tf{n}", hT[:, 2 * n:2 * n + 2], bank(f"tf{n}").rearrange("p (c t) -> p c t", c=2))
            act.wait_ge(r_top, 1)
            for t in range(TT):
                last = nc.scalar.activation(gexp[:, t], lg[:, t], ACT.Exp, bias=negtop[:, t:t + 1])
            last.then_inc(r_exp, 1)
            drained_of(act, "meta")
            act.wait_ge(gathered, 1)
            nc.scalar.activation(xg, ps[:, XBK, :].rearrange("p (c s) -> p c s", c=C), ACT.Copy).then_inc(xg_ready, 1)
            nblk = act.value_load(cnt_i[0:1, 0:1], min_val=NE, max_val=NBLK)
            with act.Fori(0, nblk) as i:
                act.wait_ge(g_limited, i + 1)
                nc.scalar.activation(sig, gact, ACT.Sigmoid, scale=1.702).then_inc(sig_done, 1)
                act.wait_ge(pt_done, i + 1)
                nc.scalar.activation(scat, ps[:, GBK, 0:T], ACT.Copy).then_inc(scat_ready, 1)
                act.wait_ge(gathered, i + 2)
                nc.scalar.activation(xg, ps[:, XBK, :].rearrange("p (c s) -> p c s", c=C), ACT.Copy)\
                    .then_inc(xg_ready, 1)
                act.wait_ge(freed[eslot["dn1"]], i + 1)
                nc.scalar.activation(y_slot, ps[:, ZBK, :], ACT.Copy).then_inc(yslot_ready, 1)
            act.wait_ge(scattered, nblk + 1)
            for t in range(TT):
                nc.scalar.activation(r_hT[:, t * D:(t + 1) * D],
                                     ps[:, YB + 2 * t:YB + 2 * t + 2, :].rearrange("p b n -> p (b n)"), ACT.Square,
                                     accum_out=ss[:, t:t + 1]).then_inc(fin_sq, 1)
            act.wait_ge(fin_v, 1)
            nc.scalar.activation(std[:, 0:2], msq[:, 0:2], ACT.Sqrt).then_inc(fin_std, 1)

        @block.tensor
        def _(pe):
            mm = nc.tensor.matmul

            def begin(name):
                b, turn = AT[name]
                if turn:
                    pe.wait_ge(drained[b], turn)
                return ps[:, b, :]

            def end(name, ins):
                ins.then_inc(filled[AT[name][0]], 1)

            def weights(name):
                pe.wait_ge(loaded[slot_of[name]], need[name])

            def transpose4(name, src, n):
                o = begin(name)
                for j in range(2):
                    for t in range(TT):
                        last = nc.tensor.transpose(o[:, j * T + t * P:j * T + t * P + P],
                                                   src[:, t, (2 * n + j) * P:(2 * n + j + 1) * P], ident[:])
                end(name, last)

            def feature_group(name, ws, src, kk=C):
                o = begin(name)
                for j, w in enumerate(ws):
                    for k in range(kk):
                        last = mm(o[:, j * T:(j + 1) * T], w(k), src[:, k, :], start=(k == 0), stop=(k == kk - 1))
                return last

            def token_part(o, w, n, src, t):
                for k in range(C):
                    last = mm(o, src[:, k, t * P:(t + 1) * P], w[:, k, 0:n], start=(k == 0), stop=(k == C - 1))
                return last

            def stationary(w, j):
                return lambda k: w[:, k, j * P:(j + 1) * P]

            pe.wait_ge(consts, 1)
            pe.wait_ge(vec_loaded, 16 * 12)
            end("vec", nc.tensor.transpose(begin("vec")[:, 0:P], vrow[:], ident[:]))
            pe.wait_ge(xs_ready, 2)
            for n in range(4):
                transpose4(f"tm{n}", xs, n)
            for n in range(4):
                drained_of(pe, f"tm{n}")
            weights("q")
            w = wslot("q", C, 512)
            for n in range(2):
                last = feature_group(f"q{n}", [stationary(w, 2 * n), stationary(w, 2 * n + 1)], hT)
                end(f"q{n}", last)
            weights("kcvs")
            w = wslot("kcvs", C, 512)
            end("kcvc", feature_group("kcvc", [stationary(w, 0), stationary(w, 1)], hT))
            feature_group("ksvs", [stationary(w, 2)], hT)
            for t in range(TT):
                last = token_part(bank("ksvs")[:, T + t * P:T + t * P + P], w[:, :, 384:512], P, hT, t)
            end("ksvs", last)
            weights("kwg")
            w = wslot("kwg", C, GCOL)
            feature_group("kwvw", [stationary(w, 0)], hT)
            for t in range(TT):
                last = token_part(bank("kwvw")[:, T + t * P:T + t * P + P], w[:, :, P:2 * P], P, hT, t)
            end("kwvw", last)
            o = begin("gn")
            for t in range(TT):
                last = token_part(o[:, t * 24:(t + 1) * 24], w[:, :, 2 * P:2 * P + 24], 24, hT, t)
            end("gn", last)
            o = begin("if")
            for j in range(2):
                for k in range(C):
                    last = mm(o[0:HM, j * T:(j + 1) * T], w[:, k, GW + HM * j:GW + HM * j + HM], hT[:, k, :],
                              start=(k == 0), stop=(k == C - 1))
            end("if", last)
            weights("xm")
            w = wslot("xm", C, 512)
            for n in range(2):
                end(f"xm{n}", feature_group(f"xm{n}", [stationary(w, 2 * n), stationary(w, 2 * n + 1)], hT))
            weights("phik")
            weights("phiv")
            pe.wait_ge(blk_ready, 2)
            for g in range(2):
                name = "cmpAB"[0:3] + "AB"[g]
                o = begin(name)
                for kind in range(2):
                    w = wslot(("phik", "phiv")[kind], CMP_BLOCK, P)
                    for s in range(CMP_BLOCK):
                        last = mm(o[:, kind * CW:kind * CW + NCMP], w[g * DA:(g + 1) * DA, s],
                                  blocks[g * DA:(g + 1) * DA, kind, s], start=(s == 0), stop=(s == CMP_BLOCK - 1))
                end(name, last)
            pe.wait_ge(xs_ready, 4)
            for n in range(4):
                transpose4(f"te{n}", mem_tok, n)
            weights("op")
            w = wslot("op", C, 512)
            for t in range(TT):
                end(f"op{t}", token_part(begin(f"op{t}"), w, 512, hT, t))
            pe.wait_ge(gelu_done, 1)
            pe.wait_ge(small_loaded, 16 * 6)
            o = begin("cmp2")
            for g in range(2):
                mm(o[g * DA:(g + 1) * DA, 0:NCMP], w2[:, 0], gel[:, 0, g, 0:NCMP], start=True, stop=True)
            for g in range(2):
                last = mm(o[0:NCMP, CW + g * DA:CW + (g + 1) * DA], gel[:, 1, g, 0:NCMP], w2[:, 1],
                          start=True, stop=True)
            end("cmp2", last)
            drained_of(pe, "cmp2")
            drained_of(pe, "q0")
            drained_of(pe, "q1")
            for g in range(2):
                name = ("csA", "csB")[g]
                o = begin(name)
                for t in range(TT):
                    for c in range(PAIRS):
                        a = (t * PAIRS + c) * CW
                        last = mm(o[:, a:a + NCMP], qT[g * DA:(g + 1) * DA, c, t * P:(t + 1) * P],
                                  kcT[g * DA:(g + 1) * DA, 0:NCMP], start=True, stop=True)
                end(name, last)
            pe.wait_ge(rows_ready, 1)
            o = begin("mt")
            for kind in range(2):
                for t in range(TT):
                    last = nc.tensor.transpose(o[:, (kind * TT + t) * HM:(kind * TT + t + 1) * HM],
                                               rows[:, 5 + 2 * kind, t * P:(t + 1) * P], ident[0:HM, 0:HM])
            end("mt", last)

            def filler(name):
                kind, n = name[:2], int(name[2])
                half = f"{kind}{n // 2}"
                weights(half)
                w = wslot(half, C, 512)
                if kind in ("ga", "gb"):
                    src = hT
                else:
                    src = memT
                    for m in range(4):
                        drained_of(pe, f"te{m}")
                if kind == "vx":
                    last = token_part(begin(name), w, 512, memT, n % 2)
                else:
                    j = 2 * (n % 2)
                    last = feature_group(name, [stationary(w, j), stationary(w, j + 1)], src)
                end(name, last)
            for h in range(HA + 1):
                if h >= 1:
                    m = h - 1
                    pe.wait_ge(s_prob, 2 * m + 2)
                    o = begin(f"ta{m}")
                    for b in range(2):
                        for t in range(TT):
                            last = nc.tensor.transpose(o[:, b * T + t * P:b * T + t * P + P], pr[:, t, b, 0:P], ident[:])
                    end(f"ta{m}", last)
                    o = begin(f"tb{m}")
                    for b in range(2):
                        nc.tensor.transpose(o[:, b * P:(b + 1) * P], pr[:, 1, b, P:T], ident[:])
                    pe.wait_ge(cm_done, 1)
                    nat = (m % 2) * PAIRS + m // 2
                    for t in range(TT):
                        last = nc.tensor.transpose(o[0:NCMP, T + t * P:T + t * P + P], pcmp[:, t, nat, 0:NCMP], ident[:])
                    end(f"tb{m}", last)
                if h < HA:
                    c, g = h // 2, h % 2
                    drained_of(pe, "ksvs")
                    drained_of(pe, "kwvw")
                    for t in range(TT):
                        o = begin(f"sc{h}_{t}")
                        n = P * (t + 1)
                        for b in range(2):
                            last = mm(o[:, b * n:(b + 1) * n], qT[g * DA:(g + 1) * DA, c, t * P:(t + 1) * P],
                                      kskw[g * DA:(g + 1) * DA, b, 0:n], start=True, stop=True)
                        end(f"sc{h}_{t}", last)
                    for name in filler_names(h)[:1]:
                        filler(name)
                if h == 1:
                    pe.wait_ge(wm_loaded, 48)
                    pe.wait_ge(xc_ready, 1)
                    drained_of(pe, "xm0")
                    for t in range(TT):
                        o = begin(f"mv{t}")
                        for m in range(HM):
                            last = mm(o[:, m * DM:(m + 1) * DM], xm[:, m, t * P:(t + 1) * P], wm[:, 2, m],
                                      start=True, stop=True)
                        end(f"mv{t}", last)
                    for m in range(HM):
                        o = begin(f"mq{m}")
                        for k in range(2):
                            last = mm(o[:, k * T:(k + 1) * T], wm[:, k, m], xc[:, m], start=True, stop=True)
                        end(f"mq{m}", last)
                if 3 <= h <= 6:
                    m = h - 3
                    drained_of(pe, f"ms{m}")
                    drained_of(pe, "mv0")
                    drained_of(pe, "mv1")
                    o = begin(f"mn{m}")
                    b = m % 2
                    mm(o[:, 0:DM + 1], dm[:, b, 0, 0:P], mv[:, 0, m, 0:DM + 1], start=True, stop=True)
                    mm(o[:, T:T + DM + 1], dm[:, b, 0, P:T], mv[:, 0, m, 0:DM + 1], start=True, stop=False)
                    last = mm(o[:, T:T + DM + 1], dm[:, b, 1, 0:P], mv[:, 1, m, 0:DM + 1], start=False, stop=True)
                    end(f"mn{m}", last)
                if 2 <= h <= 5:
                    m = h - 2
                    drained_of(pe, f"mq{m}")
                    o = begin(f"mb{m}")
                    end(f"mb{m}", mm(o[:, 0:T], ident[0:HM, m:m + 1].broadcast_to([HM, P]), mrow,
                                     start=True, stop=True))
                    o = begin(f"ms{m}")
                    mm(o[:, 0:T], mqk[:, m, 1, 0:P], mqk[:, m, 0], start=True, stop=True)
                    last = mm(o[:, T:T + P], mqk[:, m, 1, P:T], mqk[:, m, 0, P:T], start=True, stop=True)
                    end(f"ms{m}", last)
                if h >= 2 and h % 2 == 0:
                    c = h // 2 - 1
                    o = begin(f"pv{c}")
                    for g in range(2):
                        m = 2 * c + g
                        drained_of(pe, f"ta{m}")
                        drained_of(pe, f"tb{m}")
                        og = o[g * DA:(g + 1) * DA]
                        for b in range(2):
                            mm(og[:, 0:T], vsvw[:, b, 0, g * DA:(g + 1) * DA], pT[:, g, 0, b * T:(b + 1) * T],
                               start=(b == 0), stop=False)
                        for b in range(2):
                            mm(og[:, P:T], vsvw[:, b, 1, g * DA:(g + 1) * DA], pT[:, g, 1, b * P:(b + 1) * P],
                               start=False, stop=False)
                        last = mm(og[:, 0:T], vc[0:NCMP, g], pT[0:NCMP, g, 1, T:2 * T], start=False, stop=True)
                    end(f"pv{c}", last)
                if h < HA:
                    for name in filler_names(h)[1:]:
                        filler(name)
            pe.wait_ge(hn_ready, 1)
            for n in range(2):
                o = begin(f"ty{n}")
                for j in range(2):
                    for t in range(TT):
                        last = nc.tensor.transpose(o[:, j * T + t * P:j * T + t * P + P], hs[:, t, 2 * n + j], ident[:])
                end(f"ty{n}", last)
            weights("ua")
            weights("ub")
            drained_of(pe, "pv3")
            drained_of(pe, "ty0")
            drained_of(pe, "ty1")
            for n in range(4):
                w = wslot("ua", PAIRS, D)
                end(f"ua{n}", feature_group(f"ua{n}", [stationary(w, 2 * n), stationary(w, 2 * n + 1)], yaT, PAIRS))
                w = wslot("ub", HM, D)
                end(f"ub{n}", feature_group(f"ub{n}", [stationary(w, 2 * n), stationary(w, 2 * n + 1)], ybT, HM))

            def token_groups(prefix, piece_name, src):
                for n in range(2):
                    weights(f"{piece_name}{n}")
                    w = wslot(f"{piece_name}{n}", C, 512)
                    for t in range(TT):
                        name = f"{prefix}{n}_{t}"
                        end(name, token_part(begin(name), w, 512, src, t))

            pe.wait_ge(merged_ready, 4)
            token_groups("om", "om", sga)
            pe.wait_ge(xs_ready, 6)
            for n in range(4):
                transpose4(f"tx{n}", xs, n)
            for n in range(4):
                drained_of(pe, f"tx{n}")
            for n in range(4):
                weights(f"qx{n // 2}")
                w = wslot(f"qx{n // 2}", C, 512)
                j = 2 * (n % 2)
                end(f"qx{n}", feature_group(f"qx{n}", [stationary(w, j), stationary(w, j + 1)], hT))
            for n in range(4):
                drained_of(pe, f"kx{n}")
                drained_of(pe, f"vx{n}")
            for h in range(HX):
                drained_of(pe, f"qx{h}")
                o = begin(f"sx{h}")
                for t in range(TT):
                    for k in range(2):
                        last = mm(o[:, t * T:(t + 1) * T], qx[:, 2 * h + k, t * P:(t + 1) * P], kx[:, 2 * h + k],
                                  start=(k == 0), stop=(k == 1))
                end(f"sx{h}", last)
            for h in range(HX):
                pe.wait_ge(cx_prob, h + 1)
                o = begin(f"pt{h}")
                for mt in range(2):
                    for t in range(TT):
                        last = nc.tensor.transpose(o[:, mt * T + t * P:mt * T + t * P + P],
                                                   px[:, 2 * (h % 2) + t, mt * P:(mt + 1) * P], ident[:])
                end(f"pt{h}", last)
                drained_of(pe, f"pt{h}")
                o = begin(f"ox{h}")
                for k in range(2):
                    for mt in range(2):
                        last = mm(o[:, k * T:(k + 1) * T], vx[:, mt, (2 * h + k) * P:(2 * h + k + 1) * P],
                                  pxT[:, h % 2, mt], start=(mt == 0), stop=(mt == 1))
                end(f"ox{h}", last)
            for h in range(HX):
                drained_of(pe, f"ox{h}")
            token_groups("ro", "ox", oxT)
            pe.wait_ge(xs_ready, 8)
            for n in range(4):
                transpose4(f"tf{n}", xs, n)
            for n in range(4):
                drained_of(pe, f"tf{n}")
            o = begin("rt")
            for t in range(TT):
                last = token_part(o[:, t * NE:(t + 1) * NE], wr, NE, hT, t)
            end("rt", last)
            pe.wait_ge(r_gate, 1)
            pe.wait_ge(consts, 2)
            o = begin("pos")
            mm(o[0:NE, 0:T], mask[:, 0], strict, start=True, stop=False)
            mm(o[0:NE, P:T], mask[:, 1], strict[:, 0:P], start=False, stop=True)
            for t in range(TT):
                last = mm(o[0:NE, T + t * P:T + t * P + P], mask[:, t], ident[:], start=True, stop=True)
            end("pos", last)
            o = begin("cnt")
            for t in range(TT):
                mm(o[0:NE, t * P:(t + 1) * P], gate[:, t], ident[:], start=True, stop=True)
            for t in range(TT):
                last = mm(o[0:NE, T:T + 1], mask[:, t], ones[:, 0:1], start=(t == 0), stop=(t == 1))
            end("cnt", last)
            pe.wait_ge(r_ovf, 1)
            o = begin("rank")
            mm(o[0:NE, 0:MORE], strict[0:NE, 0:NE], ovf, start=True, stop=False)
            last = mm(o[0:NE, 0:MORE], ones[0:NE, 0:NE], ovs, start=False, stop=True)
            end("rank", last)
            pe.wait_ge(r_sel, 1)
            o = begin("meta")
            mm(o[0:1, 0:16], eidx[0:NE, 0:1], blksel[:, NE:NE + 16], start=True, stop=True)
            last = mm(o[0:1, 16:16 + MORE], ones[0:NE, 0:1], ovf, start=True, stop=True)
            end("meta", last)
            o = begin("blk")
            for t in range(TT):
                mm(o[:, t * BCOL:(t + 1) * BCOL], posT[:, t * P:(t + 1) * P], blksel, start=True, stop=False)
                mm(o[:, t * BCOL:(t + 1) * BCOL], ones[0:NE, 0:P], blkoff, start=False, stop=True)
                last = mm(o[:, (2 + t) * BCOL:(3 + t) * BCOL], gateT[:, t * P:(t + 1) * P], blksel,
                          start=True, stop=True)
            end("blk", last)
            for b in range(BANKS):
                pe.wait_ge(drained[b], USES[b])
            for t in range(TT):
                for n in range(2):
                    last = mm(ps[:, YB + 2 * t + n, :], ident[:], x_tok[:, t, n * 512:(n + 1) * 512],
                              start=True, stop=False, skip_group_check=True)
            last.then_inc(y_begun, 1)

            def gather(i):
                pe.wait_ge(place_ready, i + 1)
                for c in range(C):
                    for t in range(TT):
                        last = mm(ps[:, XBK, c * SLOTS:(c + 1) * SLOTS], xs[:, t, c * P:(c + 1) * P],
                                  place[:, t], start=(t == 0), stop=(t == 1))
                last.then_inc(gathered, 1)

            def scatter():
                for t in range(TT):
                    for n in range(2):
                        half = slice(n * SLOTS, (n + 1) * SLOTS)
                        last = mm(ps[:, YB + 2 * t + n, :], scat[half, t * P:(t + 1) * P], y_slot[half, :],
                                  start=False, stop=False, skip_group_check=True)
                last.then_inc(scattered, 1)

            def halves(bk, stationary_, moving, start, stop):
                for n in range(2):
                    last = mm(ps[n * SLOTS:(n + 1) * SLOTS, bk, :], stationary_, moving(n), start=start, stop=stop,
                              skip_group_check=True)
                return last

            gather(0)
            pe.wait_ge(late_loaded, 32)
            drained_of(pe, "meta")
            nblk = pe.value_load(cnt_i[0:1, 0:1], min_val=NE, max_val=NBLK)
            with pe.Fori(0, nblk) as i:
                pe.wait_ge(cur_ready, i + 1)
                for b in range(2):
                    halves(GBK + b, cur, lambda n: bgu_rows[:, b * D + n * 512:b * D + n * 512 + 512], True, False)
                pe.wait_ge(xg_ready, i + 1)
                for j in range(4):
                    s = eslot[EXPERT_PIECES[j]]
                    pe.wait_ge(loaded[s], i * 16 + (16 * dmas[s] + 16))
                    w = ring[:, s].rearrange("p (k n) -> p k n", k=2)
                    for k in range(2):
                        kk = 2 * j + k
                        for b in range(2):
                            last = halves(GBK + b, xg[:, kk],
                                          lambda n: w[:, k, b * D + n * 512:b * D + n * 512 + 512], False, kk == 7)
                    last.then_inc(freed[s], 1)
                pe.wait_ge(scat_ready, i + 1)
                pe.wait_ge(yslot_ready, i + 1)
                scatter()
                pe.wait_ge(h_ready, i + 1)
                for c in range(4):
                    last = nc.tensor.transpose(ps[:, ZBK, c * P:(c + 1) * P], hact[:, c * P:(c + 1) * P], ident[:])
                last.then_inc(ht_done, 1)
                pe.wait_ge(placeg_ready, i + 1)
                for t in range(TT):
                    last = nc.tensor.transpose(ps[:, GBK, t * P:(t + 1) * P], placeg[:, t], ident[:])
                last.then_inc(pt_done, 1)
                gather(i + 1)
                pe.wait_ge(hT_ready, i + 1)
                halves(ZBK, cur, lambda n: bdn_rows[:, n * 512:n * 512 + 512], True, False)
                for j in range(2):
                    s = eslot[EXPERT_PIECES[4 + j]]
                    pe.wait_ge(loaded[s], i * 16 + (16 * dmas[s] + 16))
                    w = ring[:, s].rearrange("p (k n) -> p k n", k=4)
                    for k in range(4):
                        last = halves(ZBK, hactT[:, k, j], lambda n: w[:, k, n * 512:n * 512 + 512], False,
                                      j == 1 and k == 3)
                    last.then_inc(freed[s], 1)
            pe.wait_ge(yslot_ready, nblk + 1)
            pe.wait_ge(scat_ready, nblk + 1)
            scatter()

        @block.vector
        def _(dve):
            count = [0]
            V = nc.vector

            def link(ins):
                count[0] += 1
                ins.then_inc(v_chain, 1)
                dve.wait_ge(v_chain, count[0])

            def drain(name, ins):
                ins.then_inc(drained[AT[name][0]], 1)

            def norm(n, src, dst, gain=None):
                dve.wait_ge(sq_done, 2 * n + 2)
                V.tensor_scalar(msq[:, 2 * n:2 * n + 2], ss[:, 2 * n:2 * n + 2], 1.0 / D, EPS, ALU.mult, ALU.add)\
                    .then_inc(msq_ready, 1)
                dve.wait_ge(std_ready, n + 1)
                link(V.reciprocal(rstd[:, 2 * n:2 * n + 2], std[:, 2 * n:2 * n + 2]))
                for t in range(TT):
                    r = rstd[:, 2 * n + t:2 * n + t + 1]
                    if gain is None:
                        ins = V.tensor_scalar(dst[:, t], src[:, t], r, None, ALU.mult)
                    else:
                        ins = V.scalar_tensor_tensor(out=dst[:, t], in0=src[:, t], scalar=r, in1=gain, op0=ALU.mult,
                                                     op1=ALU.mult)
                    ins.then_inc(xs_ready, 1)

            def gained(name, dst, g0, n):
                filled_of(dve, name)
                g = vT[:, g0 + 2 * n:g0 + 2 * n + 2].unsqueeze(2).broadcast_to([P, 2, T])
                drain(name, V.tensor_tensor(dst[:, 2 * n:2 * n + 2],
                                            bank(name).rearrange("p (c t) -> p c t", c=2), g, ALU.mult))

            def col(r):
                return vT[:, r:r + 1]

            dve.wait_ge(consts, 1)
            norm(0, x_tok, xs)
            filled_of(dve, "vec")
            V.tensor_copy(vT[:], bank("vec")[:, 0:P]).then_inc(drained[AT["vec"][0]], 1)
            drained_of(dve, "vec")
            gained("tm1", hT, R_MIX, 1)
            gained("tm3", hT, R_MIX, 3)
            dve.wait_ge(mem_loaded, 32)
            norm(1, mem_tok, mem_tok)
            for name, b in (("ksvs", 0), ("kwvw", 1)):
                filled_of(dve, name)
                V.tensor_copy(kskw[:, b], bank(name)[:, 0:T])
                drain(name, V.tensor_copy(vsvw[:, b], bank(name)[:, T:2 * T].rearrange("p (t e) -> p t e", t=TT)))
            drained_of(dve, "kcvc")
            for kind, r in ((0, R_PEK), (1, R_PEV)):
                sub = kcvc[:, kind].rearrange("p (j s) -> p s j", s=CMP_STRIDE)
                for half in range(2):
                    s0 = half * CMP_STRIDE
                    pe_b = vT[:, r + s0:r + s0 + CMP_STRIDE].unsqueeze(2).broadcast_to([P, CMP_STRIDE, NCMP])
                    last = V.tensor_tensor(blocks[:, kind, s0:s0 + CMP_STRIDE], sub[:, :, half:half + NCMP], pe_b,
                                           ALU.add)
                last.then_inc(blk_ready, 1)
            gflat = gates[:].rearrange("p t h b -> p (t h b)")
            filled_of(dve, "gn")
            drain("gn", V.tensor_copy(gflat, bank("gn")[:, 0:2 * 24]))
            filled_of(dve, "if")
            dve.wait_ge(small_loaded, 16 * 6)
            V.tensor_scalar(rows[:, 0], bank("if")[0:HM, 0:T], bif[0:HM, 0:1], None, ALU.add)
            drain("if", V.tensor_scalar(rows[:, 1], bank("if")[0:HM, T:2 * T], bif[0:HM, 1:2], None, ALU.add))
            drained_of(dve, "if")
            V.scalar_tensor_tensor(out=rows[:, 2], in0=rows[:, 1], scalar=-1.0, in1=rows[:, 1], op0=ALU.mult,
                                   op1=ALU.max).then_inc(fabs_ready, 1)
            filled_of(dve, "xm1")
            drain("xm1", V.tensor_copy(xm[:, 2:4], bank("xm1").rearrange("p (c t) -> p c t", c=2)))
            drained_of(dve, "xm0")
            drained_of(dve, "xm1")
            for h in range(HM):
                last = V.tensor_scalar(conv[:, h], xm[:, h], col(R_WC + 3 * HM + h), col(R_BC + h), ALU.mult, ALU.add)
            for r in range(2, -1, -1):
                link(last)
                s = 3 - r
                for h in range(HM):
                    last = V.scalar_tensor_tensor(out=conv[:, h, s:T], in0=xm[:, h, 0:T - s],
                                                  scalar=col(R_WC + r * HM + h), in1=conv[:, h, s:T],
                                                  op0=ALU.mult, op1=ALU.add)
            last.then_inc(conv_ready, 1)
            dve.wait_ge(gate_e, 1)
            link(V.tensor_scalar(gflat, gflat, 1.0, None, ALU.add))
            link(V.reciprocal(gflat, gflat))
            dve.wait_ge(softp_ready, 1)
            link(V.scalar_tensor_tensor(out=rows[:, 1], in0=rows[:, 1], scalar=0.0, in1=rows[:, 3], op0=ALU.min,
                                        op1=ALU.subtract))
            link(V.tensor_tensor_scan(rows[:, 4], ones[0:HM], rows[:, 1], 0.0, ALU.mult, ALU.add))
            link(V.tensor_tensor(rows[:, 5], rows[:, 0], rows[:, 4], ALU.subtract))
            link(V.tensor_tensor_scan(mrow, ones[0:HM], rows[:, 5], 0.0, ALU.mult, ALU.max))
            V.tensor_tensor(rows[:, 7], rows[:, 4], mrow, ALU.add).then_inc(rows_ready, 1)
            dve.wait_ge(silu_e, 1)
            link(V.tensor_scalar(r_xc[:], r_xc[:], 1.0, None, ALU.add))
            link(V.reciprocal(r_xc[:], r_xc[:]))
            V.tensor_tensor(r_xc[:], r_xc[:], r_tmp[:], ALU.mult).then_inc(xc_ready, 1)
            for g in range(2):
                name = ("cmpA", "cmpB")[g]
                filled_of(dve, name)
                drain(name, V.tensor_copy(
                    hid.rearrange("p (k g j) -> p k g j", k=2, g=2)[:, :, g, 0:NCMP],
                    bank(name)[:, 0:2 * CW].rearrange("p (k j) -> p k j", k=2)[:, :, 0:NCMP]))
            drained_of(dve, "cmpA")
            drained_of(dve, "cmpB")
            link(V.tensor_tensor(hid2, hid, hid, ALU.mult))
            link(V.tensor_scalar(hid2, hid2, 0.044715, 1.0, ALU.mult, ALU.add))
            V.tensor_tensor(hid2, hid2, hid, ALU.mult).then_inc(gelu_in, 1)
            dve.wait_ge(gelu_e, 1)
            link(V.tensor_scalar(hid2, hid2, 1.0, None, ALU.add))
            link(V.reciprocal(hid2, hid2))
            V.tensor_tensor(gel.rearrange("p k g j -> p (k g j)"), hid, hid2, ALU.mult).then_inc(gelu_done, 1)
            gained("te1", memT, R_MEM, 1)
            gained("te3", memT, R_MEM, 3)
            drained_of(dve, "op0")
            drained_of(dve, "op1")
            link(V.tensor_scalar(r_so[:], r_so[:], 1.0, None, ALU.add))
            link(V.reciprocal(r_so[:], r_so[:]))
            filled_of(dve, "cmp2")
            V.tensor_copy(kcT[:, 0:NCMP], bank("cmp2")[:, 0:NCMP])
            drain("cmp2", V.tensor_copy(vc[0:NCMP], bank("cmp2")[0:NCMP, CW:CW + P].rearrange("p (g d) -> p g d", g=2)))
            for g in range(2):
                name = ("csA", "csB")[g]
                filled_of(dve, name)
                for t in range(TT):
                    s = bank(name)[:, t * PAIRS * CW:(t + 1) * PAIRS * CW].rearrange("p (c j) -> p c j", j=CW)
                    m = rmaskc[:, t, 0:NCMP].unsqueeze(1).broadcast_to([P, PAIRS, NCMP])
                    last = V.scalar_tensor_tensor(out=pcmp[:, t, g * PAIRS:(g + 1) * PAIRS, 0:NCMP],
                                                  in0=s[:, :, 0:NCMP], scalar=float(DA) ** -0.5, in1=m,
                                                  op0=ALU.mult, op1=ALU.add)
                drain(name, last)
            drained_of(dve, "csB")
            pflat = pcmp[:].rearrange("p t h j -> p (t h) j")
            valid = pflat[:, :, 0:NCMP]
            link(V.tensor_reduce(cst, valid, AX.X, ALU.max))
            V.tensor_tensor(valid, valid, cst.unsqueeze(2).broadcast_to([P, TT * HA, NCMP]), ALU.subtract)\
                .then_inc(cm_in, 1)
            dve.wait_ge(cm_e, 1)
            link(V.tensor_reduce(cst, valid, AX.X, ALU.add))
            link(V.reciprocal(cst, cst))
            link(V.tensor_tensor(cst.rearrange("p (t h) -> p t h", t=TT), cst.rearrange("p (t h) -> p t h", t=TT),
                                 gates[:, :, :, 0], ALU.mult))
            link(V.tensor_tensor(valid, valid, cst.unsqueeze(2).broadcast_to([P, TT * HA, NCMP]), ALU.mult))
            for t in range(TT):
                last = V.tensor_tensor(pcmp[:, t, :, 0:NCMP], pcmp[:, t, :, 0:NCMP],
                                       mmaskc[:, t, 0:NCMP].unsqueeze(1).broadcast_to([P, HA, NCMP]), ALU.mult)
            last.then_inc(cm_done, 1)
            filled_of(dve, "mt")
            drain("mt", V.tensor_copy(cmcol, bank("mt")[:, 0:16].rearrange("p (k t h) -> p k t h", k=2, t=TT)))
            drained_of(dve, "mt")

            def filler(name):
                kind, n = name[:2], int(name[2])
                if kind == "vx":
                    filled_of(dve, name)
                    drain(name, V.tensor_copy(vx[:, n % 2, (n // 2) * 512:(n // 2) * 512 + 512], bank(name)))

            def sigmoid_rest(r):
                link(V.tensor_scalar(r[:], r[:], 1.0, None, ALU.add))
                link(V.reciprocal(r[:], r[:]))

            for h in range(HA + 1):
                if h >= 1:
                    m = h - 1
                    filled_of(dve, f"tb{m}")
                    V.tensor_copy(pT[:, m % 2, 1, 0:T], bank(f"tb{m}")[:, 0:T])
                    drain(f"tb{m}", V.tensor_copy(pT[0:NCMP, m % 2, 1, T:2 * T], bank(f"tb{m}")[0:NCMP, T:2 * T]))
                if h < HA:
                    g, nat = h % 2, (h % 2) * PAIRS + h // 2
                    for t in range(TT):
                        name, n = f"sc{h}_{t}", P * (t + 1)
                        filled_of(dve, name)
                        m = causal[:, T - n:T].unsqueeze(1).broadcast_to([P, 2, n])
                        drain(name, V.scalar_tensor_tensor(
                            out=pr[:, t, :, 0:n], in0=bank(name)[:, 0:2 * n].rearrange("p (b n) -> p b n", b=2),
                            scalar=float(DA) ** -0.5, in1=m, op0=ALU.mult, op1=ALU.add))
                        drained_of(dve, name)
                        V.tensor_reduce(nmax[:, 2 * t:2 * t + 2], pr[:, t, :, 0:n], AX.X, ALU.max, negate=True)\
                            .then_inc(s_max, 1)
                    for name in filler_names(h)[:1]:
                        filler(name)
                    for t in range(TT):
                        dve.wait_ge(s_exp, 2 * h + t + 1)
                        link(V.reciprocal(rinv[:, 2 * t:2 * t + 2], rsum[:, 2 * t:2 * t + 2]))
                        V.tensor_tensor(fac[:, 2 * t:2 * t + 2], rinv[:, 2 * t:2 * t + 2], gates[:, t, nat, 1:3],
                                        ALU.mult).then_inc(s_fac, 1)
                if h == 1:
                    for t in range(TT):
                        filled_of(dve, f"mv{t}")
                        drain(f"mv{t}", V.tensor_copy(mv[:, t, :, 0:DM], bank(f"mv{t}").rearrange("p (h e) -> p h e", h=HM)))
                if 3 <= h <= 6:
                    m = h - 3
                    name = f"mn{m}"
                    filled_of(dve, name)
                    num = bank(name).rearrange("p (t e) -> p t e", t=TT)
                    link(V.tensor_scalar(den[:, 0:2].unsqueeze(2), num[:, :, DM:DM + 1], -1.0, None, ALU.mult))
                    link(V.tensor_tensor(den[:, 0:2].unsqueeze(2), num[:, :, DM:DM + 1], den[:, 0:2].unsqueeze(2), ALU.max))
                    dve.wait_ge(em_done, 1)
                    link(V.tensor_tensor(den[:, 0:2], den[:, 0:2], emcol[:, :, m], ALU.max))
                    link(V.reciprocal(den[:, 2:4], den[:, 0:2]))
                    for t in range(TT):
                        last = V.scalar_tensor_tensor(out=hs[:, t, m], in0=num[:, t, 0:DM],
                                                      scalar=den[:, 2 + t:3 + t], in1=so[:, t, m * DM:(m + 1) * DM],
                                                      op0=ALU.mult, op1=ALU.mult,
                                                      accum_out=hsum[:, t * HM + m:t * HM + m + 1])
                    drain(name, last)
                if 2 <= h <= 5:
                    m = h - 2
                    name = f"mb{m}"
                    filled_of(dve, name)
                    if m >= 2:
                        filled_of(dve, f"mn{m - 2}")
                    V.tensor_scalar(dm[:, m % 2, 0], bank(name)[:, 0:T], cmcol[:, 0, 0, m:m + 1], 0.0,
                                    ALU.subtract, ALU.max)
                    drain(name, V.tensor_scalar(dm[:, m % 2, 1, 0:P], bank(name)[:, P:T], cmcol[:, 0, 1, m:m + 1],
                                                0.0, ALU.subtract, ALU.max))
                    name = f"ms{m}"
                    filled_of(dve, name)
                    dve.wait_ge(dm_e, m + 1)
                    link(V.tensor_tensor(dm[:, m % 2, :, 0:P], dm[:, m % 2, :, 0:P],
                                         upper[:].unsqueeze(1).broadcast_to([P, 2, P]), ALU.mult))
                    flat = r_dm[:, (m % 2) * 512:(m % 2) * 512 + 384]
                    drain(name, V.tensor_tensor(flat, flat, bank(name)[:, 0:384], ALU.mult))
                if h == 6:
                    for m in range(HM):
                        drained_of(dve, f"mn{m}")
                    link(V.tensor_scalar(hsum, hsum, 1.0 / DM, None, ALU.mult))
                    h3 = hs[:].rearrange("p t h e -> p (t h) e")
                    link(V.tensor_tensor(h3, h3, hsum.unsqueeze(2).broadcast_to([P, TT * HM, DM]), ALU.subtract))
                    sq = r_xm[:].rearrange("p (h e) -> p h e", e=DM)
                    link(V.tensor_tensor(sq, h3, h3, ALU.mult))
                    link(V.tensor_reduce(lnm, sq, AX.X, ALU.add))
                    V.tensor_scalar(lnm, lnm, 1.0 / DM, EPS, ALU.mult, ALU.add).then_inc(var_ready, 1)
                    for m in range(HM):
                        V.tensor_scalar(ybT[:, m], xc[:, m], col(R_SKIP + m), None, ALU.mult)
                if h == 7:
                    dve.wait_ge(lstd_ready, 1)
                    link(V.reciprocal(hst, hst))
                    V.tensor_tensor(h3, h3, hst.unsqueeze(2).broadcast_to([P, TT * HM, DM]), ALU.mult)\
                        .then_inc(hn_ready, 1)
                if h == 4:
                    for n in range(4):
                        drained_of(dve, f"ga{n}")
                    sigmoid_rest(r_ga)
                if h == 5:
                    for n in range(4):
                        drained_of(dve, f"gb{n}")
                    sigmoid_rest(r_gb)
                if h < HA:
                    for name in filler_names(h)[1:]:
                        filler(name)
            for n in range(2):
                filled_of(dve, f"ty{n}")
                for j in range(2):
                    m = 2 * n + j
                    last = V.scalar_tensor_tensor(out=ybT[:, m], in0=bank(f"ty{n}")[:, j * T:(j + 1) * T],
                                                  scalar=col(R_GAIN + m), in1=ybT[:, m], op0=ALU.mult, op1=ALU.add)
                drain(f"ty{n}", last)
            for n in range(4):
                for name, g in ((f"ua{n}", sga), (f"ub{n}", sgb)):
                    filled_of(dve, name)
                    drain(name, V.tensor_tensor(g[:, 2 * n:2 * n + 2], bank(name).rearrange("p (c t) -> p c t", c=2),
                                                g[:, 2 * n:2 * n + 2], ALU.mult))
                drained_of(dve, f"ub{n}")
                V.tensor_tensor(sga[:, 2 * n:2 * n + 2], sga[:, 2 * n:2 * n + 2], sgb[:, 2 * n:2 * n + 2], ALU.add)\
                    .then_inc(merged_ready, 1)

            def residual(prefix):
                for n in range(2):
                    for t in range(TT):
                        name = f"{prefix}{n}_{t}"
                        filled_of(dve, name)
                        xv = x_tok[:, t, n * 512:(n + 1) * 512]
                        drain(name, V.tensor_tensor(xv, bank(name), xv, ALU.add))
                for n in range(4):
                    drained_of(dve, f"{prefix}{n // 2}_{n % 2}")

            dve.wait_ge(x_again, 16)
            residual("om")
            norm(2, x_tok, xs)
            gained("tx1", hT, R_X, 1)
            gained("tx3", hT, R_X, 3)
            for n in (1, 3):
                filled_of(dve, f"qx{n}")
                drain(f"qx{n}", V.tensor_copy(qx[:, 2 * n:2 * n + 2], bank(f"qx{n}").rearrange("p (c t) -> p c t", c=2)))

            def cross_max(h):
                name = f"sx{h}"
                filled_of(dve, name)
                j = 2 * (h % 2)
                if h >= 2:
                    filled_of(dve, f"pt{h - 2}")
                link(V.tensor_reduce(nmax[:, j:j + 2], bank(name).rearrange("p (t m) -> p t m", t=TT), AX.X, ALU.max,
                                     negate=True))
                V.tensor_scalar(nmax[:, j:j + 2], nmax[:, j:j + 2], float(2 * P) ** -0.5, None, ALU.mult)\
                    .then_inc(cx_max, 1)
                drained_of(dve, name)
                V.reciprocal(rinv[:, j:j + 2], rsum[:, j:j + 2]).then_inc(cx_inv, 1)

            for h in range(HX + 1):
                if h < HX:
                    cross_max(h)
                if h >= 1:
                    m = h - 1
                    filled_of(dve, f"pt{m}")
                    drain(f"pt{m}", V.tensor_copy(pxT[:, m % 2], bank(f"pt{m}").rearrange("p (m t) -> p m t", m=2)))
            residual("ro")
            dve.wait_ge(gffn_loaded, 16)
            norm(3, x_tok, xs, gffn)
            for n in (1, 3):
                filled_of(dve, f"tf{n}")
                drain(f"tf{n}", V.tensor_copy(hT[:, 2 * n:2 * n + 2], bank(f"tf{n}").rearrange("p (c t) -> p c t", c=2)))
            dve.wait_ge(consts, 2)
            filled_of(dve, "rt")
            drain("rt", V.tensor_tensor(lg, bank("rt")[:, 0:2 * NE].rearrange("p (t e) -> p t e", t=TT),
                                        brow.unsqueeze(1).broadcast_to([P, TT, NE]), ALU.add))
            drained_of(dve, "rt")
            for t in range(TT):
                last = V.max(top[:, t], lg[:, t])
            link(last)
            V.tensor_scalar(negtop.unsqueeze(2), top[:, :, 0:1], -1.0, None, ALU.mult).then_inc(r_top, 1)
            for t in range(TT):
                V.tensor_scalar(lge[:, t], lg[:, t], top[:, t, 3:4], None, ALU.is_equal)
                last = V.tensor_scalar(gate[:, t], lg[:, t], top[:, t, 3:4], None, ALU.is_gt)
            link(last)
            for t in range(TT):
                V.tensor_tensor_scan(lgm[:, t], ones[:, 0:NE], lge[:, t], 0.0, ALU.mult, ALU.add)
                last = V.tensor_reduce(gsum[:, t:t + 1], gate[:, t], AX.X, ALU.add)
            link(last)
            link(V.tensor_scalar(gsum[:, 0:2], gsum[:, 0:2], -1.0, float(TOPK), ALU.mult, ALU.add))
            for t in range(TT):
                last = V.scalar_tensor_tensor(out=lge[:, t], in0=lgm[:, t], scalar=gsum[:, t:t + 1], in1=lge[:, t],
                                              op0=ALU.is_le, op1=ALU.mult)
            link(last)
            link(V.tensor_tensor(mask, gate, lge, ALU.add))
            dve.wait_ge(r_exp, 1)
            link(V.tensor_tensor(gexp, gexp, mask, ALU.mult))
            link(V.tensor_reduce(gsum[:, 0:2], gexp, AX.X, ALU.add))
            link(V.reciprocal(gsum[:, 2:4], gsum[:, 0:2]))
            V.tensor_tensor(gate, gexp, gsum[:, 2:4].unsqueeze(2).broadcast_to([P, TT, NE]), ALU.mult)\
                .then_inc(r_gate, 1)
            filled_of(dve, "pos")
            link(V.tensor_copy(mT, bank("pos")[0:NE, T:2 * T]))
            link(V.scalar_tensor_tensor(out=posT, in0=bank("pos")[0:NE, 0:T], scalar=1024.0, in1=mT, op0=ALU.add,
                                        op1=ALU.mult))
            drain("pos", V.tensor_scalar(posT, posT, -1024.0, None, ALU.add))
            filled_of(dve, "cnt")
            V.tensor_copy(gateT, bank("cnt")[0:NE, 0:T])
            drain("cnt", V.tensor_copy(cnt, bank("cnt")[0:NE, T:T + 1]))
            drained_of(dve, "cnt")
            for c in range(MORE):
                last = V.tensor_scalar(ovf[:, c:c + 1], cnt, float(SLOTS * (c + 1)), None, ALU.is_gt)
            link(last)
            link(V.memset(ovs, 0.0))
            link(V.tensor_copy(ovs[:, 1:2], ovf[:, 0:1]))
            V.tensor_tensor(ovs[:, 2:3], ovf[:, 0:1], ovf[:, 1:2], ALU.add).then_inc(r_ovf, 1)
            filled_of(dve, "rank")
            drain("rank", V.tensor_copy(rank, bank("rank")[0:NE, 0:MORE]))
            drained_of(dve, "rank")
            for c in range(MORE):
                last = V.tensor_scalar(sel3[:, c], idx16[0:NE], rank[:, c:c + 1], ovf[:, c:c + 1], ALU.is_equal, ALU.mult)
            link(last)
            more = slice(NE, NE + 16)
            link(V.tensor_tensor(blksel[:, more], sel3[:, 0], sel3[:, 1], ALU.add))
            link(V.tensor_tensor(blksel[:, more], blksel[:, more], sel3[:, 2], ALU.add))
            link(V.tensor_scalar(blkoff[:, more], sel3[:, 0], -float(SLOTS), None, ALU.mult))
            link(V.scalar_tensor_tensor(out=blkoff[:, more], in0=sel3[:, 1], scalar=-float(2 * SLOTS),
                                        in1=blkoff[:, more], op0=ALU.mult, op1=ALU.add))
            V.scalar_tensor_tensor(out=blkoff[:, more], in0=sel3[:, 2], scalar=-float(3 * SLOTS),
                                   in1=blkoff[:, more], op0=ALU.mult, op1=ALU.add).then_inc(r_sel, 1)
            filled_of(dve, "meta")
            link(V.tensor_copy(metas[:, 1:17], bank("meta")[0:1, 0:16]))
            link(V.tensor_reduce(metas[:, 0:1], bank("meta")[0:1, 16:16 + MORE], AX.X, ALU.add))
            link(V.tensor_scalar(metas[:, 0:1], metas[:, 0:1], float(NE), None, ALU.add))
            drain("meta", V.tensor_copy(cnt_i[:, 0:17], metas[:, 0:17]))
            filled_of(dve, "blk")
            V.tensor_copy(pos_b, bank("blk")[:, 0:2 * BCOL].rearrange("p (t b) -> p t b", t=TT))
            drain("blk", V.tensor_copy(gate_b, bank("blk")[:, 2 * BCOL:4 * BCOL].rearrange("p (t b) -> p t b", t=TT)))
            drained_of(dve, "blk")
            V.memset(scat, 0.0).then_inc(scat_ready, 1)
            V.memset(y_slot, 0.0).then_inc(yslot_ready, 1)

            def find_slots(i):
                for t in range(TT):
                    last = V.tensor_scalar(place[:, t], iota_s[:, 0:SLOTS], pos_b[:, t, bass.ds(i, 1)], None, ALU.is_equal)
                last.then_inc(place_ready, 1)

            find_slots(0)
            nblk = dve.value_load(cnt_i[0:1, 0:1], min_val=NE, max_val=NBLK)
            with dve.Fori(0, nblk) as i:
                dve.wait_ge(yslot_ready, i + 1)
                V.tensor_copy(cur, blksel[:, bass.ds(i, 1)].broadcast_to([NE, SLOTS])).then_inc(cur_ready, 1)
                dve.wait_ge(scat_ready, i + 1)
                for t in range(TT):
                    last = V.tensor_scalar(placeg[:, t], iota_s, pos_b[:, t, bass.ds(i, 1)],
                                           gate_b[:, t, bass.ds(i, 1)], ALU.is_equal, ALU.mult)
                last.then_inc(placeg_ready, 1)
                dve.wait_ge(xg_ready, i + 1)
                find_slots(i + 1)
                dve.wait_ge(freed[eslot["gu3"]], i + 1)
                V.tensor_scalar(gact, ps[:, GBK, :], 7.0, None, ALU.min).then_inc(g_limited, 1)
                V.tensor_scalar(uact, ps[:, UBK, :], -7.0, 7.0, ALU.max, ALU.min).then_inc(g_chain, 1)
                dve.wait_ge(g_limited, i + 1)
                dve.wait_ge(g_chain, i * 2 + 1)
                V.scalar_tensor_tensor(out=uact, in0=uact, scalar=1.0, in1=gact, op0=ALU.add, op1=ALU.mult)\
                    .then_inc(g_chain, 1)
                dve.wait_ge(g_chain, i * 2 + 2)
                dve.wait_ge(sig_done, i + 1)
                V.tensor_tensor(hact, uact, sig, ALU.mult).then_inc(h_ready, 1)
                dve.wait_ge(ht_done, i + 1)
                V.tensor_copy(hactT.rearrange("p c n s -> p (c n s)"), ps[:, ZBK, :]).then_inc(hT_ready, 1)
            dve.wait_ge(fin_sq, 2)
            dve.wait_ge(gfin_loaded, 16)
            V.tensor_scalar(msq[:, 0:2], ss[:, 0:2], 1.0 / D, EPS, ALU.mult, ALU.add).then_inc(fin_v, 1)
            dve.wait_ge(fin_std, 1)
            V.reciprocal(rstd[:, 0:2], std[:, 0:2]).then_inc(fin_v, 1)
            dve.wait_ge(fin_v, 2)
            for t in range(TT):
                V.scalar_tensor_tensor(out=x_tok[:, t], in0=ps[:, YB + 2 * t:YB + 2 * t + 2, :]
                                       .rearrange("p b n -> p (b n)"), scalar=rstd[:, t:t + 1], in1=gfin,
                                       op0=ALU.mult, op1=ALU.mult).then_inc(out_ready, 1)


_INS = ["x", "mem", "g_mix", "w_in", "pe_cmp_k", "pe_cmp_v", "w_phi1_k", "w_phi2_k", "w_phi1_v", "w_phi2_v",
        "w_conv", "b_conv", "w_q_m", "w_k_m", "w_v_m", "b_i", "b_f", "mh_gain", "skip_m", "w_up_a", "w_up_b",
        "w_o_mix", "g_x", "g_mem", "w_q_x", "w_k_x", "w_v_x", "w_o_x", "g_ffn", "w_router", "b_router",
        "w_gu", "b_gu", "w_down", "b_down", "g_final"]


def kernel(**inputs):
    import numpy as _np
    import concourse.bacc as _bacc
    from concourse import mybir as _mybir
    from concourse.bass_utils import run_bass_kernel_spmd as _run

    nc = _bacc.Bacc("TRN2", target_bir_lowering=False, num_devices=1)
    arrays, args = {}, {}
    for name in _INS:
        a = _np.ascontiguousarray(inputs[name])
        arrays[f"in_{name}_dram"] = a
        args[name] = nc.dram_tensor(f"in_{name}_dram", a.shape, _mybir.dt.from_np(a.dtype), kind="ExternalInput").ap()
    out = nc.dram_tensor("out_0_dram", (1, T, D), F32, kind="ExternalOutput").ap()
    program(nc, args, out)
    r = _run(nc, [arrays], core_ids=[0])
    return r.results[0]["out_0_dram"]
```

```python
from contextlib import ExitStack

import concourse.bass as bass
from concourse import mybir

F32 = mybir.dt.float32
I32 = mybir.dt.int32
ALU = mybir.AluOpType
ACT = mybir.ActivationFunctionType
AX = mybir.AxisListType

P = 128
T = 256
TT = T // P
D = 1024
C = D // P
EPS = 1e-5
NEG = -1e30

HA, DA = 8, 64
PAIRS = HA // 2
CMP_BLOCK, CMP_STRIDE = 32, 16
NCMP = T // CMP_STRIDE - 1
CW = 16
HM, DM = 4, 128
HX = 4
NE, TOPK = 32, 4
SLOTS = 64
MORE = T // SLOTS - 1
NBLK = NE + T * TOPK // SLOTS - 1
BCOL = 48
assert NBLK < BCOL

Q0, KC0, VC0, KS0, VS0, KW0, VW0, GN0 = 0, 512, 640, 768, 896, 1024, 1152, 1280
XM0 = GN0 + 3 * HA
OP0 = XM0 + 512
IF0 = OP0 + 512
GA0 = IF0 + 2 * HM
GB0 = GA0 + D
GW = XM0 - KW0
GCOL = GW + 2 * HM

R_MIX, R_X, R_MEM, R_FFN, R_BC, R_WC, R_GAIN, R_SKIP, R_PEK, R_PEV = 0, 8, 16, 24, 32, 36, 52, 56, 64, 96

SLOT_N = 6
SLOT_W = 4096

PIECES = ["q", "kcvs", "kwg", "xm", "phik", "phiv", "op", "ga0", "ga1", "gb0", "gb1",
          "kx0", "kx1", "vx0", "vx1", "ua", "ub", "om0", "om1", "qx0", "qx1", "ox0", "ox1"]
LAST_USE = {"q": "q1", "kcvs": "ksvs", "kwg": "if", "xm": "xm1", "phik": "cmpB", "phiv": "cmpB", "op": "op1",
            "ga0": "ga1", "ga1": "ga3", "gb0": "gb1", "gb1": "gb3", "kx0": "kx1", "kx1": "kx3", "vx0": "vx1",
            "vx1": "vx3", "ua": "ub3", "ub": "ub3", "om0": "om0_1", "om1": "om1_1", "qx0": "qx1", "qx1": "qx3",
            "ox0": "ro0_1", "ox1": "ro1_1"}
DMAS = {"kwg": 2, "phik": 2, "phiv": 2}
EXPERT_PIECES = ["gu0", "gu1", "gu2", "gu3", "dn0", "dn1"]

FILL = [("ga", n) for n in range(4)] + [("gb", n) for n in range(4)] + \
       [("kx", n) for n in range(4)] + [("vx", n) for n in range(4)]


def filler_names(step):
    return [f"{k}{n}" for k, n in FILL[2 * step:2 * step + 2]]


def group_order():
    g = ["gmix", "tm0", "tm1", "tm2", "tm3", "vec", "q0", "q1", "kcvc", "ksvs", "kwvw", "gn", "if", "xm0", "xm1",
         "cmpA", "cmpB", "te0", "te1", "te2", "te3", "op0", "cmpT", "op1", "cmp2", "csA", "csB", "mt"]
    for h in range(HA + 1):
        if h >= 1:
            g += [f"ta{h - 1}", f"tb{h - 1}"]
        if h < HA:
            g += [f"sc{h}_0", f"sc{h}_1"] + filler_names(h)[:1]
        if h == 1:
            g += ["mv0", "mv1", "mq0", "mq1", "mq2", "mq3"]
        if 3 <= h <= 6:
            g += [f"mn{h - 3}"]
        if 2 <= h <= 5:
            g += [f"mb{h - 2}", f"ms{h - 2}"]
        if h >= 2 and h % 2 == 0:
            g += [f"pv{h // 2 - 1}"]
        if h < HA:
            g += filler_names(h)[1:]
        if h == HA:
            g += ["ty0", "ty1"]
    for n in range(4):
        g += [f"ua{n}", f"ub{n}"]
    g += ["om0_0", "om0_1", "om1_0", "tx0", "tx1", "om1_1", "tx2", "tx3"]
    g += ["qx0", "qx1", "sx0", "qx2", "sx1", "qx3", "sx2", "pt0", "sx3", "ox0"]
    for h in range(1, HX):
        g += [f"pt{h}", f"ox{h}"]
    g += ["ro0_0", "ro0_1", "ro1_0", "tf0", "tf1", "ro1_1", "tf2", "tf3"]
    g += ["rt", "pos", "cnt", "rank", "meta", "blk"]
    return g


GROUPS = group_order()
BANKS = 8
AT = {name: (i % BANKS, i // BANKS) for i, name in enumerate(GROUPS)}
USES = [sum(1 for b, _ in AT.values() if b == k) for k in range(BANKS)]

YB = 0
GBK, UBK, XBK, ZBK = 4, 5, 6, 7


def program(nc, A, out):
    ctx = ExitStack()
    with ctx:
        def sb(name, shape, dt=F32):
            return ctx.enter_context(nc.sbuf_tensor(name, shape, dt))

        def sem(name):
            return ctx.enter_context(nc.semaphore(name))

        ps = ctx.enter_context(nc.psum_tensor("ps", [P, BANKS, 512], F32))

        ring = sb("ring", [P, SLOT_N, SLOT_W])
        r_x = sb("r_x", [P, TT * D])
        r_mem = sb("r_mem", [P, TT * D])
        r_xs = sb("r_xs", [P, TT * D])
        r_hT = sb("r_hT", [P, C * T])
        r_memT = sb("r_memT", [P, C * T])
        r_kx = sb("r_kx", [P, C * T])
        r_ga = sb("r_ga", [P, C * T])
        r_gb = sb("r_gb", [P, C * T])
        r_q = sb("r_q", [P, PAIRS * T])
        r_p = sb("r_p", [P, 2 * 2 * T])
        r_so = sb("r_so", [P, TT * 512])
        r_xm = sb("r_xm", [P, HM * T])
        r_xc = sb("r_xc", [P, HM * T])
        r_tmp = sb("r_tmp", [P, HM * T])
        r_dm = sb("r_dm", [P, 2 * 2 * T])
        kcvc = sb("kcvc", [P, 2, T])
        kskw = sb("kskw", [P, 2, 2, T])
        vsvw = sb("vsvw", [P, 2, TT, P])
        mv = sb("mv", [P, TT, HM, DM + 4])
        vrow = sb("vrow", [P, P])
        vT = sb("vT", [P, P])
        w2 = sb("w2", [P, 2, DA])
        ident = sb("ident", [P, P])
        ones = sb("ones", [P, T])
        causal = sb("causal", [P, T])
        upper = sb("upper", [P, P])
        sm = sb("sm", [P, 512])
        cnt_i = sb("cnt_i", [1, 32], I32)

        small_at = [0]

        def small(n):
            small_at[0] += n
            assert small_at[0] <= 512
            return sm[:, small_at[0] - n:small_at[0]]

        ss, msq, std, rstd = small(8), small(8), small(8), small(8)
        rmaskc = small(2 * CW).rearrange("p (t j) -> p t j", t=TT)
        mmaskc = small(2 * CW).rearrange("p (t j) -> p t j", t=TT)
        gates = small(TT * 3 * HA).rearrange("p (t h b) -> p t h b", t=TT, b=3)
        kcT = small(2 * CW).rearrange("p (g j) -> p g j", g=2)
        bif = small(2)
        cmcol = small(16).rearrange("p (k t h) -> p k t h", k=2, t=TT)
        emcol = small(8).rearrange("p (t h) -> p t h", t=TT)
        nmax = small(4)
        rsum = small(4)
        rinv = small(4)
        fac = small(4)
        cst = small(16)
        den = small(4)
        hsum = small(8)
        hst = small(8)
        brow = small(NE)
        cst2 = small(16)
        lnm = small(8)
        nmaxx, rsumx, rinvx, rs16 = small(8), small(8), small(8), small(2)
        iota_p = small(2)

        x_tok = r_x[:].rearrange("p (t d) -> p t d", t=TT)
        pT = r_x[:].rearrange("p (b k n) -> p b k n", b=2, k=2)
        mem_tok = r_mem[:].rearrange("p (t d) -> p t d", t=TT)
        vx = mem_tok
        xs = r_xs[:].rearrange("p (t d) -> p t d", t=TT)
        mqk = r_xs[:].rearrange("p (h k t) -> p h k t", h=HM, k=2)
        hT = r_hT[:].rearrange("p (c t) -> p c t", c=C)
        memT = r_memT[:].rearrange("p (c t) -> p c t", c=C)
        oxT = memT
        kx = r_kx[:].rearrange("p (c t) -> p c t", c=C)
        wm = r_kx[:, 0:3 * HM * DM].rearrange("p (k h e) -> p k h e", k=3, h=HM)
        sga = r_ga[:].rearrange("p (c t) -> p c t", c=C)
        sgb = r_gb[:].rearrange("p (c t) -> p c t", c=C)
        rows = r_gb[0:HM, :].rearrange("p (k t) -> p k t", k=8)
        qx = sgb
        qT = r_q[:].rearrange("p (c t) -> p c t", c=PAIRS)
        yaT = qT
        pr = r_p[:].rearrange("p (t b k) -> p t b k", t=2, b=2)
        pcmp = sb("pcmp", [P, TT, HA, CW])
        vc = kcvc[:, 0, 0:P].rearrange("p (g d) -> p g d", g=2)
        mrow = kcvc[0:HM, 1]
        gmix = kcvc[0:C, 0, 0:P]
        so = r_so[:].rearrange("p (t d) -> p t d", t=TT)
        xm = r_xm[:].rearrange("p (h t) -> p h t", h=HM)
        ybT = xm
        xc = r_xc[:].rearrange("p (h t) -> p h t", h=HM)
        conv = r_tmp[:].rearrange("p (h t) -> p h t", h=HM)
        hs = r_tmp[:].rearrange("p (t h e) -> p t h e", t=TT, h=HM)
        blocks = r_dm[:, 0:2 * CMP_BLOCK * NCMP].rearrange("p (k s j) -> p k s j", k=2, s=CMP_BLOCK)
        dm = r_dm[:].rearrange("p (b s t) -> p b s t", b=2, s=2)
        px = [r_p[:].rearrange("p (t m) -> p t m", t=4), r_tmp[:].rearrange("p (t m) -> p t m", t=4)]
        wr = r_p[:, 0:C * NE].rearrange("p (c e) -> p c e", c=C)
        hid_rows, hidT, hid2 = r_p[:, 0:P], r_p[:, P:2 * P], r_p[:, 2 * P:3 * P]
        gelT = r_p[:, 3 * P:4 * P].rearrange("p (g k j) -> p g k j", g=2, k=2)
        pxT = r_dm[:].rearrange("p (b m t) -> p b m t", b=2, m=2)
        junk = {"mix": r_hT, "mem": r_memT, "x": r_xs, "ffn": r_xs}

        lg = r_gb[:, 0:64].rearrange("p (t e) -> p t e", t=TT)
        lgm = r_gb[:, 64:128].rearrange("p (t e) -> p t e", t=TT)
        top = r_gb[:, 128:144].rearrange("p (t e) -> p t e", t=TT)
        mask = r_gb[:, 144:208].rearrange("p (t e) -> p t e", t=TT)
        gexp = r_gb[:, 208:272].rearrange("p (t e) -> p t e", t=TT)
        gate = r_gb[:, 272:336].rearrange("p (t e) -> p t e", t=TT)
        gsum = r_gb[:, 336:340]
        negtop = r_gb[:, 340:342]
        posT = r_gb[0:NE, 352:608]
        gateT = r_gb[0:NE, 608:864]
        cnt = r_gb[0:NE, 864:865]
        ovf = r_gb[0:NE, 868:868 + MORE]
        ovs = r_gb[0:NE, 872:872 + MORE]
        sel3 = r_gb[0:NE, 880:880 + MORE * 16].rearrange("p (c b) -> p c b", c=MORE)
        rank = r_gb[0:NE, 928:928 + MORE]
        blksel = r_gb[0:NE, 944:944 + BCOL]
        blkoff = r_gb[0:NE, 992:992 + BCOL]
        idx16 = r_gb[:, 1040:1056]
        strict = r_gb[:, 1056:1056 + T]
        mT = r_gb[0:NE, 1312:1568]
        metas = r_gb[0:1, 1568:1568 + 32]
        eidx = r_gb[:, 1600:1602]
        lge = r_gb[:, 1608:1672].rearrange("p (t e) -> p t e", t=TT)
        pos_b = r_q[:, 0:TT * BCOL].rearrange("p (t b) -> p t b", t=TT)
        gate_b = r_q[:, TT * BCOL:2 * TT * BCOL].rearrange("p (t b) -> p t b", t=TT)
        iota_s = r_q[:, 256:256 + 2 * SLOTS]
        cur = r_q[0:NE, 400:400 + SLOTS]
        bgu_rows = r_ga[0:NE, :]
        bdn_rows = r_so[0:NE, :]
        gfin = r_xm[:]
        gffn = r_xc[:]
        xg = r_memT[:, 0:512].rearrange("p (c s) -> p c s", c=C)
        gact, uact, sig, hact = (r_memT[:, 512:1024], r_memT[:, 1024:1536], r_memT[:, 1536:2048], r_kx[:, 0:512])
        hactT = r_kx[:, 512:1024].rearrange("p (c n s) -> p c n s", c=4, n=2)
        y_slot = r_kx[:, 1024:1536]
        place = r_dm[:, 0:128].rearrange("p (t s) -> p t s", t=TT)
        placeg = r_dm[:, 128:384].rearrange("p (t s) -> p t s", t=TT)
        scat = r_dm[:, 384:640]

        loaded = [sem(f"loaded{i}") for i in range(SLOT_N)]
        freed = [sem(f"freed{i}") for i in range(SLOT_N)]
        filled = [sem(f"filled{i}") for i in range(BANKS)]
        drained = [sem(f"drained{i}") for i in range(BANKS)]
        vrow_clear, vec_loaded, gmix_loaded = sem("vrow_clear"), sem("vec_loaded"), sem("gmix_loaded")
        x_loaded, mem_loaded = sem("x_loaded"), sem("mem_loaded")
        small_loaded, wm_loaded, x_again, wr_loaded = sem("small_loaded"), sem("wm_loaded"), sem("x_again"), sem("wr_loaded")
        late_loaded, gfin_loaded, gffn_loaded = sem("late_loaded"), sem("gfin_loaded"), sem("gffn_loaded")
        consts, p_chain = sem("consts"), sem("p_chain")
        v_chain, a_chain = sem("v_chain"), sem("a_chain")
        sq_done, msq_ready = sem("sq_done"), sem("msq_ready")
        std_ready, xs_ready = sem("std_ready"), sem("xs_ready")
        gate_e, blk_ready, gelu_in = sem("gate_e"), sem("blk_ready"), sem("gelu_in")
        gelu_e, gelu_done = sem("gelu_e"), sem("gelu_done")
        fabs_ready, softp_ready = sem("fabs_ready"), sem("softp_ready")
        rows_ready, em_done = sem("rows_ready"), sem("em_done")
        conv_ready, silu_e, xc_ready = sem("conv_ready"), sem("silu_e"), sem("xc_ready")
        cm_in, cm_e, cm_done = sem("cm_in"), sem("cm_e"), sem("cm_done")
        s_max, s_exp = sem("s_max"), sem("s_exp")
        s_fac, s_prob = sem("s_fac"), sem("s_prob")
        dm_e, var_ready, lstd_ready = sem("dm_e"), sem("var_ready"), sem("lstd_ready")
        hn_ready, merged_ready = sem("hn_ready"), sem("merged_ready")
        cx_max, cx_inv, cx_prob = sem("cx_max"), sem("cx_inv"), sem("cx_prob")
        r_top, r_exp, r_gate = sem("r_top"), sem("r_exp"), sem("r_gate")
        r_ovf, r_sel, y_begun = sem("r_ovf"), sem("r_sel"), sem("y_begun")
        place_ready, placeg_ready = sem("place_ready"), sem("placeg_ready")
        gathered, xg_ready = sem("gathered"), sem("xg_ready")
        g_limited, sig_done, h_ready = sem("g_limited"), sem("sig_done"), sem("h_ready")
        cur_ready, ht_done, hT_ready, g_chain = sem("cur_ready"), sem("ht_done"), sem("hT_ready"), sem("g_chain")
        pt_done, scat_ready = sem("pt_done"), sem("scat_ready")
        yslot_ready, scattered = sem("yslot_ready"), sem("scattered")
        fin_sq, fin_v, fin_std = sem("fin_sq"), sem("fin_v"), sem("fin_std")
        out_ready, out_sem = sem("out_ready"), sem("out_sem")

        slot_of, need = {}, {}
        dmas = [0] * SLOT_N
        for n, name in enumerate(PIECES):
            s = n % SLOT_N
            dmas[s] += DMAS.get(name, 1)
            slot_of[name], need[name] = s, 16 * dmas[s]
        eslot = {name: (len(PIECES) + j) % SLOT_N for j, name in enumerate(EXPERT_PIECES)}

        def bank(name):
            return ps[:, AT[name][0], :]

        def drained_of(eng, name):
            b, turn = AT[name]
            eng.wait_ge(drained[b], turn + 1)

        def filled_of(eng, name):
            b, turn = AT[name]
            eng.wait_ge(filled[b], turn + 1)

        def wslot(name, rows_, width):
            return ring[:, slot_of[name], 0:rows_ * width].rearrange("p (c n) -> p c n", c=rows_)

        w_in = A["w_in"][0].rearrange("(c p) n -> p c n", p=P)

        def cols(w, a, b):
            return w[0].rearrange("(c p) n -> p c n", p=P)[:, :, a:b]

        gu_dram = A["w_gu"].rearrange("l e (j k p) n -> (l e) j p k n", k=2, p=P)
        dn_dram = A["w_down"].rearrange("l e (j k p) n -> (l e) j p k n", k=4, p=P)

        block = ctx.enter_context(nc.Block())

        @block.sync
        def _(sp):
            sp.dma_start(gmix, A["g_mix"][0].rearrange("(c p) -> c p", p=P)).then_inc(gmix_loaded, 16)
            x_dram = A["x"][0].rearrange("(t p) d -> p t d", p=P)
            for t in range(TT):
                sp.dma_start(x_tok[:, t], x_dram[:, t]).then_inc(x_loaded, 16)

            def piece(name):
                s = slot_of[name]
                n = PIECES.index(name)
                if n >= SLOT_N:
                    filled_of(sp, LAST_USE[PIECES[n - SLOT_N]])
                w8 = wslot(name, C, 512)
                if name == "q":
                    pairs = [(w8, w_in[:, :, Q0:Q0 + 512])]
                elif name == "kcvs":
                    pairs = [(w8, w_in[:, :, KC0:KC0 + 512])]
                elif name == "kwg":
                    w = wslot(name, C, GCOL)
                    pairs = [(w[:, :, 0:GW], w_in[:, :, KW0:XM0]), (w[:, :, GW:GCOL], w_in[:, :, IF0:GA0])]
                elif name == "xm":
                    pairs = [(w8, w_in[:, :, XM0:XM0 + 512])]
                elif name in ("phik", "phiv"):
                    w = wslot(name, CMP_BLOCK, P)
                    src = A["w_phi1_" + name[-1]][0].rearrange("(s d) n -> d s n", d=DA)
                    pairs = [(w[g * DA:(g + 1) * DA], src) for g in range(2)]
                elif name == "op":
                    pairs = [(w8, w_in[:, :, OP0:OP0 + 512])]
                elif name[:2] in ("ga", "gb"):
                    a = (GA0 if name[1] == "a" else GB0) + 512 * int(name[2])
                    pairs = [(w8, w_in[:, :, a:a + 512])]
                elif name == "ua":
                    pairs = [(wslot(name, PAIRS, D), A["w_up_a"][0].rearrange("(c p) n -> p c n", p=P))]
                elif name == "ub":
                    pairs = [(wslot(name, HM, D), A["w_up_b"][0].rearrange("(c p) n -> p c n", p=P))]
                else:
                    src = {"kx": "w_k_x", "vx": "w_v_x", "om": "w_o_mix", "qx": "w_q_x", "ox": "w_o_x"}[name[:2]]
                    a = 512 * int(name[2])
                    pairs = [(w8, cols(A[src], a, a + 512))]
                for dst, src in pairs:
                    sp.dma_start(dst, src).then_inc(loaded[s], 16)

            piece("q")
            sp.wait_ge(vrow_clear, 1)
            for name, r, n in (("g_x", R_X, C), ("g_mem", R_MEM, C), ("g_ffn", R_FFN, C),
                               ("b_conv", R_BC, HM), ("mh_gain", R_GAIN, HM), ("skip_m", R_SKIP, HM)):
                sp.dma_start(vrow[r:r + n, :], A[name][0].rearrange("(c p) -> c p", p=P)).then_inc(vec_loaded, 16)
            sp.dma_start(vrow[R_WC:R_WC + 4 * HM, :], A["w_conv"][0].rearrange("r (c p) -> (r c) p", p=P))\
                .then_inc(vec_loaded, 16)
            for r, name in ((R_PEK, "pe_cmp_k"), (R_PEV, "pe_cmp_v")):
                for g in range(2):
                    sp.dma_start(vrow[r:r + CMP_BLOCK, g * DA:(g + 1) * DA], A[name][0]).then_inc(vec_loaded, 16)
            for name in PIECES[1:]:
                piece(name)

            def expert(e, i):
                for j, name in enumerate(EXPERT_PIECES):
                    s = eslot[name]
                    if i is None:
                        filled_of(sp, LAST_USE[PIECES[len(PIECES) + j - SLOT_N]])
                    else:
                        sp.wait_ge(freed[s], i)
                    if j < 4:
                        dst, src = ring[:, s].rearrange("p (k n) -> p k n", k=2), gu_dram[e, j]
                    else:
                        dst, src = ring[:, s].rearrange("p (k n) -> p k n", k=4), dn_dram[e, j - 4]
                    sp.dma_start(dst, src).then_inc(loaded[s], 16)

            expert(0, None)
            with sp.Fori(1, NE) as i:
                expert(i, i)
            drained_of(sp, "meta")
            nblk = sp.value_load(cnt_i[0:1, 0:1], min_val=NE, max_val=NBLK)
            with sp.If(nblk > NE):
                with sp.Fori(NE, nblk) as i:
                    e = sp.value_load(cnt_i[0:1, bass.ds(i - (NE - 1), 1)], min_val=0, max_val=NE - 1)
                    expert(e, i)
            sp.wait_ge(out_ready, 2)
            sp.dma_start(out[0].rearrange("(t p) d -> p t d", p=P), x_tok).then_inc(out_sem, 16)
            sp.wait_ge(out_sem, 16)

        @block.gpsimd
        def _(pool):
            count = [0]

            def link(ins):
                count[0] += 1
                ins.then_inc(p_chain, 1)
                pool.wait_ge(p_chain, count[0])

            pool.memset(vrow[:], 0.0).then_inc(vrow_clear, 1)
            pool.memset(hid_rows, 0.0)
            link(pool.memset(ident[:], 0.0))
            pool.memset(ones[:], 1.0)
            pool.memset(sm[:], 0.0)
            pool.memset(cnt_i[:], 0)
            pool.memset(mv[:], 1.0)
            pool.memset(pcmp[:], 0.0)
            pool.memset(causal[:], 0.0)
            link(pool.affine_select(out=ident[:], in_=ident[:], compare_op=ALU.not_equal, fill=1.0, base=0,
                                    pattern=[[-1, P]], channel_multiplier=1))
            pool.affine_select(out=causal[:, P:T], in_=causal[:, P:T], compare_op=ALU.is_ge, fill=NEG, base=0,
                               pattern=[[-1, P]], channel_multiplier=1)
            pool.affine_select(out=upper[:], in_=ones[:, 0:P], compare_op=ALU.is_ge, fill=0.0, base=0,
                               pattern=[[1, P]], channel_multiplier=-1)
            for t in range(TT):
                pool.affine_select(out=rmaskc[:, t], in_=rmaskc[:, t], compare_op=ALU.is_ge, fill=NEG,
                                   base=P * t - (CMP_BLOCK - 1), pattern=[[-CMP_STRIDE, CW]], channel_multiplier=1)
                last = pool.affine_select(out=mmaskc[:, t], in_=ones[:, 0:CW], compare_op=ALU.is_ge, fill=0.0,
                                          base=P * t - (CMP_BLOCK - 1), pattern=[[-CMP_STRIDE, CW]],
                                          channel_multiplier=1)
            last.then_inc(consts, 1)
            filled_of(pool, "pv3")
            pool.dma_start(x_tok, A["x"][0].rearrange("(t p) d -> p t d", p=P)).then_inc(x_again, 16)
            filled_of(pool, "om1_1")
            pool.dma_start(bgu_rows, A["b_gu"][0]).then_inc(late_loaded, 16)
            pool.dma_start(bdn_rows, A["b_down"][0]).then_inc(late_loaded, 16)
            pool.dma_start(gfin, A["g_final"].rearrange("(a d) -> a d", a=1).partition_broadcast(P))\
                .then_inc(gfin_loaded, 16)
            pool.dma_start(gffn, A["g_ffn"].partition_broadcast(P)[:, 0]).then_inc(gffn_loaded, 16)
            filled_of(pool, "sx3")
            filled_of(pool, "pt1")
            pool.dma_start(wr, A["w_router"][0].rearrange("(c p) e -> p c e", p=P)).then_inc(wr_loaded, 16)
            pool.iota(idx16, pattern=[[1, 16]], base=0, channel_multiplier=0, allow_small_or_imprecise_dtypes=True)
            pool.iota(eidx, pattern=[[0, 2]], base=0, channel_multiplier=1, allow_small_or_imprecise_dtypes=True)
            pool.iota(iota_s, pattern=[[0, 2], [1, SLOTS]], base=0, channel_multiplier=0, allow_small_or_imprecise_dtypes=True)
            link(pool.memset(blksel, 0.0))
            pool.memset(blkoff, 0.0)
            pool.affine_select(out=blksel[:, 0:NE], in_=blksel[:, 0:NE], compare_op=ALU.not_equal, fill=1.0,
                               base=0, pattern=[[-1, NE]], channel_multiplier=1)
            pool.affine_select(out=strict, in_=ones[:], compare_op=ALU.is_gt, fill=0.0, base=0,
                               pattern=[[1, T]], channel_multiplier=-1).then_inc(consts, 1)

        @block.scalar
        def _(act):
            count = [0]

            def link(ins):
                count[0] += 1
                ins.then_inc(a_chain, 1)
                act.wait_ge(a_chain, count[0])

            m_dram = A["mem"][0].rearrange("(t p) d -> p t d", p=P)
            for t in range(TT):
                act.dma_start(mem_tok[:, t], m_dram[:, t]).then_inc(mem_loaded, 16)
            act.wait_ge(consts, 1)
            act.dma_start(bif[0:HM, 0:1], A["b_i"][0].rearrange("(h a) -> h a", a=1)).then_inc(small_loaded, 16)
            act.dma_start(bif[0:HM, 1:2], A["b_f"][0].rearrange("(h a) -> h a", a=1)).then_inc(small_loaded, 16)
            act.dma_start(w2[:, 0], A["w_phi2_k"][0]).then_inc(small_loaded, 16)
            act.dma_start(w2[:, 1], A["w_phi2_v"][0]).then_inc(small_loaded, 16)
            act.dma_start(brow, A["b_router"].partition_broadcast(P)[:, 0]).then_inc(small_loaded, 16)
            for k, name in enumerate(("w_q_m", "w_k_m", "w_v_m")):
                act.dma_start(wm[:, k], A[name][0].rearrange("h d e -> d h e")).then_inc(wm_loaded, 16)

            def squares(n, name, src):
                for t in range(TT):
                    nc.scalar.activation(junk[name][:, t * D:(t + 1) * D], src[:, t], ACT.Square,
                                         accum_out=ss[:, 2 * n + t:2 * n + t + 1]).then_inc(sq_done, 1)
                act.wait_ge(msq_ready, n + 1)
                nc.scalar.activation(std[:, 2 * n:2 * n + 2], msq[:, 2 * n:2 * n + 2], ACT.Sqrt).then_inc(std_ready, 1)

            def gained(name, dst, g0, n):
                filled_of(act, name)
                b, _ = AT[name]
                for j in range(2):
                    last = nc.scalar.activation(dst[:, 2 * n + j], bank(name)[:, j * T:(j + 1) * T], ACT.Copy,
                                                scale=vT[:, g0 + 2 * n + j:g0 + 2 * n + j + 1])
                last.then_inc(drained[b], 1)

            def copy(name, dst, src, func=ACT.Copy, **kw):
                filled_of(act, name)
                nc.scalar.activation(dst, src, func, **kw).then_inc(drained[AT[name][0]], 1)

            act.wait_ge(consts, 1)
            act.wait_ge(x_loaded, 32)
            squares(0, "mix", x_tok)
            drained_of(act, "gmix")
            gained("tm0", hT, R_MIX, 0)
            gained("tm2", hT, R_MIX, 2)
            act.wait_ge(mem_loaded, 32)
            squares(1, "mem", mem_tok)
            copy("q0", qT[:, 0:2], bank("q0").rearrange("p (c t) -> p c t", c=2))
            copy("q1", qT[:, 2:4], bank("q1").rearrange("p (c t) -> p c t", c=2))
            copy("kcvc", kcvc[:], bank("kcvc").rearrange("p (c t) -> p c t", c=2))
            filled_of(act, "kwvw")
            for half in range(2):
                for g in range(2):
                    nc.scalar.activation(kskw[half * DA:(half + 1) * DA, 1, g], bank("kwvw")[g * DA:(g + 1) * DA, 0:T],
                                         ACT.Copy)
            nc.scalar.activation(vsvw[:, 1], bank("kwvw")[:, T:2 * T].rearrange("p (t e) -> p t e", t=TT), ACT.Copy)\
                .then_inc(drained[AT["kwvw"][0]], 1)
            drained_of(act, "gn")
            nc.scalar.activation(gates[:].rearrange("p t h b -> p (t h b)"),
                                 gates[:].rearrange("p t h b -> p (t h b)"), ACT.Exp, scale=-1.0).then_inc(gate_e, 1)
            copy("xm0", xm[:, 0:2], bank("xm0").rearrange("p (c t) -> p c t", c=2))
            act.wait_ge(fabs_ready, 1)
            link(nc.scalar.activation(rows[:, 3], rows[:, 2], ACT.Exp, scale=-1.0))
            nc.scalar.activation(rows[:, 3], rows[:, 3], ACT.Ln, bias=1.0).then_inc(softp_ready, 1)
            act.wait_ge(conv_ready, 1)
            nc.scalar.activation(r_xc[:], r_tmp[:], ACT.Exp, scale=-1.0).then_inc(silu_e, 1)
            drained_of(act, "vec")
            gained("te0", memT, R_MEM, 0)
            gained("te2", memT, R_MEM, 2)
            copy("op0", so[:, 0], bank("op0"), ACT.Exp, scale=-1.0)
            act.wait_ge(gelu_in, 1)
            nc.scalar.activation(hid2, hid2, ACT.Exp, scale=-2.0 * 0.7978845608028654).then_inc(gelu_e, 1)
            copy("op1", so[:, 1], bank("op1"), ACT.Exp, scale=-1.0)
            act.wait_ge(cm_in, 1)
            nc.scalar.activation(pcmp[:], pcmp[:], ACT.Exp).then_inc(cm_e, 1)
            drained_of(act, "mt")
            nc.scalar.activation(emcol, cmcol[:, 1], ACT.Exp, scale=-1.0).then_inc(em_done, 1)

            def filler(name):
                kind, n = name[:2], int(name[2])
                if kind == "ga":
                    copy(name, sga[:, 2 * n:2 * n + 2], bank(name).rearrange("p (c t) -> p c t", c=2),
                         ACT.Exp, scale=-1.0)
                elif kind == "gb":
                    copy(name, sgb[:, 2 * n:2 * n + 2], bank(name).rearrange("p (c t) -> p c t", c=2),
                         ACT.Exp, scale=-1.0)
                elif kind == "kx":
                    copy(name, kx[:, 2 * n:2 * n + 2], bank(name).rearrange("p (c t) -> p c t", c=2))

            for h in range(HA + 1):
                if h >= 1:
                    copy(f"ta{h - 1}", pT[:, (h - 1) % 2, 0], bank(f"ta{h - 1}"))
                if h < HA:
                    for t in range(TT):
                        act.wait_ge(s_max, 2 * h + t + 1)
                        for b in range(2):
                            last = nc.scalar.activation(pr[:, t, b, 0:P * (t + 1)], pr[:, t, b, 0:P * (t + 1)],
                                                        ACT.Exp, bias=nmax[:, 2 * t + b:2 * t + b + 1],
                                                        accum_out=rsum[:, 2 * t + b:2 * t + b + 1])
                        last.then_inc(s_exp, 1)
                    for name in filler_names(h)[:1]:
                        filler(name)
                    for t in range(TT):
                        act.wait_ge(s_fac, 2 * h + t + 1)
                        for b in range(2):
                            last = nc.scalar.activation(pr[:, t, b, 0:P * (t + 1)], pr[:, t, b, 0:P * (t + 1)],
                                                        ACT.Copy, scale=fac[:, 2 * t + b:2 * t + b + 1])
                        last.then_inc(s_prob, 1)
                if h == 1:
                    for m in range(HM):
                        filled_of(act, f"mq{m}")
                        nc.scalar.activation(mqk[:, m, 0], bank(f"mq{m}")[:, 0:T], ACT.Copy)
                        nc.scalar.activation(mqk[:, m, 1], bank(f"mq{m}")[:, T:2 * T], ACT.Copy,
                                             scale=float(DM) ** -0.5).then_inc(drained[AT[f"mq{m}"][0]], 1)
                if 2 <= h <= 5:
                    m = h - 2
                    drained_of(act, f"mb{m}")
                    nc.scalar.activation(r_dm[:, (m % 2) * 512:(m % 2) * 512 + 384],
                                         r_dm[:, (m % 2) * 512:(m % 2) * 512 + 384], ACT.Exp,
                                         scale=-1.0).then_inc(dm_e, 1)
                if h == 7:
                    act.wait_ge(var_ready, 1)
                    nc.scalar.activation(hst, lnm, ACT.Sqrt).then_inc(lstd_ready, 1)
                if h >= 2 and h % 2 == 0:
                    c = h // 2 - 1
                    copy(f"pv{c}", yaT[:, c], bank(f"pv{c}")[:, 0:T])
                if h < HA:
                    for name in filler_names(h)[1:]:
                        filler(name)

            for n in range(4):
                drained_of(act, f"om{n // 2}_{n % 2}")
            squares(2, "x", x_tok)
            copy("qx0", qx[:, 0:2], bank("qx0").rearrange("p (c t) -> p c t", c=2))
            copy("qx1", qx[:, 2:4], bank("qx1").rearrange("p (c t) -> p c t", c=2))

            def cross_exp(h):
                act.wait_ge(cx_max, h + 1)
                for t in range(TT):
                    j = 2 * (h % 2) + t
                    last = nc.scalar.activation(px[h // 2][:, j], bank(f"sx{h}")[:, t * T:(t + 1) * T], ACT.Exp,
                                                bias=nmaxx[:, 2 * h + t:2 * h + t + 1], scale=rs16[:, t:t + 1],
                                                accum_out=rsumx[:, 2 * h + t:2 * h + t + 1])
                last.then_inc(drained[AT[f"sx{h}"][0]], 1)

            def cross_scale(h):
                act.wait_ge(cx_inv, h + 1)
                for t in range(TT):
                    j = 2 * (h % 2) + t
                    last = nc.scalar.activation(px[h // 2][:, j], px[h // 2][:, j], ACT.Copy,
                                                scale=rinvx[:, 2 * h + t:2 * h + t + 1])
                last.then_inc(cx_prob, 1)

            def cross_out(h):
                copy(f"ox{h}", oxT[:, 2 * h:2 * h + 2], bank(f"ox{h}").rearrange("p (c t) -> p c t", c=2))

            cross_exp(0)
            copy("qx2", qx[:, 4:6], bank("qx2").rearrange("p (c t) -> p c t", c=2))
            cross_scale(0)
            cross_exp(1)
            copy("qx3", qx[:, 6:8], bank("qx3").rearrange("p (c t) -> p c t", c=2))
            cross_scale(1)
            cross_exp(2)
            cross_scale(2)
            cross_exp(3)
            cross_scale(3)
            for h in range(HX):
                cross_out(h)
            for n in range(4):
                drained_of(act, f"ro{n // 2}_{n % 2}")
            squares(3, "ffn", x_tok)
            act.wait_ge(r_top, 1)
            for t in range(TT):
                last = nc.scalar.activation(gexp[:, t], lg[:, t], ACT.Exp, bias=negtop[:, t:t + 1])
            last.then_inc(r_exp, 1)
            drained_of(act, "meta")
            act.wait_ge(gathered, 1)
            nc.scalar.activation(xg, ps[:, XBK, :].rearrange("p (c s) -> p c s", c=C), ACT.Copy).then_inc(xg_ready, 1)
            nblk = act.value_load(cnt_i[0:1, 0:1], min_val=NE, max_val=NBLK)
            with act.Fori(0, nblk) as i:
                act.wait_ge(g_limited, i + 1)
                nc.scalar.activation(sig, gact, ACT.Sigmoid, scale=1.702).then_inc(sig_done, 1)
                act.wait_ge(pt_done, i + 1)
                nc.scalar.activation(scat, ps[:, GBK, 0:T], ACT.Copy).then_inc(scat_ready, 1)
                act.wait_ge(gathered, i + 2)
                nc.scalar.activation(xg, ps[:, XBK, :].rearrange("p (c s) -> p c s", c=C), ACT.Copy)\
                    .then_inc(xg_ready, 1)
                act.wait_ge(freed[eslot["dn1"]], i + 1)
                nc.scalar.activation(y_slot, ps[:, ZBK, :], ACT.Copy).then_inc(yslot_ready, 1)
            act.wait_ge(scattered, nblk + 1)
            for t in range(TT):
                nc.scalar.activation(r_hT[:, t * D:(t + 1) * D],
                                     ps[:, YB + 2 * t:YB + 2 * t + 2, :].rearrange("p b n -> p (b n)"), ACT.Square,
                                     accum_out=ss[:, t:t + 1]).then_inc(fin_sq, 1)
            act.wait_ge(fin_v, 1)
            nc.scalar.activation(std[:, 0:2], msq[:, 0:2], ACT.Sqrt).then_inc(fin_std, 1)

        @block.tensor
        def _(pe):
            mm = nc.tensor.matmul

            def begin(name):
                b, turn = AT[name]
                if turn:
                    pe.wait_ge(drained[b], turn)
                return ps[:, b, :]

            def end(name, ins):
                ins.then_inc(filled[AT[name][0]], 1)

            def weights(name):
                pe.wait_ge(loaded[slot_of[name]], need[name])

            def transpose4(name, src, n):
                o = begin(name)
                for j in range(2):
                    for t in range(TT):
                        last = nc.tensor.transpose(o[:, j * T + t * P:j * T + t * P + P],
                                                   src[:, t, (2 * n + j) * P:(2 * n + j + 1) * P], ident[:])
                end(name, last)

            def feature_group(name, ws, src, kk=C, ready=None):
                o = begin(name)
                for j, w in enumerate(ws):
                    for k in range(kk):
                        if ready and j == 0:
                            ready(k)
                        last = mm(o[:, j * T:(j + 1) * T], w(k), src[:, k, :], start=(k == 0), stop=(k == kk - 1))
                return last

            def token_part(o, w, n, src, t, ready=None):
                for k in range(C):
                    if ready:
                        ready(k)
                    last = mm(o, src[:, k, t * P:(t + 1) * P], w[:, k, 0:n], start=(k == 0), stop=(k == C - 1))
                return last

            def stationary(w, j):
                return lambda k: w[:, k, j * P:(j + 1) * P]

            def chunks_of(prefix):
                return lambda k: drained_of(pe, f"{prefix}{k // 2}")

            pe.wait_ge(consts, 1)
            pe.wait_ge(gmix_loaded, 16)
            end("gmix", nc.tensor.transpose(begin("gmix")[:, 0:C], gmix, ident[0:C, 0:C]))
            pe.wait_ge(xs_ready, 2)
            for n in range(4):
                transpose4(f"tm{n}", xs, n)
            pe.wait_ge(vec_loaded, 16 * 11)
            end("vec", nc.tensor.transpose(begin("vec")[:, 0:P], vrow[:], ident[:]))
            weights("q")
            w = wslot("q", C, 512)
            for n in range(2):
                last = feature_group(f"q{n}", [stationary(w, 2 * n), stationary(w, 2 * n + 1)], hT, ready=chunks_of("tm"))
                end(f"q{n}", last)
            weights("kcvs")
            w = wslot("kcvs", C, 512)
            end("kcvc", feature_group("kcvc", [stationary(w, 0), stationary(w, 1)], hT))
            feature_group("ksvs", [stationary(w, 2)], hT)
            for t in range(TT):
                last = token_part(bank("ksvs")[:, T + t * P:T + t * P + P], w[:, :, 384:512], P, hT, t)
            end("ksvs", last)
            weights("kwg")
            w = wslot("kwg", C, GCOL)
            feature_group("kwvw", [stationary(w, 0)], hT)
            for t in range(TT):
                last = token_part(bank("kwvw")[:, T + t * P:T + t * P + P], w[:, :, P:2 * P], P, hT, t)
            end("kwvw", last)
            o = begin("gn")
            for t in range(TT):
                last = token_part(o[:, t * 24:(t + 1) * 24], w[:, :, 2 * P:2 * P + 24], 24, hT, t)
            end("gn", last)
            o = begin("if")
            for k in range(C):
                for j in range(2):
                    last = mm(o[32 * j:32 * j + HM, j * T:(j + 1) * T], w[:, k, GW + HM * j:GW + HM * j + HM], hT[:, k, :],
                              start=(k == 0), stop=(k == C - 1))
            end("if", last)
            weights("xm")
            w = wslot("xm", C, 512)
            for n in range(2):
                end(f"xm{n}", feature_group(f"xm{n}", [stationary(w, 2 * n), stationary(w, 2 * n + 1)], hT))
            weights("phik")
            weights("phiv")
            pe.wait_ge(blk_ready, 2)
            oo = [begin("cmpA"), begin("cmpB")]
            wk, wv = wslot("phik", CMP_BLOCK, P), wslot("phiv", CMP_BLOCK, P)
            for s in range(CMP_BLOCK):
                for g in range(2):
                    for kind in range(2):
                        a = 32 * (2 * g + kind)
                        last = mm(oo[g][a:a + NCMP, 0:P], blocks[g * DA:(g + 1) * DA, kind, s],
                                  (wk, wv)[kind][g * DA:(g + 1) * DA, s], start=(s == 0), stop=(s == CMP_BLOCK - 1))
                        if s == CMP_BLOCK - 1 and kind == 1:
                            end(("cmpA", "cmpB")[g], last)
            pe.wait_ge(xs_ready, 4)
            for n in range(4):
                transpose4(f"te{n}", mem_tok, n)
            weights("op")
            w = wslot("op", C, 512)
            end("op0", token_part(begin("op0"), w, 512, hT, 0))
            drained_of(pe, "cmpA")
            drained_of(pe, "cmpB")
            end("cmpT", nc.tensor.transpose(begin("cmpT")[:, 0:P], hid_rows, ident[:]))
            end("op1", token_part(begin("op1"), w, 512, hT, 1))
            pe.wait_ge(gelu_done, 1)
            pe.wait_ge(small_loaded, 16 * 5)
            o = begin("cmp2")
            for g in range(2):
                for half in range(2):
                    mm(o[half * DA:(half + 1) * DA, g * CW:g * CW + NCMP], w2[:, 0], gelT[:, g, 0, 0:NCMP],
                       start=True, stop=True)
            for g in range(2):
                last = mm(o[0:NCMP, 2 * CW + g * DA:2 * CW + (g + 1) * DA], gelT[:, g, 1, 0:NCMP], w2[:, 1],
                          start=True, stop=True)
            end("cmp2", last)
            drained_of(pe, "cmp2")
            drained_of(pe, "q0")
            drained_of(pe, "q1")
            for half in range(2):
                name = ("csA", "csB")[half]
                o = begin(name)
                for t in range(TT):
                    for c in range(PAIRS):
                        a = (t * PAIRS + c) * CW
                        last = mm(o[:, a:a + NCMP], qT[half * DA:(half + 1) * DA, c, t * P:(t + 1) * P],
                                  kcT[half * DA:(half + 1) * DA, c // 2, 0:NCMP], start=True, stop=True)
                end(name, last)
            pe.wait_ge(rows_ready, 1)
            o = begin("mt")
            for kind in range(2):
                for t in range(TT):
                    last = nc.tensor.transpose(o[:, (kind * TT + t) * HM:(kind * TT + t + 1) * HM],
                                               rows[:, 5 + 2 * kind, t * P:(t + 1) * P], ident[0:HM, 0:HM])
            end("mt", last)

            def filler(name):
                kind, n = name[:2], int(name[2])
                half = f"{kind}{n // 2}"
                weights(half)
                w = wslot(half, C, 512)
                if kind in ("ga", "gb"):
                    src = hT
                else:
                    src = memT
                    for m in range(4):
                        drained_of(pe, f"te{m}")
                if kind == "vx":
                    last = token_part(begin(name), w, 512, memT, n % 2)
                else:
                    j = 2 * (n % 2)
                    last = feature_group(name, [stationary(w, j), stationary(w, j + 1)], src)
                end(name, last)
            for h in range(HA + 1):
                if h >= 1:
                    m = h - 1
                    pe.wait_ge(s_prob, 2 * m + 2)
                    o = begin(f"ta{m}")
                    for b in range(2):
                        for t in range(TT):
                            last = nc.tensor.transpose(o[:, b * T + t * P:b * T + t * P + P], pr[:, t, b, 0:P], ident[:])
                    end(f"ta{m}", last)
                    o = begin(f"tb{m}")
                    for b in range(2):
                        nc.tensor.transpose(o[:, b * P:(b + 1) * P], pr[:, 1, b, P:T], ident[:])
                    pe.wait_ge(cm_done, 1)
                    for t in range(TT):
                        last = nc.tensor.transpose(o[0:NCMP, T + t * P:T + t * P + P], pcmp[:, t, m, 0:NCMP], ident[:])
                    end(f"tb{m}", last)
                if h < HA:
                    c, half, g = h // 2, h % 2, h // PAIRS
                    drained_of(pe, "ksvs")
                    drained_of(pe, "kwvw")
                    for t in range(TT):
                        o = begin(f"sc{h}_{t}")
                        n = P * (t + 1)
                        for b in range(2):
                            last = mm(o[:, b * n:(b + 1) * n], qT[half * DA:(half + 1) * DA, c, t * P:(t + 1) * P],
                                      kskw[half * DA:(half + 1) * DA, b, g, 0:n], start=True, stop=True)
                        end(f"sc{h}_{t}", last)
                    for name in filler_names(h)[:1]:
                        filler(name)
                if h == 1:
                    pe.wait_ge(wm_loaded, 48)
                    pe.wait_ge(xc_ready, 1)
                    drained_of(pe, "xm0")
                    for t in range(TT):
                        o = begin(f"mv{t}")
                        for m in range(HM):
                            last = mm(o[:, m * DM:(m + 1) * DM], xm[:, m, t * P:(t + 1) * P], wm[:, 2, m],
                                      start=True, stop=True)
                        end(f"mv{t}", last)
                    for m in range(HM):
                        o = begin(f"mq{m}")
                        for k in range(2):
                            last = mm(o[:, k * T:(k + 1) * T], wm[:, k, m], xc[:, m], start=True, stop=True)
                        end(f"mq{m}", last)
                if 3 <= h <= 6:
                    m = h - 3
                    drained_of(pe, f"ms{m}")
                    drained_of(pe, "mv0")
                    drained_of(pe, "mv1")
                    o = begin(f"mn{m}")
                    b = m % 2
                    mm(o[:, 0:DM + 1], dm[:, b, 0, 0:P], mv[:, 0, m, 0:DM + 1], start=True, stop=True)
                    mm(o[:, T:T + DM + 1], dm[:, b, 0, P:T], mv[:, 0, m, 0:DM + 1], start=True, stop=False)
                    last = mm(o[:, T:T + DM + 1], dm[:, b, 1, 0:P], mv[:, 1, m, 0:DM + 1], start=False, stop=True)
                    end(f"mn{m}", last)
                if 2 <= h <= 5:
                    m = h - 2
                    drained_of(pe, f"mq{m}")
                    o = begin(f"mb{m}")
                    end(f"mb{m}", mm(o[:, 0:T], ident[0:HM, m:m + 1].broadcast_to([HM, P]), mrow,
                                     start=True, stop=True))
                    o = begin(f"ms{m}")
                    mm(o[:, 0:T], mqk[:, m, 1, 0:P], mqk[:, m, 0], start=True, stop=True)
                    last = mm(o[:, T:T + P], mqk[:, m, 1, P:T], mqk[:, m, 0, P:T], start=True, stop=True)
                    end(f"ms{m}", last)
                if h >= 2 and h % 2 == 0:
                    c = h // 2 - 1
                    o = begin(f"pv{c}")
                    g = c // 2
                    for m in (2 * c, 2 * c + 1):
                        drained_of(pe, f"ta{m}")
                        drained_of(pe, f"tb{m}")
                    vg = slice(g * DA, (g + 1) * DA)
                    for b in range(2):
                        for half in range(2):
                            mm(o[half * DA:(half + 1) * DA, 0:T], vsvw[:, b, 0, vg], pT[:, half, 0, b * T:(b + 1) * T],
                               start=(b == 0), stop=False)
                    for b in range(2):
                        for half in range(2):
                            mm(o[half * DA:(half + 1) * DA, P:T], vsvw[:, b, 1, vg],
                               pT[:, half, 1, b * P:(b + 1) * P], start=False, stop=False)
                    for half in range(2):
                        last = mm(o[half * DA:(half + 1) * DA, 0:T], vc[0:NCMP, g],
                                  pT[0:NCMP, half, 1, T:2 * T], start=False, stop=True)
                    end(f"pv{c}", last)
                if h < HA:
                    for name in filler_names(h)[1:]:
                        filler(name)
            pe.wait_ge(hn_ready, 1)
            for n in range(2):
                o = begin(f"ty{n}")
                for j in range(2):
                    for t in range(TT):
                        last = nc.tensor.transpose(o[:, j * T + t * P:j * T + t * P + P], hs[:, t, 2 * n + j], ident[:])
                end(f"ty{n}", last)
            weights("ua")
            weights("ub")
            drained_of(pe, "pv3")
            drained_of(pe, "ty0")
            drained_of(pe, "ty1")
            for n in range(4):
                w = wslot("ua", PAIRS, D)
                end(f"ua{n}", feature_group(f"ua{n}", [stationary(w, 2 * n), stationary(w, 2 * n + 1)], yaT, PAIRS))
                w = wslot("ub", HM, D)
                end(f"ub{n}", feature_group(f"ub{n}", [stationary(w, 2 * n), stationary(w, 2 * n + 1)], ybT, HM))

            def token_group(prefix, piece_name, src, n, t, ready):
                weights(f"{piece_name}{n}")
                name = f"{prefix}{n}_{t}"
                end(name, token_part(begin(name), wslot(f"{piece_name}{n}", C, 512), 512, src, t, ready))

            def project_and_turn(prefix, piece_name, src, turned, ready):
                token_group(prefix, piece_name, src, 0, 0, ready)
                token_group(prefix, piece_name, src, 0, 1, ready)
                token_group(prefix, piece_name, src, 1, 0, ready)
                drained_of(pe, f"{prefix}0_0")
                drained_of(pe, f"{prefix}0_1")
                transpose4(f"{turned}0", x_tok, 0)
                transpose4(f"{turned}1", x_tok, 1)
                token_group(prefix, piece_name, src, 1, 1, ready)
                drained_of(pe, f"{prefix}1_0")
                drained_of(pe, f"{prefix}1_1")
                transpose4(f"{turned}2", x_tok, 2)
                transpose4(f"{turned}3", x_tok, 3)

            project_and_turn("om", "om", sga, "tx", lambda k: pe.wait_ge(merged_ready, k // 2 + 1))

            def cross_query(n):
                weights(f"qx{n // 2}")
                w = wslot(f"qx{n // 2}", C, 512)
                j = 2 * (n % 2)
                end(f"qx{n}", feature_group(f"qx{n}", [stationary(w, j), stationary(w, j + 1)], hT,
                                            ready=chunks_of("tx")))

            def cross_scores(h):
                drained_of(pe, f"qx{h}")
                o = begin(f"sx{h}")
                for t in range(TT):
                    for k in range(2):
                        last = mm(o[:, t * T:(t + 1) * T], qx[:, 2 * h + k, t * P:(t + 1) * P], kx[:, 2 * h + k],
                                  start=(k == 0), stop=(k == 1))
                end(f"sx{h}", last)

            def cross_turn(h):
                pe.wait_ge(cx_prob, h + 1)
                o = begin(f"pt{h}")
                for mt in range(2):
                    for t in range(TT):
                        last = nc.tensor.transpose(o[:, mt * T + t * P:mt * T + t * P + P],
                                                   px[h // 2][:, 2 * (h % 2) + t, mt * P:(mt + 1) * P], ident[:])
                end(f"pt{h}", last)

            def cross_values(h):
                drained_of(pe, f"pt{h}")
                o = begin(f"ox{h}")
                for k in range(2):
                    for mt in range(2):
                        last = mm(o[:, k * T:(k + 1) * T], vx[:, mt, (2 * h + k) * P:(2 * h + k + 1) * P],
                                  pxT[:, h % 2, mt], start=(mt == 0), stop=(mt == 1))
                end(f"ox{h}", last)

            for n in range(4):
                drained_of(pe, f"kx{n}")
                drained_of(pe, f"vx{n}")
            cross_query(0)
            cross_query(1)
            cross_scores(0)
            cross_query(2)
            cross_scores(1)
            cross_query(3)
            cross_scores(2)
            cross_turn(0)
            cross_scores(3)
            cross_values(0)
            for h in range(1, HX):
                cross_turn(h)
                cross_values(h)
            project_and_turn("ro", "ox", oxT, "tf", chunks_of("ox"))
            pe.wait_ge(wr_loaded, 16)
            o = begin("rt")
            for t in range(TT):
                last = token_part(o[:, t * NE:(t + 1) * NE], wr, NE, hT, t, chunks_of("tf"))
            end("rt", last)
            pe.wait_ge(r_gate, 1)
            pe.wait_ge(consts, 2)
            o = begin("pos")
            mm(o[0:NE, 0:T], mask[:, 0], strict, start=True, stop=False)
            mm(o[0:NE, P:T], mask[:, 1], strict[:, 0:P], start=False, stop=True)
            for t in range(TT):
                last = mm(o[0:NE, T + t * P:T + t * P + P], mask[:, t], ident[:], start=True, stop=True)
            end("pos", last)
            o = begin("cnt")
            for t in range(TT):
                mm(o[0:NE, t * P:(t + 1) * P], gate[:, t], ident[:], start=True, stop=True)
            for t in range(TT):
                last = mm(o[0:NE, T:T + 1], mask[:, t], ones[:, 0:1], start=(t == 0), stop=(t == 1))
            end("cnt", last)
            pe.wait_ge(r_ovf, 1)
            o = begin("rank")
            mm(o[0:NE, 0:MORE], strict[0:NE, 0:NE], ovf, start=True, stop=False)
            last = mm(o[0:NE, 0:MORE], ones[0:NE, 0:NE], ovs, start=False, stop=True)
            end("rank", last)
            pe.wait_ge(r_sel, 1)
            o = begin("meta")
            mm(o[0:1, 0:16], eidx[0:NE, 0:1], blksel[:, NE:NE + 16], start=True, stop=True)
            last = mm(o[0:1, 16:16 + MORE], ones[0:NE, 0:1], ovf, start=True, stop=True)
            end("meta", last)
            o = begin("blk")
            for t in range(TT):
                mm(o[:, t * BCOL:(t + 1) * BCOL], posT[:, t * P:(t + 1) * P], blksel, start=True, stop=False)
                mm(o[:, t * BCOL:(t + 1) * BCOL], ones[0:NE, 0:P], blkoff, start=False, stop=True)
                last = mm(o[:, (2 + t) * BCOL:(3 + t) * BCOL], gateT[:, t * P:(t + 1) * P], blksel,
                          start=True, stop=True)
            end("blk", last)
            for b in range(BANKS):
                pe.wait_ge(drained[b], USES[b])
            for t in range(TT):
                for n in range(2):
                    last = mm(ps[:, YB + 2 * t + n, :], ident[:], x_tok[:, t, n * 512:(n + 1) * 512],
                              start=True, stop=False, skip_group_check=True)
            last.then_inc(y_begun, 1)

            pe.wait_ge(xs_ready, 6)

            def gather(i):
                pe.wait_ge(place_ready, i + 1)
                for c in range(C):
                    for t in range(TT):
                        last = mm(ps[:, XBK, c * SLOTS:(c + 1) * SLOTS], xs[:, t, c * P:(c + 1) * P],
                                  place[:, t], start=(t == 0), stop=(t == 1))
                last.then_inc(gathered, 1)

            def scatter():
                for t in range(TT):
                    for n in range(2):
                        half = slice(n * SLOTS, (n + 1) * SLOTS)
                        last = mm(ps[:, YB + 2 * t + n, :], scat[half, t * P:(t + 1) * P], y_slot[half, :],
                                  start=False, stop=False, skip_group_check=True)
                last.then_inc(scattered, 1)

            def halves(bk, stationary_, moving, start, stop):
                for n in range(2):
                    last = mm(ps[n * SLOTS:(n + 1) * SLOTS, bk, :], stationary_, moving(n), start=start, stop=stop,
                              skip_group_check=True)
                return last

            gather(0)
            pe.wait_ge(late_loaded, 32)
            drained_of(pe, "meta")
            nblk = pe.value_load(cnt_i[0:1, 0:1], min_val=NE, max_val=NBLK)
            with pe.Fori(0, nblk) as i:
                pe.wait_ge(cur_ready, i + 1)
                for b in range(2):
                    halves(GBK + b, cur, lambda n: bgu_rows[:, b * D + n * 512:b * D + n * 512 + 512], True, False)
                pe.wait_ge(xg_ready, i + 1)
                for j in range(4):
                    s = eslot[EXPERT_PIECES[j]]
                    pe.wait_ge(loaded[s], i * 16 + (16 * dmas[s] + 16))
                    w = ring[:, s].rearrange("p (k n) -> p k n", k=2)
                    for k in range(2):
                        kk = 2 * j + k
                        for b in range(2):
                            last = halves(GBK + b, xg[:, kk],
                                          lambda n: w[:, k, b * D + n * 512:b * D + n * 512 + 512], False, kk == 7)
                    last.then_inc(freed[s], 1)
                pe.wait_ge(scat_ready, i + 1)
                pe.wait_ge(yslot_ready, i + 1)
                scatter()
                pe.wait_ge(h_ready, i + 1)
                for c in range(4):
                    last = nc.tensor.transpose(ps[:, ZBK, c * P:(c + 1) * P], hact[:, c * P:(c + 1) * P], ident[:])
                last.then_inc(ht_done, 1)
                pe.wait_ge(placeg_ready, i + 1)
                for t in range(TT):
                    last = nc.tensor.transpose(ps[:, GBK, t * P:(t + 1) * P], placeg[:, t], ident[:])
                last.then_inc(pt_done, 1)
                gather(i + 1)
                pe.wait_ge(hT_ready, i + 1)
                halves(ZBK, cur, lambda n: bdn_rows[:, n * 512:n * 512 + 512], True, False)
                for j in range(2):
                    s = eslot[EXPERT_PIECES[4 + j]]
                    pe.wait_ge(loaded[s], i * 16 + (16 * dmas[s] + 16))
                    w = ring[:, s].rearrange("p (k n) -> p k n", k=4)
                    for k in range(4):
                        last = halves(ZBK, hactT[:, k, j], lambda n: w[:, k, n * 512:n * 512 + 512], False,
                                      j == 1 and k == 3)
                    last.then_inc(freed[s], 1)
            pe.wait_ge(yslot_ready, nblk + 1)
            pe.wait_ge(scat_ready, nblk + 1)
            scatter()

        @block.vector
        def _(dve):
            count = [0]
            V = nc.vector

            def link(ins):
                count[0] += 1
                ins.then_inc(v_chain, 1)
                dve.wait_ge(v_chain, count[0])

            def drain(name, ins):
                ins.then_inc(drained[AT[name][0]], 1)

            def norm(n, src, dst, gain=None):
                dve.wait_ge(sq_done, 2 * n + 2)
                V.tensor_scalar(msq[:, 2 * n:2 * n + 2], ss[:, 2 * n:2 * n + 2], 1.0 / D, EPS, ALU.mult, ALU.add)\
                    .then_inc(msq_ready, 1)
                dve.wait_ge(std_ready, n + 1)
                link(V.reciprocal(rstd[:, 2 * n:2 * n + 2], std[:, 2 * n:2 * n + 2]))
                for t in range(TT if dst is not None else 0):
                    r = rstd[:, 2 * n + t:2 * n + t + 1]
                    if gain is None:
                        ins = V.tensor_scalar(dst[:, t], src[:, t], r, None, ALU.mult)
                    else:
                        ins = V.scalar_tensor_tensor(out=dst[:, t], in0=src[:, t], scalar=r, in1=gain, op0=ALU.mult,
                                                     op1=ALU.mult)
                    ins.then_inc(xs_ready, 1)

            def gained(name, dst, g0, n):
                filled_of(dve, name)
                g = vT[:, g0 + 2 * n:g0 + 2 * n + 2].unsqueeze(2).broadcast_to([P, 2, T])
                drain(name, V.tensor_tensor(dst[:, 2 * n:2 * n + 2],
                                            bank(name).rearrange("p (c t) -> p c t", c=2), g, ALU.mult))

            def col(r):
                return vT[:, r:r + 1]

            dve.wait_ge(consts, 1)
            norm(0, x_tok, xs)
            filled_of(dve, "gmix")
            drain("gmix", V.tensor_copy(vT[:, 0:C], bank("gmix")[:, 0:C]))
            drained_of(dve, "gmix")
            gained("tm1", hT, R_MIX, 1)
            gained("tm3", hT, R_MIX, 3)
            filled_of(dve, "vec")
            drain("vec", V.tensor_copy(vT[:, C:P], bank("vec")[:, C:P]))
            drained_of(dve, "vec")
            dve.wait_ge(mem_loaded, 32)
            norm(1, mem_tok, mem_tok)
            filled_of(dve, "ksvs")
            for half in range(2):
                for g in range(2):
                    V.tensor_copy(kskw[half * DA:(half + 1) * DA, 0, g], bank("ksvs")[g * DA:(g + 1) * DA, 0:T])
            drain("ksvs", V.tensor_copy(vsvw[:, 0], bank("ksvs")[:, T:2 * T].rearrange("p (t e) -> p t e", t=TT)))
            drained_of(dve, "kcvc")
            for kind, r in ((0, R_PEK), (1, R_PEV)):
                sub = kcvc[:, kind].rearrange("p (j s) -> p s j", s=CMP_STRIDE)
                for half in range(2):
                    s0 = half * CMP_STRIDE
                    pe_b = vT[:, r + s0:r + s0 + CMP_STRIDE].unsqueeze(2).broadcast_to([P, CMP_STRIDE, NCMP])
                    last = V.tensor_tensor(blocks[:, kind, s0:s0 + CMP_STRIDE], sub[:, :, half:half + NCMP], pe_b,
                                           ALU.add)
                last.then_inc(blk_ready, 1)
            gflat = gates[:].rearrange("p t h b -> p (t h b)")
            filled_of(dve, "gn")
            drain("gn", V.tensor_copy(gflat, bank("gn")[:, 0:2 * 24]))
            filled_of(dve, "if")
            dve.wait_ge(small_loaded, 16 * 5)
            V.tensor_scalar(rows[:, 0], bank("if")[0:HM, 0:T], bif[0:HM, 0:1], None, ALU.add)
            drain("if", V.tensor_copy(rows[:, 1], bank("if")[32:32 + HM, T:2 * T]))
            drained_of(dve, "if")
            link(V.tensor_scalar(rows[:, 1], rows[:, 1], bif[0:HM, 1:2], None, ALU.add))
            V.scalar_tensor_tensor(out=rows[:, 2], in0=rows[:, 1], scalar=-1.0, in1=rows[:, 1], op0=ALU.mult,
                                   op1=ALU.max).then_inc(fabs_ready, 1)
            filled_of(dve, "xm1")
            drain("xm1", V.tensor_copy(xm[:, 2:4], bank("xm1").rearrange("p (c t) -> p c t", c=2)))
            drained_of(dve, "xm0")
            drained_of(dve, "xm1")
            for h in range(HM):
                last = V.tensor_scalar(conv[:, h], xm[:, h], col(R_WC + 3 * HM + h), col(R_BC + h), ALU.mult, ALU.add)
            for r in range(2, -1, -1):
                link(last)
                s = 3 - r
                for h in range(HM):
                    last = V.scalar_tensor_tensor(out=conv[:, h, s:T], in0=xm[:, h, 0:T - s],
                                                  scalar=col(R_WC + r * HM + h), in1=conv[:, h, s:T],
                                                  op0=ALU.mult, op1=ALU.add)
            last.then_inc(conv_ready, 1)
            dve.wait_ge(gate_e, 1)
            link(V.tensor_scalar(gflat, gflat, 1.0, None, ALU.add))
            link(V.reciprocal(gflat, gflat))
            dve.wait_ge(softp_ready, 1)
            link(V.scalar_tensor_tensor(out=rows[:, 1], in0=rows[:, 1], scalar=0.0, in1=rows[:, 3], op0=ALU.min,
                                        op1=ALU.subtract))
            link(V.tensor_tensor_scan(rows[:, 4], ones[0:HM], rows[:, 1], 0.0, ALU.mult, ALU.add))
            link(V.tensor_tensor(rows[:, 5], rows[:, 0], rows[:, 4], ALU.subtract))
            link(V.tensor_tensor_scan(mrow, ones[0:HM], rows[:, 5], 0.0, ALU.mult, ALU.max))
            V.tensor_tensor(rows[:, 7], rows[:, 4], mrow, ALU.add).then_inc(rows_ready, 1)
            dve.wait_ge(silu_e, 1)
            link(V.tensor_scalar(r_xc[:], r_xc[:], 1.0, None, ALU.add))
            link(V.reciprocal(r_xc[:], r_xc[:]))
            V.tensor_tensor(r_xc[:], r_xc[:], r_tmp[:], ALU.mult).then_inc(xc_ready, 1)
            for g in range(2):
                name = ("cmpA", "cmpB")[g]
                filled_of(dve, name)
                for kind in range(2):
                    a = 32 * (2 * g + kind)
                    last = V.tensor_copy(hid_rows[a:a + NCMP], bank(name)[a:a + NCMP, 0:P])
                drain(name, last)
            gained("te1", memT, R_MEM, 1)
            gained("te3", memT, R_MEM, 3)
            filled_of(dve, "cmpT")
            drain("cmpT", V.tensor_copy(hidT, bank("cmpT")[:, 0:P]))
            drained_of(dve, "cmpT")
            link(V.tensor_tensor(hid2, hidT, hidT, ALU.mult))
            link(V.tensor_scalar(hid2, hid2, 0.044715, 1.0, ALU.mult, ALU.add))
            V.tensor_tensor(hid2, hid2, hidT, ALU.mult).then_inc(gelu_in, 1)
            dve.wait_ge(gelu_e, 1)
            link(V.tensor_scalar(hid2, hid2, 1.0, None, ALU.add))
            link(V.reciprocal(hid2, hid2))
            V.tensor_tensor(gelT.rearrange("p g k j -> p (g k j)"), hidT, hid2, ALU.mult).then_inc(gelu_done, 1)
            filled_of(dve, "cmp2")
            V.tensor_copy(kcT[:, :, 0:NCMP], bank("cmp2")[:, 0:2 * CW].rearrange("p (g j) -> p g j", g=2)[:, :, 0:NCMP])
            drain("cmp2", V.tensor_copy(vc[0:NCMP], bank("cmp2")[0:NCMP, 2 * CW:2 * CW + P]
                                        .rearrange("p (g d) -> p g d", g=2)))
            for g in range(2):
                name = ("csA", "csB")[g]
                filled_of(dve, name)
                for t in range(TT):
                    s = bank(name)[:, t * PAIRS * CW:(t + 1) * PAIRS * CW].rearrange("p (c j) -> p c j", j=CW)
                    m = rmaskc[:, t, 0:NCMP].unsqueeze(1).broadcast_to([P, PAIRS, NCMP])
                    last = V.scalar_tensor_tensor(out=pcmp[:, t].rearrange("p (c e) j -> p c e j", e=2)[:, :, g, 0:NCMP],
                                                  in0=s[:, :, 0:NCMP], scalar=float(DA) ** -0.5, in1=m,
                                                  op0=ALU.mult, op1=ALU.add)
                drain(name, last)
            drained_of(dve, "csB")
            pflat = pcmp[:].rearrange("p t h j -> p (t h) j")
            valid = pflat[:, :, 0:NCMP]
            link(V.tensor_reduce(cst, valid, AX.X, ALU.max))
            V.tensor_tensor(valid, valid, cst.unsqueeze(2).broadcast_to([P, TT * HA, NCMP]), ALU.subtract)\
                .then_inc(cm_in, 1)
            dve.wait_ge(cm_e, 1)
            link(V.tensor_reduce(cst, valid, AX.X, ALU.add))
            link(V.reciprocal(cst, cst))
            link(V.tensor_tensor(cst.rearrange("p (t h) -> p t h", t=TT), cst.rearrange("p (t h) -> p t h", t=TT),
                                 gates[:, :, :, 0], ALU.mult))
            link(V.tensor_tensor(valid, valid, cst.unsqueeze(2).broadcast_to([P, TT * HA, NCMP]), ALU.mult))
            for t in range(TT):
                last = V.tensor_tensor(pcmp[:, t, :, 0:NCMP], pcmp[:, t, :, 0:NCMP],
                                       mmaskc[:, t, 0:NCMP].unsqueeze(1).broadcast_to([P, HA, NCMP]), ALU.mult)
            last.then_inc(cm_done, 1)
            filled_of(dve, "mt")
            drain("mt", V.tensor_copy(cmcol, bank("mt")[:, 0:16].rearrange("p (k t h) -> p k t h", k=2, t=TT)))
            drained_of(dve, "mt")
            drained_of(dve, "op0")
            drained_of(dve, "op1")
            link(V.tensor_scalar(r_so[:], r_so[:], 1.0, None, ALU.add))
            link(V.reciprocal(r_so[:], r_so[:]))

            def filler(name):
                kind, n = name[:2], int(name[2])
                if kind == "vx":
                    filled_of(dve, name)
                    drain(name, V.tensor_copy(vx[:, n % 2, (n // 2) * 512:(n // 2) * 512 + 512], bank(name)))

            def sigmoid_rest(r):
                link(V.tensor_scalar(r[:], r[:], 1.0, None, ALU.add))
                link(V.reciprocal(r[:], r[:]))

            for h in range(HA + 1):
                if h >= 1:
                    m = h - 1
                    filled_of(dve, f"tb{m}")
                    V.tensor_copy(pT[:, m % 2, 1, 0:T], bank(f"tb{m}")[:, 0:T])
                    drain(f"tb{m}", V.tensor_copy(pT[0:NCMP, m % 2, 1, T:2 * T], bank(f"tb{m}")[0:NCMP, T:2 * T]))
                if h < HA:
                    for t in range(TT):
                        name, n = f"sc{h}_{t}", P * (t + 1)
                        filled_of(dve, name)
                        m = causal[:, T - n:T].unsqueeze(1).broadcast_to([P, 2, n])
                        drain(name, V.scalar_tensor_tensor(
                            out=pr[:, t, :, 0:n], in0=bank(name)[:, 0:2 * n].rearrange("p (b n) -> p b n", b=2),
                            scalar=float(DA) ** -0.5, in1=m, op0=ALU.mult, op1=ALU.add))
                        drained_of(dve, name)
                        V.tensor_reduce(nmax[:, 2 * t:2 * t + 2], pr[:, t, :, 0:n], AX.X, ALU.max, negate=True)\
                            .then_inc(s_max, 1)
                    for name in filler_names(h)[:1]:
                        filler(name)
                    for t in range(TT):
                        dve.wait_ge(s_exp, 2 * h + t + 1)
                        link(V.reciprocal(rinv[:, 2 * t:2 * t + 2], rsum[:, 2 * t:2 * t + 2]))
                        V.tensor_tensor(fac[:, 2 * t:2 * t + 2], rinv[:, 2 * t:2 * t + 2], gates[:, t, h, 1:3],
                                        ALU.mult).then_inc(s_fac, 1)
                if h == 1:
                    for t in range(TT):
                        filled_of(dve, f"mv{t}")
                        drain(f"mv{t}", V.tensor_copy(mv[:, t, :, 0:DM], bank(f"mv{t}").rearrange("p (h e) -> p h e", h=HM)))
                if 3 <= h <= 6:
                    m = h - 3
                    name = f"mn{m}"
                    filled_of(dve, name)
                    num = bank(name).rearrange("p (t e) -> p t e", t=TT)
                    link(V.tensor_scalar(den[:, 0:2].unsqueeze(2), num[:, :, DM:DM + 1], -1.0, None, ALU.mult))
                    link(V.tensor_tensor(den[:, 0:2].unsqueeze(2), num[:, :, DM:DM + 1], den[:, 0:2].unsqueeze(2), ALU.max))
                    dve.wait_ge(em_done, 1)
                    link(V.tensor_tensor(den[:, 0:2], den[:, 0:2], emcol[:, :, m], ALU.max))
                    link(V.reciprocal(den[:, 2:4], den[:, 0:2]))
                    for t in range(TT):
                        last = V.scalar_tensor_tensor(out=hs[:, t, m], in0=num[:, t, 0:DM],
                                                      scalar=den[:, 2 + t:3 + t], in1=so[:, t, m * DM:(m + 1) * DM],
                                                      op0=ALU.mult, op1=ALU.mult,
                                                      accum_out=hsum[:, t * HM + m:t * HM + m + 1])
                    drain(name, last)
                if 2 <= h <= 5:
                    m = h - 2
                    name = f"mb{m}"
                    filled_of(dve, name)
                    if m >= 2:
                        filled_of(dve, f"mn{m - 2}")
                    V.tensor_scalar(dm[:, m % 2, 0], bank(name)[:, 0:T], cmcol[:, 0, 0, m:m + 1], 0.0,
                                    ALU.subtract, ALU.max)
                    drain(name, V.tensor_scalar(dm[:, m % 2, 1, 0:P], bank(name)[:, P:T], cmcol[:, 0, 1, m:m + 1],
                                                0.0, ALU.subtract, ALU.max))
                    name = f"ms{m}"
                    filled_of(dve, name)
                    dve.wait_ge(dm_e, m + 1)
                    link(V.tensor_tensor(dm[:, m % 2, :, 0:P], dm[:, m % 2, :, 0:P],
                                         upper[:].unsqueeze(1).broadcast_to([P, 2, P]), ALU.mult))
                    flat = r_dm[:, (m % 2) * 512:(m % 2) * 512 + 384]
                    drain(name, V.tensor_tensor(flat, flat, bank(name)[:, 0:384], ALU.mult))
                if h == 6:
                    for m in range(HM):
                        drained_of(dve, f"mn{m}")
                    link(V.tensor_scalar(hsum, hsum, 1.0 / DM, None, ALU.mult))
                    h3 = hs[:].rearrange("p t h e -> p (t h) e")
                    link(V.tensor_tensor(h3, h3, hsum.unsqueeze(2).broadcast_to([P, TT * HM, DM]), ALU.subtract))
                    sq = r_xm[:].rearrange("p (h e) -> p h e", e=DM)
                    link(V.tensor_tensor(sq, h3, h3, ALU.mult))
                    link(V.tensor_reduce(lnm, sq, AX.X, ALU.add))
                    V.tensor_scalar(lnm, lnm, 1.0 / DM, EPS, ALU.mult, ALU.add).then_inc(var_ready, 1)
                    for m in range(HM):
                        V.tensor_scalar(ybT[:, m], xc[:, m], col(R_SKIP + m), None, ALU.mult)
                if h == 7:
                    dve.wait_ge(lstd_ready, 1)
                    link(V.reciprocal(hst, hst))
                    V.tensor_tensor(h3, h3, hst.unsqueeze(2).broadcast_to([P, TT * HM, DM]), ALU.mult)\
                        .then_inc(hn_ready, 1)
                if h == 4:
                    for n in range(4):
                        drained_of(dve, f"ga{n}")
                    sigmoid_rest(r_ga)
                if h == 5:
                    for n in range(4):
                        drained_of(dve, f"gb{n}")
                    sigmoid_rest(r_gb)
                if h < HA:
                    for name in filler_names(h)[1:]:
                        filler(name)
            for n in range(2):
                filled_of(dve, f"ty{n}")
                for j in range(2):
                    m = 2 * n + j
                    last = V.scalar_tensor_tensor(out=ybT[:, m], in0=bank(f"ty{n}")[:, j * T:(j + 1) * T],
                                                  scalar=col(R_GAIN + m), in1=ybT[:, m], op0=ALU.mult, op1=ALU.add)
                drain(f"ty{n}", last)
            for n in range(4):
                for name, g in ((f"ua{n}", sga), (f"ub{n}", sgb)):
                    filled_of(dve, name)
                    drain(name, V.tensor_tensor(g[:, 2 * n:2 * n + 2], bank(name).rearrange("p (c t) -> p c t", c=2),
                                                g[:, 2 * n:2 * n + 2], ALU.mult))
                drained_of(dve, f"ub{n}")
                V.tensor_tensor(sga[:, 2 * n:2 * n + 2], sga[:, 2 * n:2 * n + 2], sgb[:, 2 * n:2 * n + 2], ALU.add)\
                    .then_inc(merged_ready, 1)

            def residual(prefix):
                for n in range(2):
                    for t in range(TT):
                        name = f"{prefix}{n}_{t}"
                        filled_of(dve, name)
                        xv = x_tok[:, t, n * 512:(n + 1) * 512]
                        drain(name, V.tensor_tensor(xv, bank(name), xv, ALU.add))
                for n in range(4):
                    drained_of(dve, f"{prefix}{n // 2}_{n % 2}")

            dve.wait_ge(x_again, 16)
            residual("om")
            for n in range(4):
                gained(f"tx{n}", hT, R_X, n)
            norm(2, None, None)
            link(V.tensor_scalar(rs16, rstd[:, 4:6], float(2 * P) ** -0.5, None, ALU.mult))

            def cross_max(h):
                name = f"sx{h}"
                j = slice(2 * h, 2 * h + 2)
                filled_of(dve, name)
                link(V.tensor_reduce(nmaxx[:, j], bank(name).rearrange("p (t m) -> p t m", t=TT), AX.X, ALU.max,
                                     negate=True))
                V.tensor_tensor(nmaxx[:, j], nmaxx[:, j], rs16, ALU.mult).then_inc(cx_max, 1)

            def cross_inv(h):
                drained_of(dve, f"sx{h}")
                V.reciprocal(rinvx[:, 2 * h:2 * h + 2], rsumx[:, 2 * h:2 * h + 2]).then_inc(cx_inv, 1)

            def cross_turned(h):
                filled_of(dve, f"pt{h}")
                drain(f"pt{h}", V.tensor_copy(pxT[:, h % 2], bank(f"pt{h}").rearrange("p (m t) -> p m t", m=2)))

            cross_max(0)
            cross_inv(0)
            cross_max(1)
            cross_inv(1)
            cross_max(2)
            cross_inv(2)
            cross_turned(0)
            cross_max(3)
            cross_inv(3)
            for h in range(1, HX):
                if h >= 2:
                    filled_of(dve, f"ox{h - 2}")
                cross_turned(h)
            residual("ro")
            for n in range(4):
                gained(f"tf{n}", hT, R_FFN, n)
            dve.wait_ge(gffn_loaded, 16)
            norm(3, x_tok, xs, gffn)
            dve.wait_ge(consts, 2)
            filled_of(dve, "rt")
            for t in range(TT):
                last = V.scalar_tensor_tensor(out=lg[:, t], in0=bank("rt")[:, t * NE:(t + 1) * NE],
                                              scalar=rstd[:, 6 + t:7 + t], in1=brow, op0=ALU.mult, op1=ALU.add)
            drain("rt", last)
            drained_of(dve, "rt")
            for t in range(TT):
                last = V.max(top[:, t], lg[:, t])
            link(last)
            V.tensor_scalar(negtop.unsqueeze(2), top[:, :, 0:1], -1.0, None, ALU.mult).then_inc(r_top, 1)
            for t in range(TT):
                V.tensor_scalar(lge[:, t], lg[:, t], top[:, t, 3:4], None, ALU.is_equal)
                last = V.tensor_scalar(gate[:, t], lg[:, t], top[:, t, 3:4], None, ALU.is_gt)
            link(last)
            for t in range(TT):
                V.tensor_tensor_scan(lgm[:, t], ones[:, 0:NE], lge[:, t], 0.0, ALU.mult, ALU.add)
                last = V.tensor_reduce(gsum[:, t:t + 1], gate[:, t], AX.X, ALU.add)
            link(last)
            link(V.tensor_scalar(gsum[:, 0:2], gsum[:, 0:2], -1.0, float(TOPK), ALU.mult, ALU.add))
            for t in range(TT):
                last = V.scalar_tensor_tensor(out=lge[:, t], in0=lgm[:, t], scalar=gsum[:, t:t + 1], in1=lge[:, t],
                                              op0=ALU.is_le, op1=ALU.mult)
            link(last)
            link(V.tensor_tensor(mask, gate, lge, ALU.add))
            dve.wait_ge(r_exp, 1)
            link(V.tensor_tensor(gexp, gexp, mask, ALU.mult))
            link(V.tensor_reduce(gsum[:, 0:2], gexp, AX.X, ALU.add))
            link(V.reciprocal(gsum[:, 2:4], gsum[:, 0:2]))
            V.tensor_tensor(gate, gexp, gsum[:, 2:4].unsqueeze(2).broadcast_to([P, TT, NE]), ALU.mult)\
                .then_inc(r_gate, 1)
            filled_of(dve, "pos")
            link(V.tensor_copy(mT, bank("pos")[0:NE, T:2 * T]))
            link(V.scalar_tensor_tensor(out=posT, in0=bank("pos")[0:NE, 0:T], scalar=1024.0, in1=mT, op0=ALU.add,
                                        op1=ALU.mult))
            drain("pos", V.tensor_scalar(posT, posT, -1024.0, None, ALU.add))
            filled_of(dve, "cnt")
            V.tensor_copy(gateT, bank("cnt")[0:NE, 0:T])
            drain("cnt", V.tensor_copy(cnt, bank("cnt")[0:NE, T:T + 1]))
            drained_of(dve, "cnt")
            for c in range(MORE):
                last = V.tensor_scalar(ovf[:, c:c + 1], cnt, float(SLOTS * (c + 1)), None, ALU.is_gt)
            link(last)
            link(V.memset(ovs, 0.0))
            link(V.tensor_copy(ovs[:, 1:2], ovf[:, 0:1]))
            V.tensor_tensor(ovs[:, 2:3], ovf[:, 0:1], ovf[:, 1:2], ALU.add).then_inc(r_ovf, 1)
            filled_of(dve, "rank")
            drain("rank", V.tensor_copy(rank, bank("rank")[0:NE, 0:MORE]))
            drained_of(dve, "rank")
            for c in range(MORE):
                last = V.tensor_scalar(sel3[:, c], idx16[0:NE], rank[:, c:c + 1], ovf[:, c:c + 1], ALU.is_equal, ALU.mult)
            link(last)
            more = slice(NE, NE + 16)
            link(V.tensor_tensor(blksel[:, more], sel3[:, 0], sel3[:, 1], ALU.add))
            link(V.tensor_tensor(blksel[:, more], blksel[:, more], sel3[:, 2], ALU.add))
            link(V.tensor_scalar(blkoff[:, more], sel3[:, 0], -float(SLOTS), None, ALU.mult))
            link(V.scalar_tensor_tensor(out=blkoff[:, more], in0=sel3[:, 1], scalar=-float(2 * SLOTS),
                                        in1=blkoff[:, more], op0=ALU.mult, op1=ALU.add))
            V.scalar_tensor_tensor(out=blkoff[:, more], in0=sel3[:, 2], scalar=-float(3 * SLOTS),
                                   in1=blkoff[:, more], op0=ALU.mult, op1=ALU.add).then_inc(r_sel, 1)
            filled_of(dve, "meta")
            link(V.tensor_copy(metas[:, 1:17], bank("meta")[0:1, 0:16]))
            link(V.tensor_reduce(metas[:, 0:1], bank("meta")[0:1, 16:16 + MORE], AX.X, ALU.add))
            link(V.tensor_scalar(metas[:, 0:1], metas[:, 0:1], float(NE), None, ALU.add))
            drain("meta", V.tensor_copy(cnt_i[:, 0:17], metas[:, 0:17]))
            filled_of(dve, "blk")
            V.tensor_copy(pos_b, bank("blk")[:, 0:2 * BCOL].rearrange("p (t b) -> p t b", t=TT))
            drain("blk", V.tensor_copy(gate_b, bank("blk")[:, 2 * BCOL:4 * BCOL].rearrange("p (t b) -> p t b", t=TT)))
            drained_of(dve, "blk")
            V.memset(scat, 0.0).then_inc(scat_ready, 1)
            V.memset(y_slot, 0.0).then_inc(yslot_ready, 1)

            def find_slots(i):
                for t in range(TT):
                    last = V.tensor_scalar(place[:, t], iota_s[:, 0:SLOTS], pos_b[:, t, bass.ds(i, 1)], None, ALU.is_equal)
                last.then_inc(place_ready, 1)

            find_slots(0)
            nblk = dve.value_load(cnt_i[0:1, 0:1], min_val=NE, max_val=NBLK)
            with dve.Fori(0, nblk) as i:
                dve.wait_ge(yslot_ready, i + 1)
                V.tensor_copy(cur, blksel[:, bass.ds(i, 1)].broadcast_to([NE, SLOTS])).then_inc(cur_ready, 1)
                dve.wait_ge(scat_ready, i + 1)
                for t in range(TT):
                    last = V.tensor_scalar(placeg[:, t], iota_s, pos_b[:, t, bass.ds(i, 1)],
                                           gate_b[:, t, bass.ds(i, 1)], ALU.is_equal, ALU.mult)
                last.then_inc(placeg_ready, 1)
                dve.wait_ge(xg_ready, i + 1)
                find_slots(i + 1)
                dve.wait_ge(freed[eslot["gu3"]], i + 1)
                V.tensor_scalar(gact, ps[:, GBK, :], 7.0, None, ALU.min).then_inc(g_limited, 1)
                V.tensor_scalar(uact, ps[:, UBK, :], -7.0, 7.0, ALU.max, ALU.min).then_inc(g_chain, 1)
                dve.wait_ge(g_limited, i + 1)
                dve.wait_ge(g_chain, i * 2 + 1)
                V.scalar_tensor_tensor(out=uact, in0=uact, scalar=1.0, in1=gact, op0=ALU.add, op1=ALU.mult)\
                    .then_inc(g_chain, 1)
                dve.wait_ge(g_chain, i * 2 + 2)
                dve.wait_ge(sig_done, i + 1)
                V.tensor_tensor(hact, uact, sig, ALU.mult).then_inc(h_ready, 1)
                dve.wait_ge(ht_done, i + 1)
                V.tensor_copy(hactT.rearrange("p c n s -> p (c n s)"), ps[:, ZBK, :]).then_inc(hT_ready, 1)
            dve.wait_ge(fin_sq, 2)
            dve.wait_ge(gfin_loaded, 16)
            V.tensor_scalar(msq[:, 0:2], ss[:, 0:2], 1.0 / D, EPS, ALU.mult, ALU.add).then_inc(fin_v, 1)
            dve.wait_ge(fin_std, 1)
            V.reciprocal(rstd[:, 0:2], std[:, 0:2]).then_inc(fin_v, 1)
            dve.wait_ge(fin_v, 2)
            for t in range(TT):
                V.scalar_tensor_tensor(out=x_tok[:, t], in0=ps[:, YB + 2 * t:YB + 2 * t + 2, :]
                                       .rearrange("p b n -> p (b n)"), scalar=rstd[:, t:t + 1], in1=gfin,
                                       op0=ALU.mult, op1=ALU.mult).then_inc(out_ready, 1)


_INS = ["x", "mem", "g_mix", "w_in", "pe_cmp_k", "pe_cmp_v", "w_phi1_k", "w_phi2_k", "w_phi1_v", "w_phi2_v",
        "w_conv", "b_conv", "w_q_m", "w_k_m", "w_v_m", "b_i", "b_f", "mh_gain", "skip_m", "w_up_a", "w_up_b",
        "w_o_mix", "g_x", "g_mem", "w_q_x", "w_k_x", "w_v_x", "w_o_x", "g_ffn", "w_router", "b_router",
        "w_gu", "b_gu", "w_down", "b_down", "g_final"]


def kernel(**inputs):
    import numpy as _np
    import concourse.bacc as _bacc
    from concourse import mybir as _mybir
    from concourse.bass_utils import run_bass_kernel_spmd as _run

    nc = _bacc.Bacc("TRN2", target_bir_lowering=False, num_devices=1)
    arrays, args = {}, {}
    for name in _INS:
        a = _np.ascontiguousarray(inputs[name])
        arrays[f"in_{name}_dram"] = a
        args[name] = nc.dram_tensor(f"in_{name}_dram", a.shape, _mybir.dt.from_np(a.dtype), kind="ExternalInput").ap()
    out = nc.dram_tensor("out_0_dram", (1, T, D), F32, kind="ExternalOutput").ap()
    program(nc, args, out)
    r = _run(nc, [arrays], core_ids=[0])
    return r.results[0]["out_0_dram"]
```

```python
from contextlib import ExitStack

import concourse.bass as bass
from concourse import mybir

F32 = mybir.dt.float32
I32 = mybir.dt.int32
ALU = mybir.AluOpType
ACT = mybir.ActivationFunctionType
AX = mybir.AxisListType

P = 128
T = 256
TT = T // P
D = 1024
C = D // P
EPS = 1e-5
NEG = -1e30

HA, DA = 8, 64
PAIRS = HA // 2
CMP_BLOCK, CMP_STRIDE = 32, 16
NCMP = T // CMP_STRIDE - 1
CW = 16
HM, DM = 4, 128
HX = 4
NE, TOPK = 32, 4
SLOTS = 64
MORE = T // SLOTS - 1
NBLK = NE + T * TOPK // SLOTS - 1
BCOL = 48
assert NBLK < BCOL

Q0, KC0, VC0, KS0, VS0, KW0, VW0, GN0 = 0, 512, 640, 768, 896, 1024, 1152, 1280
XM0 = GN0 + 3 * HA
OP0 = XM0 + 512
IF0 = OP0 + 512
GA0 = IF0 + 2 * HM
GB0 = GA0 + D
GW = XM0 - KW0
GCOL = GW + 2 * HM

R_MIX, R_X, R_MEM, R_FFN, R_BC, R_WC, R_GAIN, R_SKIP, R_PEK, R_PEV = 0, 8, 16, 24, 32, 36, 52, 56, 64, 96

SLOT_N = 6
SLOT_W = 4096

PIECES = ["q", "kcvs", "kwg", "xm", "phik", "phiv", "op", "ga0", "ga1", "gb0", "gb1",
          "kx0", "kx1", "vx0", "vx1", "ua", "ub", "om0", "om1", "qx0", "qx1", "ox0", "ox1"]
LAST_USE = {"q": "q1", "kcvs": "ksvs", "kwg": "if", "xm": "xm1", "phik": "cmpB", "phiv": "cmpB", "op": "op1",
            "ga0": "ga1", "ga1": "ga3", "gb0": "gb1", "gb1": "gb3", "kx0": "kx1", "kx1": "kx3", "vx0": "vx1",
            "vx1": "vx3", "ua": "ub3", "ub": "ub3", "om0": "om0_1", "om1": "om1_1", "qx0": "qx1", "qx1": "qx3",
            "ox0": "ro0_1", "ox1": "ro1_1"}
DMAS = {"kwg": 2, "phik": 2, "phiv": 2}
EXPERT_PIECES = ["gu0", "gu1", "gu2", "gu3", "dn0", "dn1"]
HEADS = 3

FILL = [("ga", n) for n in range(4)] + [("gb", n) for n in range(4)] + \
       [("kx", n) for n in range(4)] + [("vx", n) for n in range(4)]


def filler_names(step):
    return [f"{k}{n}" for k, n in FILL[2 * step:2 * step + 2]]


def group_order():
    g = ["gmix", "tm0", "tm1", "tm2", "tm3", "q0", "q1", "vec", "kcvc", "ksvs", "kwvw", "gn", "if", "xm0", "xm1",
         "cmpA", "cmpB", "te0", "te1", "te2", "te3", "op0", "cmpT", "op1", "cmp2", "csA", "csB", "mt"]
    for h in range(HA + 1):
        if h >= 1:
            g += [f"ta{h - 1}", f"tb{h - 1}"]
        if h < HA:
            g += [f"sc{h}_0", f"sc{h}_1"] + filler_names(h)[:1]
        if h == 1:
            g += ["mv0", "mv1", "mq0", "mq1", "mq2", "mq3"]
        if 3 <= h <= 6:
            g += [f"mn{h - 3}"]
        if 2 <= h <= 5:
            g += [f"mb{h - 2}", f"ms{h - 2}"]
        if h == HA:
            g += ["ty0", "ty1"] + filler_names(HA - 1)[1:]
        if h >= 2 and h % 2 == 0:
            g += [f"pv{h // 2 - 1}"]
        if h < HA - 1:
            g += filler_names(h)[1:]
    for n in range(4):
        g += [f"ua{n}", f"ub{n}"]
    g += ["om0_0", "om0_1", "om1_0", "tx0", "tx1", "om1_1", "tx2", "tx3"]
    g += ["qx0", "qx1", "sx0", "qx2", "sx1", "qx3", "sx2", "pt0", "sx3"]
    for h in range(1, HX):
        g += [f"pt{h}", f"ox{h - 1}"]
    g += [f"ox{HX - 1}"]
    g += ["ro0_0", "ro0_1", "ro1_0", "tf0", "tf1", "ro1_1", "tf2", "tf3"]
    return g


BANKS = 8
ROUTING = [("rt", 4), ("slot", 5), ("pos", 7), ("cnt", 6), ("rank", 7), ("meta", 6), ("blk", 7)]


def placed_groups():
    at, uses = {}, [0] * BANKS
    for name, b in [(name, i % BANKS) for i, name in enumerate(group_order())] + ROUTING:
        at[name] = (b, uses[b])
        uses[b] += 1
    return at


AT = placed_groups()

YB = 0
GBK, UBK, XBK, ZBK = 4, 5, 6, 7


def program(nc, A, out):
    ctx = ExitStack()
    with ctx:
        def sb(name, shape, dt=F32):
            return ctx.enter_context(nc.sbuf_tensor(name, shape, dt))

        def sem(name):
            return ctx.enter_context(nc.semaphore(name))

        ps = ctx.enter_context(nc.psum_tensor("ps", [P, BANKS, 512], F32))

        ring = sb("ring", [P, SLOT_N, SLOT_W])
        r_x = sb("r_x", [P, TT * D])
        r_mem = sb("r_mem", [P, TT * D])
        r_xs = sb("r_xs", [P, TT * D])
        r_hT = sb("r_hT", [P, C * T])
        r_memT = sb("r_memT", [P, C * T])
        r_kx = sb("r_kx", [P, C * T])
        r_ga = sb("r_ga", [P, C * T])
        r_gb = sb("r_gb", [P, C * T])
        r_q = sb("r_q", [P, PAIRS * T])
        r_so = sb("r_so", [P, TT * 512])
        r_xmc = sb("r_xmc", [P, 2 * HM * T])
        r_xm = r_xmc[:, 0:HM * T]
        r_xc = r_xmc[:, HM * T:2 * HM * T]
        r_tp = sb("r_tp", [P, 2 * HM * T])
        r_tmp = r_tp[:, 0:HM * T]
        r_p = r_tp[:, HM * T:2 * HM * T]
        r_dm = sb("r_dm", [P, 2 * 2 * T])
        r_at = sb("r_at", [P, 8 * T])
        kskw = r_at[:, 0:4 * T].rearrange("p (b g t) -> p b g t", b=2, g=2)
        vsvw = r_at[:, 4 * T:6 * T].rearrange("p (b t e) -> p b t e", b=2, t=TT)
        kcvc = r_at[:, 6 * T:8 * T].rearrange("p (b t) -> p b t", b=2)
        mv = sb("mv", [P, TT, HM, DM + 4])
        vrow = sb("vrow", [P, P])
        vT = sb("vT", [P, P])
        w2 = sb("w2", [P, 2, DA])
        ident = sb("ident", [P, P])
        ones = sb("ones", [P, T])
        causal = sb("causal", [P, T])
        upper = sb("upper", [P, P])
        sm = sb("sm", [P, 512])
        cnt_i = sb("cnt_i", [1, 32], I32)

        small_at = [0]

        def small(n):
            small_at[0] += n
            assert small_at[0] <= 512
            return sm[:, small_at[0] - n:small_at[0]]

        ss, msq, std, rstd = small(8), small(8), small(8), small(8)
        rmaskc = small(2 * CW).rearrange("p (t j) -> p t j", t=TT)
        mmaskc = small(2 * CW).rearrange("p (t j) -> p t j", t=TT)
        gates = small(TT * 3 * HA).rearrange("p (t h b) -> p t h b", t=TT, b=3)
        kcT = small(2 * CW).rearrange("p (g j) -> p g j", g=2)
        bif = small(2)
        cmcol = small(16).rearrange("p (k t h) -> p k t h", k=2, t=TT)
        emcol = small(8).rearrange("p (t h) -> p t h", t=TT)
        nmax = small(4)
        rsum = small(4)
        rinv = small(4)
        fac = small(4)
        cst = small(16)
        den = small(4)
        hsum = small(8)
        hst = small(8)
        brow = small(NE)
        cst2 = small(16)
        lnm = small(8)
        warm = small(1)
        nmaxx, rsumx, rinvx, rs16 = small(8), small(8), small(8), small(2)
        iota_p = small(2)

        x_tok = r_x[:].rearrange("p (t d) -> p t d", t=TT)
        pT = r_x[:].rearrange("p (b k n) -> p b k n", b=2, k=2)
        mem_tok = r_mem[:].rearrange("p (t d) -> p t d", t=TT)
        vx = mem_tok
        xs = r_xs[:].rearrange("p (t d) -> p t d", t=TT)
        mqk = r_xs[:].rearrange("p (h k t) -> p h k t", h=HM, k=2)
        hT = r_hT[:].rearrange("p (c t) -> p c t", c=C)
        memT = r_memT[:].rearrange("p (c t) -> p c t", c=C)
        oxT = memT
        kx = r_kx[:].rearrange("p (c t) -> p c t", c=C)
        wm = r_kx[:, 0:3 * HM * DM].rearrange("p (k h e) -> p k h e", k=3, h=HM)
        sga = r_ga[:].rearrange("p (c t) -> p c t", c=C)
        sgb = r_gb[:].rearrange("p (c t) -> p c t", c=C)
        rows = r_gb[0:HM, :].rearrange("p (k t) -> p k t", k=8)
        qx = sgb
        qT = r_q[:].rearrange("p (c t) -> p c t", c=PAIRS)
        yaT = qT
        pr = r_p.rearrange("p (t b k) -> p t b k", t=2, b=2)
        pcmp = sb("pcmp", [P, TT, HA, CW])
        vc = kcvc[:, 0, 0:P].rearrange("p (g d) -> p g d", g=2)
        mrow = kcvc[0:HM, 1]
        gmix = kcvc[0:C, 0, 0:P]
        so = r_so[:].rearrange("p (t d) -> p t d", t=TT)
        xm = r_xm.rearrange("p (h t) -> p h t", h=HM)
        ybT = xm
        xc = r_xc.rearrange("p (h t) -> p h t", h=HM)
        conv = r_tmp.rearrange("p (h t) -> p h t", h=HM)
        hs = r_tmp.rearrange("p (t h e) -> p t h e", t=TT, h=HM)
        blocks = r_dm[:, 0:2 * CMP_BLOCK * NCMP].rearrange("p (k s j) -> p k s j", k=2, s=CMP_BLOCK)
        dm = r_dm[:].rearrange("p (b s t) -> p b s t", b=2, s=2)
        px = [r_p.rearrange("p (t m) -> p t m", t=4), r_tmp.rearrange("p (t m) -> p t m", t=4)]
        wr = r_q[:, 512:512 + C * NE].rearrange("p (c e) -> p c e", c=C)
        hid_rows, hidT, hid2 = r_p[:, 0:P], r_p[:, P:2 * P], r_p[:, 2 * P:3 * P]
        gelT = r_p[:, 3 * P:4 * P].rearrange("p (g k j) -> p g k j", g=2, k=2)
        pxT = r_dm[:].rearrange("p (b m t) -> p b m t", b=2, m=2)
        junk = {"mix": r_hT, "mem": r_memT, "x": r_xs, "ffn": r_xs}

        lg = r_gb[:, 0:64].rearrange("p (t e) -> p t e", t=TT)
        lgm = r_gb[:, 64:128].rearrange("p (t e) -> p t e", t=TT)
        top = r_gb[:, 128:144].rearrange("p (t e) -> p t e", t=TT)
        mask = r_gb[:, 144:208].rearrange("p (t e) -> p t e", t=TT)
        gexp = r_gb[:, 208:272].rearrange("p (t e) -> p t e", t=TT)
        gate = r_gb[:, 272:336].rearrange("p (t e) -> p t e", t=TT)
        gsum = r_gb[:, 336:340]
        negtop = r_gb[:, 340:342]
        posT = r_gb[0:NE, 352:608]
        gateT = r_gb[0:NE, 608:864]
        cnt = r_gb[0:NE, 864:865]
        ovf = r_gb[0:NE, 868:868 + MORE]
        ovs = r_gb[0:NE, 872:872 + MORE]
        sel3 = r_gb[0:NE, 880:880 + MORE * 16].rearrange("p (c b) -> p c b", c=MORE)
        rank = r_gb[0:NE, 928:928 + MORE]
        blksel = r_gb[0:NE, 944:944 + BCOL]
        blkoff = r_gb[0:NE, 992:992 + BCOL]
        idx16 = r_gb[:, 1040:1056]
        strict = r_gb[:, 1056:1056 + T]
        mT = r_gb[0:NE, 1312:1568]
        metas = r_gb[0:1, 1568:1568 + 32]
        eidx = r_gb[:, 1600:1602]
        lge = r_gb[:, 1608:1672].rearrange("p (t e) -> p t e", t=TT)
        pos_b = r_q[:, 0:TT * BCOL].rearrange("p (t b) -> p t b", t=TT)
        gate_b = r_q[:, TT * BCOL:2 * TT * BCOL].rearrange("p (t b) -> p t b", t=TT)
        iota_s = r_q[:, 256:256 + 2 * SLOTS]
        cur = r_q[0:NE, 400:400 + SLOTS]
        bgu_rows = r_ga[0:NE, :]
        bdn_rows = r_so[0:NE, :]
        gfin = r_xmc[:, 0:D]
        odd_slot = [[r_at[:], r_mem[:]], [r_tp[:], r_hT[:]], [r_xmc[:], r_xs[:]]]
        gain_ffn = vT[:, R_FFN:R_FFN + C].unsqueeze(2).broadcast_to([P, C, SLOTS])
        xg = r_memT[:, 0:512].rearrange("p (c s) -> p c s", c=C)
        gact, uact, sig, hact = (r_memT[:, 512:1024], r_memT[:, 1024:1536], r_memT[:, 1536:2048], r_kx[:, 0:512])
        hactT = r_kx[:, 512:1024].rearrange("p (c n s) -> p c n s", c=4, n=2)
        y_slot = r_kx[:, 1024:1536]
        place = r_dm[:, 0:128].rearrange("p (t s) -> p t s", t=TT)
        placeg = r_dm[:, 128:384].rearrange("p (t s) -> p t s", t=TT)
        scat = r_dm[:, 384:640]

        loaded = [sem(f"loaded{i}") for i in range(SLOT_N)]
        freed = [sem(f"freed{i}") for i in range(SLOT_N)]
        filled = [sem(f"filled{i}") for i in range(BANKS)]
        drained = [sem(f"drained{i}") for i in range(BANKS)]
        vrow_clear, vec_loaded, gmix_loaded = sem("vrow_clear"), sem("vec_loaded"), sem("gmix_loaded")
        x_loaded, mem_loaded = sem("x_loaded"), sem("mem_loaded")
        small_loaded, wm_loaded, x_again, wr_loaded = sem("small_loaded"), sem("wm_loaded"), sem("x_again"), sem("wr_loaded")
        late_loaded, gfin_loaded = sem("late_loaded"), sem("gfin_loaded")
        odd_loaded = [sem(f"odd_loaded{j}") for j in range(HEADS)]
        odd_freed = [sem(f"odd_freed{j}") for j in range(HEADS)]
        consts, p_chain = sem("consts"), sem("p_chain")
        v_chain, a_chain = sem("v_chain"), sem("a_chain")
        sq_done, msq_ready = sem("sq_done"), sem("msq_ready")
        std_ready, xs_ready = sem("std_ready"), sem("xs_ready")
        gate_e, blk_ready, gelu_in = sem("gate_e"), sem("blk_ready"), sem("gelu_in")
        gelu_e, gelu_done = sem("gelu_e"), sem("gelu_done")
        fabs_ready, softp_ready = sem("fabs_ready"), sem("softp_ready")
        rows_ready, em_done = sem("rows_ready"), sem("em_done")
        conv_ready, silu_e, xc_ready = sem("conv_ready"), sem("silu_e"), sem("xc_ready")
        cm_in, cm_e, cm_done = sem("cm_in"), sem("cm_e"), sem("cm_done")
        s_max, s_exp = sem("s_max"), sem("s_exp")
        s_fac, s_prob = sem("s_fac"), sem("s_prob")
        dm_e, var_ready, lstd_ready = sem("dm_e"), sem("var_ready"), sem("lstd_ready")
        hn_ready, merged_ready = sem("hn_ready"), sem("merged_ready")
        cx_max, cx_inv, cx_prob = sem("cx_max"), sem("cx_inv"), sem("cx_prob")
        r_top, r_exp, r_gate = sem("r_top"), sem("r_exp"), sem("r_gate")
        r_ovf, r_sel = sem("r_ovf"), sem("r_sel")
        place_ready, placeg_ready = sem("place_ready"), sem("placeg_ready")
        gathered, xg_ready = sem("gathered"), sem("xg_ready")
        g_limited, sig_done, h_ready = sem("g_limited"), sem("sig_done"), sem("h_ready")
        cur_ready, ht_done, hT_ready, g_chain = sem("cur_ready"), sem("ht_done"), sem("hT_ready"), sem("g_chain")
        pt_done, scat_ready = sem("pt_done"), sem("scat_ready")
        yslot_ready, scattered = sem("yslot_ready"), sem("scattered")
        fin_sq, fin_v, fin_std = sem("fin_sq"), sem("fin_v"), sem("fin_std")
        out_ready, out_sem = sem("out_ready"), sem("out_sem")

        slot_of, need = {}, {}
        dmas = [0] * SLOT_N
        for n, name in enumerate(PIECES):
            s = n % SLOT_N
            dmas[s] += DMAS.get(name, 1)
            slot_of[name], need[name] = s, 16 * dmas[s]
        eslot = {name: (len(PIECES) + j) % SLOT_N for j, name in enumerate(EXPERT_PIECES)}

        def bank(name):
            return ps[:, AT[name][0], :]

        def drained_of(eng, name):
            b, turn = AT[name]
            eng.wait_ge(drained[b], turn + 1)

        def filled_of(eng, name):
            b, turn = AT[name]
            eng.wait_ge(filled[b], turn + 1)

        def is_block(i, n):
            return isinstance(i, int) and i == n

        def wslot(name, rows_, width):
            return ring[:, slot_of[name], 0:rows_ * width].rearrange("p (c n) -> p c n", c=rows_)

        w_in = A["w_in"][0].rearrange("(c p) n -> p c n", p=P)

        def cols(w, a, b):
            return w[0].rearrange("(c p) n -> p c n", p=P)[:, :, a:b]

        gu_dram = A["w_gu"].rearrange("l e (j k p) n -> (l e) j p k n", k=2, p=P)
        dn_dram = A["w_down"].rearrange("l e (j k p) n -> (l e) j p k n", k=4, p=P)

        more = slice(NE, NE + 16)

        block = ctx.enter_context(nc.Block())

        @block.sync
        def _(sp):
            sp.dma_start(gmix, A["g_mix"][0].rearrange("(c p) -> c p", p=P)).then_inc(gmix_loaded, 16)
            x_dram = A["x"][0].rearrange("(t p) d -> p t d", p=P)
            for t in range(TT):
                sp.dma_start(x_tok[:, t], x_dram[:, t]).then_inc(x_loaded, 16)

            def piece(name):
                s = slot_of[name]
                n = PIECES.index(name)
                if n >= SLOT_N:
                    filled_of(sp, LAST_USE[PIECES[n - SLOT_N]])
                w8 = wslot(name, C, 512)
                if name == "q":
                    pairs = [(w8, w_in[:, :, Q0:Q0 + 512])]
                elif name == "kcvs":
                    pairs = [(w8, w_in[:, :, KC0:KC0 + 512])]
                elif name == "kwg":
                    w = wslot(name, C, GCOL)
                    pairs = [(w[:, :, 0:GW], w_in[:, :, KW0:XM0]), (w[:, :, GW:GCOL], w_in[:, :, IF0:GA0])]
                elif name == "xm":
                    pairs = [(w8, w_in[:, :, XM0:XM0 + 512])]
                elif name in ("phik", "phiv"):
                    w = wslot(name, CMP_BLOCK, P)
                    src = A["w_phi1_" + name[-1]][0].rearrange("(s d) n -> d s n", d=DA)
                    pairs = [(w[g * DA:(g + 1) * DA], src) for g in range(2)]
                elif name == "op":
                    pairs = [(w8, w_in[:, :, OP0:OP0 + 512])]
                elif name[:2] in ("ga", "gb"):
                    a = (GA0 if name[1] == "a" else GB0) + 512 * int(name[2])
                    pairs = [(w8, w_in[:, :, a:a + 512])]
                elif name == "ua":
                    pairs = [(wslot(name, PAIRS, D), A["w_up_a"][0].rearrange("(c p) n -> p c n", p=P))]
                elif name == "ub":
                    pairs = [(wslot(name, HM, D), A["w_up_b"][0].rearrange("(c p) n -> p c n", p=P))]
                else:
                    src = {"kx": "w_k_x", "vx": "w_v_x", "om": "w_o_mix", "qx": "w_q_x", "ox": "w_o_x"}[name[:2]]
                    a = 512 * int(name[2])
                    pairs = [(w8, cols(A[src], a, a + 512))]
                for dst, src in pairs:
                    sp.dma_start(dst, src).then_inc(loaded[s], 16)

            piece("q")
            m_dram = A["mem"][0].rearrange("(t p) d -> p t d", p=P)
            for t in range(TT):
                sp.dma_start(mem_tok[:, t], m_dram[:, t]).then_inc(mem_loaded, 16)
            sp.wait_ge(vrow_clear, 1)
            for name, r, n in (("g_x", R_X, C), ("g_mem", R_MEM, C), ("g_ffn", R_FFN, C),
                               ("b_conv", R_BC, HM), ("mh_gain", R_GAIN, HM), ("skip_m", R_SKIP, HM)):
                sp.dma_start(vrow[r:r + n, :], A[name][0].rearrange("(c p) -> c p", p=P)).then_inc(vec_loaded, 16)
            sp.dma_start(vrow[R_WC:R_WC + 4 * HM, :], A["w_conv"][0].rearrange("r (c p) -> (r c) p", p=P))\
                .then_inc(vec_loaded, 16)
            for r, name in ((R_PEK, "pe_cmp_k"), (R_PEV, "pe_cmp_v")):
                for g in range(2):
                    sp.dma_start(vrow[r:r + CMP_BLOCK, g * DA:(g + 1) * DA], A[name][0]).then_inc(vec_loaded, 16)
            for name in ("kcvs", "kwg", "xm"):
                piece(name)
            sp.wait_ge(consts, 1)
            sp.dma_start(bif[0:HM, 0:1], A["b_i"][0].rearrange("(h a) -> h a", a=1)).then_inc(small_loaded, 16)
            sp.dma_start(bif[0:HM, 1:2], A["b_f"][0].rearrange("(h a) -> h a", a=1)).then_inc(small_loaded, 16)
            sp.dma_start(w2[:, 0], A["w_phi2_k"][0]).then_inc(small_loaded, 16)
            sp.dma_start(w2[:, 1], A["w_phi2_v"][0]).then_inc(small_loaded, 16)
            sp.dma_start(brow, A["b_router"].partition_broadcast(P)[:, 0]).then_inc(small_loaded, 16)
            for k, name in enumerate(("w_q_m", "w_k_m", "w_v_m")):
                sp.dma_start(wm[:, k], A[name][0].rearrange("h d e -> d h e")).then_inc(wm_loaded, 16)
            for name in PIECES[4:]:
                piece(name)

            def expert_piece(e, j):
                name = EXPERT_PIECES[j]
                s = eslot[name]
                if j < 4:
                    dst, src = ring[:, s].rearrange("p (k n) -> p k n", k=2), gu_dram[e, j]
                else:
                    dst, src = ring[:, s].rearrange("p (k n) -> p k n", k=4), dn_dram[e, j - 4]
                sp.dma_start(dst, src).then_inc(loaded[s], 16)

            def first_block(part):
                for j in part:
                    filled_of(sp, LAST_USE[PIECES[len(PIECES) + j - SLOT_N]])
                    expert_piece(0, j)

            def odd_half(e, j, k):
                sp.dma_start(odd_slot[j][k], gu_dram[e, j][:, k]).then_inc(odd_loaded[j], 16)

            def odd_heads(p):
                for j in range(HEADS):
                    sp.wait_ge(odd_freed[j], p)
                    for k in range(2):
                        odd_half(p * 2 + 1, j, k)

            def even_heads(p):
                for j in range(HEADS):
                    sp.wait_ge(freed[eslot[EXPERT_PIECES[j]]], p)
                    expert_piece(p * 2, j)

            def others(i):
                for j in range(HEADS, 6):
                    sp.wait_ge(freed[eslot[EXPERT_PIECES[j]]], i)
                    expert_piece(i, j)

            first_block(range(2))
            filled_of(sp, "pv3")
            odd_half(1, 0, 0)
            filled_of(sp, "ub3")
            odd_half(1, 2, 0)
            first_block(range(2, 4))
            filled_of(sp, "ox3")
            odd_half(1, 0, 1)
            odd_half(1, 1, 0)
            first_block(range(4, 6))
            sp.wait_ge(sq_done, 8)
            odd_half(1, 2, 1)
            filled_of(sp, "rt")
            odd_half(1, 1, 1)
            even_heads(1)
            others(1)
            for p in (1, 2):
                odd_heads(p)
                others(p * 2)
                even_heads(p + 1)
                others(p * 2 + 1)
            with sp.Fori(3, NE // 2 - 1) as p:
                others(p * 2)
                odd_heads(p)
                others(p * 2 + 1)
                even_heads(p + 1)
            others(NE - 2)
            odd_heads(NE // 2 - 1)
            others(NE - 1)
            drained_of(sp, "meta")
            nblk = sp.value_load(cnt_i[0:1, 0:1], min_val=NE, max_val=NBLK)
            with sp.If(nblk > NE):
                with sp.Fori(NE, nblk) as i:
                    e = sp.value_load(cnt_i[0:1, bass.ds(i - (NE - 1), 1)], min_val=0, max_val=NE - 1)
                    for j in range(6):
                        sp.wait_ge(freed[eslot[EXPERT_PIECES[j]]], i - NE // 2 if j < HEADS else i)
                        expert_piece(e, j)
            for t in range(TT):
                sp.wait_ge(out_ready, t + 1)
                sp.dma_start(out[0, t * P:(t + 1) * P], x_tok[:, t]).then_inc(out_sem, 16)
            sp.wait_ge(out_sem, 16 * TT)

        @block.gpsimd
        def _(pool):
            count = [0]

            def link(ins):
                count[0] += 1
                ins.then_inc(p_chain, 1)
                pool.wait_ge(p_chain, count[0])

            pool.memset(vrow[:], 0.0).then_inc(vrow_clear, 1)
            pool.memset(hid_rows, 0.0)
            link(pool.memset(ident[:], 0.0))
            pool.memset(ones[:], 1.0)
            pool.memset(sm[:], 0.0)
            pool.memset(cnt_i[:], 0)
            pool.memset(mv[:], 1.0)
            pool.memset(pcmp[:], 0.0)
            pool.memset(causal[:], 0.0)
            link(pool.affine_select(out=ident[:], in_=ident[:], compare_op=ALU.not_equal, fill=1.0, base=0,
                                    pattern=[[-1, P]], channel_multiplier=1))
            pool.affine_select(out=causal[:, P:T], in_=causal[:, P:T], compare_op=ALU.is_ge, fill=NEG, base=0,
                               pattern=[[-1, P]], channel_multiplier=1)
            pool.affine_select(out=upper[:], in_=ones[:, 0:P], compare_op=ALU.is_ge, fill=0.0, base=0,
                               pattern=[[1, P]], channel_multiplier=-1)
            for t in range(TT):
                pool.affine_select(out=rmaskc[:, t], in_=rmaskc[:, t], compare_op=ALU.is_ge, fill=NEG,
                                   base=P * t - (CMP_BLOCK - 1), pattern=[[-CMP_STRIDE, CW]], channel_multiplier=1)
                last = pool.affine_select(out=mmaskc[:, t], in_=ones[:, 0:CW], compare_op=ALU.is_ge, fill=0.0,
                                          base=P * t - (CMP_BLOCK - 1), pattern=[[-CMP_STRIDE, CW]],
                                          channel_multiplier=1)
            last.then_inc(consts, 1)
            filled_of(pool, "pv3")
            pool.dma_start(x_tok, A["x"][0].rearrange("(t p) d -> p t d", p=P)).then_inc(x_again, 16)
            filled_of(pool, "om1_1")
            pool.dma_start(bgu_rows, A["b_gu"][0]).then_inc(late_loaded, 16)
            pool.dma_start(bdn_rows, A["b_down"][0]).then_inc(late_loaded, 16)
            filled_of(pool, "sx3")
            filled_of(pool, "pt1")
            pool.dma_start(wr, A["w_router"][0].rearrange("(c p) e -> p c e", p=P)).then_inc(wr_loaded, 16)
            pool.iota(idx16, pattern=[[1, 16]], base=0, channel_multiplier=0, allow_small_or_imprecise_dtypes=True)
            pool.iota(eidx, pattern=[[0, 2]], base=0, channel_multiplier=1, allow_small_or_imprecise_dtypes=True)
            pool.iota(iota_s, pattern=[[0, 2], [1, SLOTS]], base=0, channel_multiplier=0, allow_small_or_imprecise_dtypes=True)
            link(pool.memset(blksel, 0.0))
            pool.memset(blkoff, 0.0)
            pool.affine_select(out=blksel[:, 0:NE], in_=blksel[:, 0:NE], compare_op=ALU.not_equal, fill=1.0,
                               base=0, pattern=[[-1, NE]], channel_multiplier=1)
            pool.affine_select(out=strict, in_=ones[:], compare_op=ALU.is_gt, fill=0.0, base=0,
                               pattern=[[1, T]], channel_multiplier=-1).then_inc(consts, 1)
            pool.wait_ge(odd_freed[2], NE // 2)
            pool.dma_start(gfin, A["g_final"].rearrange("(a d) -> a d", a=1).partition_broadcast(P))\
                .then_inc(gfin_loaded, 16)

        @block.scalar
        def _(act):
            count = [0]

            def link(ins):
                count[0] += 1
                ins.then_inc(a_chain, 1)
                act.wait_ge(a_chain, count[0])

            def squares(n, name, src, prefix=None):
                for t in range(TT):
                    if prefix:
                        drained_of(act, f"{prefix}0_{t}")
                        drained_of(act, f"{prefix}1_{t}")
                    nc.scalar.activation(junk[name][:, t * D:(t + 1) * D], src[:, t], ACT.Square,
                                         accum_out=ss[:, 2 * n + t:2 * n + t + 1]).then_inc(sq_done, 1)
                act.wait_ge(msq_ready, n + 1)
                nc.scalar.activation(std[:, 2 * n:2 * n + 2], msq[:, 2 * n:2 * n + 2], ACT.Sqrt).then_inc(std_ready, 1)

            def gained(name, dst, g0, n):
                filled_of(act, name)
                b, _ = AT[name]
                for j in range(2):
                    last = nc.scalar.activation(dst[:, 2 * n + j], bank(name)[:, j * T:(j + 1) * T], ACT.Copy,
                                                scale=vT[:, g0 + 2 * n + j:g0 + 2 * n + j + 1])
                last.then_inc(drained[b], 1)

            def copy(name, dst, src, func=ACT.Copy, **kw):
                filled_of(act, name)
                nc.scalar.activation(dst, src, func, **kw).then_inc(drained[AT[name][0]], 1)

            def square_root_table():
                nc.scalar.activation(warm, warm, ACT.Sqrt)

            act.wait_ge(consts, 1)
            square_root_table()
            act.wait_ge(x_loaded, 32)
            squares(0, "mix", x_tok)
            drained_of(act, "gmix")
            gained("tm0", hT, R_MIX, 0)
            gained("tm2", hT, R_MIX, 2)
            act.wait_ge(mem_loaded, 32)
            squares(1, "mem", mem_tok)
            copy("q0", qT[:, 0:2], bank("q0").rearrange("p (c t) -> p c t", c=2))
            copy("q1", qT[:, 2:4], bank("q1").rearrange("p (c t) -> p c t", c=2))
            copy("kcvc", kcvc, bank("kcvc").rearrange("p (c t) -> p c t", c=2))
            filled_of(act, "kwvw")
            for half in range(2):
                for g in range(2):
                    nc.scalar.activation(kskw[half * DA:(half + 1) * DA, 1, g], bank("kwvw")[g * DA:(g + 1) * DA, 0:T],
                                         ACT.Copy)
            nc.scalar.activation(vsvw[:, 1], bank("kwvw")[:, T:2 * T].rearrange("p (t e) -> p t e", t=TT), ACT.Copy)\
                .then_inc(drained[AT["kwvw"][0]], 1)
            drained_of(act, "gn")
            nc.scalar.activation(gates[:].rearrange("p t h b -> p (t h b)"),
                                 gates[:].rearrange("p t h b -> p (t h b)"), ACT.Tanh, scale=0.5).then_inc(gate_e, 1)
            copy("xm0", xm[:, 0:2], bank("xm0").rearrange("p (c t) -> p c t", c=2))
            act.wait_ge(fabs_ready, 1)
            link(nc.scalar.activation(rows[:, 3], rows[:, 2], ACT.Exp, scale=-1.0))
            nc.scalar.activation(rows[:, 3], rows[:, 3], ACT.Ln, bias=1.0).then_inc(softp_ready, 1)
            act.wait_ge(conv_ready, 1)
            nc.scalar.activation(r_xc, r_tmp, ACT.Tanh, scale=0.5).then_inc(silu_e, 1)
            drained_of(act, "vec")
            gained("te0", memT, R_MEM, 0)
            gained("te2", memT, R_MEM, 2)
            copy("op0", so[:, 0], bank("op0"), ACT.Tanh, scale=0.5)
            act.wait_ge(gelu_in, 1)
            nc.scalar.activation(hid2, hid2, ACT.Tanh, scale=0.7978845608028654).then_inc(gelu_e, 1)
            copy("op1", so[:, 1], bank("op1"), ACT.Tanh, scale=0.5)
            act.wait_ge(cm_in, 1)
            nc.scalar.activation(pcmp[:], pcmp[:], ACT.Exp).then_inc(cm_e, 1)
            drained_of(act, "mt")
            nc.scalar.activation(emcol, cmcol[:, 1], ACT.Exp, scale=-1.0).then_inc(em_done, 1)

            def filler(name):
                kind, n = name[:2], int(name[2])
                if kind == "ga":
                    copy(name, sga[:, 2 * n:2 * n + 2], bank(name).rearrange("p (c t) -> p c t", c=2),
                         ACT.Tanh, scale=0.5)
                elif kind == "gb":
                    copy(name, sgb[:, 2 * n:2 * n + 2], bank(name).rearrange("p (c t) -> p c t", c=2),
                         ACT.Tanh, scale=0.5)
                elif kind == "kx":
                    copy(name, kx[:, 2 * n:2 * n + 2], bank(name).rearrange("p (c t) -> p c t", c=2))

            for h in range(HA + 1):
                if h >= 1:
                    copy(f"ta{h - 1}", pT[:, (h - 1) % 2, 0], bank(f"ta{h - 1}"))
                if h < HA:
                    for t in range(TT):
                        act.wait_ge(s_max, 2 * h + t + 1)
                        for b in range(2):
                            last = nc.scalar.activation(pr[:, t, b, 0:P * (t + 1)], pr[:, t, b, 0:P * (t + 1)],
                                                        ACT.Exp, bias=nmax[:, 2 * t + b:2 * t + b + 1],
                                                        accum_out=rsum[:, 2 * t + b:2 * t + b + 1])
                        last.then_inc(s_exp, 1)
                    for name in filler_names(h)[:1]:
                        filler(name)
                    for t in range(TT):
                        act.wait_ge(s_fac, 2 * h + t + 1)
                        for b in range(2):
                            last = nc.scalar.activation(pr[:, t, b, 0:P * (t + 1)], pr[:, t, b, 0:P * (t + 1)],
                                                        ACT.Copy, scale=fac[:, 2 * t + b:2 * t + b + 1])
                        last.then_inc(s_prob, 1)
                if h == 1:
                    for m in range(HM):
                        filled_of(act, f"mq{m}")
                        nc.scalar.activation(mqk[:, m, 0], bank(f"mq{m}")[:, 0:T], ACT.Copy)
                        nc.scalar.activation(mqk[:, m, 1], bank(f"mq{m}")[:, T:2 * T], ACT.Copy,
                                             scale=float(DM) ** -0.5).then_inc(drained[AT[f"mq{m}"][0]], 1)
                if 2 <= h <= 5:
                    m = h - 2
                    drained_of(act, f"mb{m}")
                    nc.scalar.activation(r_dm[:, (m % 2) * 512:(m % 2) * 512 + 384],
                                         r_dm[:, (m % 2) * 512:(m % 2) * 512 + 384], ACT.Exp,
                                         scale=-1.0).then_inc(dm_e, 1)
                if h == 7:
                    act.wait_ge(var_ready, 1)
                    nc.scalar.activation(hst, lnm, ACT.Sqrt).then_inc(lstd_ready, 1)
                if h >= 2 and h % 2 == 0:
                    c = h // 2 - 1
                    copy(f"pv{c}", yaT[:, c], bank(f"pv{c}")[:, 0:T])
                if h < HA - 1:
                    for name in filler_names(h)[1:]:
                        filler(name)

            square_root_table()
            squares(2, "x", x_tok, "om")
            copy("qx0", qx[:, 0:2], bank("qx0").rearrange("p (c t) -> p c t", c=2))
            copy("qx1", qx[:, 2:4], bank("qx1").rearrange("p (c t) -> p c t", c=2))

            def cross_exp(h):
                act.wait_ge(cx_max, h + 1)
                for t in range(TT):
                    j = 2 * (h % 2) + t
                    last = nc.scalar.activation(px[h // 2][:, j], bank(f"sx{h}")[:, t * T:(t + 1) * T], ACT.Exp,
                                                bias=nmaxx[:, 2 * h + t:2 * h + t + 1], scale=rs16[:, t:t + 1],
                                                accum_out=rsumx[:, 2 * h + t:2 * h + t + 1])
                last.then_inc(drained[AT[f"sx{h}"][0]], 1)

            def cross_scale(h):
                act.wait_ge(cx_inv, h + 1)
                for t in range(TT):
                    j = 2 * (h % 2) + t
                    last = nc.scalar.activation(px[h // 2][:, j], px[h // 2][:, j], ACT.Copy,
                                                scale=rinvx[:, 2 * h + t:2 * h + t + 1])
                last.then_inc(cx_prob, 1)

            def cross_out(h):
                copy(f"ox{h}", oxT[:, 2 * h:2 * h + 2], bank(f"ox{h}").rearrange("p (c t) -> p c t", c=2))

            cross_exp(0)
            copy("qx2", qx[:, 4:6], bank("qx2").rearrange("p (c t) -> p c t", c=2))
            cross_scale(0)
            cross_exp(1)
            copy("qx3", qx[:, 6:8], bank("qx3").rearrange("p (c t) -> p c t", c=2))
            cross_scale(1)
            cross_exp(2)
            cross_scale(2)
            cross_exp(3)
            cross_scale(3)
            for h in range(HX):
                cross_out(h)
            square_root_table()
            squares(3, "ffn", x_tok, "ro")
            act.wait_ge(r_top, 1)
            for t in range(TT):
                last = nc.scalar.activation(gexp[:, t], lg[:, t], ACT.Exp, bias=negtop[:, t:t + 1])
            last.then_inc(r_exp, 1)
            def block_steps(i):
                act.wait_ge(g_limited, i + 1)
                nc.scalar.activation(sig, gact, ACT.Sigmoid, scale=1.702).then_inc(sig_done, 1)
                act.wait_ge(pt_done, i + 1)
                nc.scalar.activation(scat, ps[:, GBK, 0:T], ACT.Copy).then_inc(scat_ready, 1)
                act.wait_ge(freed[eslot["dn1"]], i + 1)
                nc.scalar.activation(y_slot, ps[:, ZBK, :], ACT.Copy).then_inc(yslot_ready, 1)

            block_steps(0)
            drained_of(act, "meta")
            nblk = act.value_load(cnt_i[0:1, 0:1], min_val=NE, max_val=NBLK)
            with act.Fori(1, nblk) as i:
                block_steps(i)
            square_root_table()
            act.wait_ge(scattered, nblk)
            for t in range(TT):
                nc.scalar.activation(r_hT[:, t * D:(t + 1) * D],
                                     ps[:, YB + 2 * t:YB + 2 * t + 2, :].rearrange("p b n -> p (b n)"), ACT.Square,
                                     accum_out=ss[:, t:t + 1]).then_inc(fin_sq, 1)
            act.wait_ge(fin_v, 1)
            nc.scalar.activation(std[:, 0:2], msq[:, 0:2], ACT.Sqrt).then_inc(fin_std, 1)

        @block.tensor
        def _(pe):
            mm = nc.tensor.matmul

            def begin(name):
                b, turn = AT[name]
                if turn:
                    pe.wait_ge(drained[b], turn)
                return ps[:, b, :]

            def end(name, ins):
                ins.then_inc(filled[AT[name][0]], 1)

            def weights(name):
                pe.wait_ge(loaded[slot_of[name]], need[name])

            def transpose4(name, src, n):
                o = begin(name)
                for j in range(2):
                    for t in range(TT):
                        last = nc.tensor.transpose(o[:, j * T + t * P:j * T + t * P + P],
                                                   src[:, t, (2 * n + j) * P:(2 * n + j + 1) * P], ident[:])
                end(name, last)

            def feature_group(name, ws, src, kk=C, ready=None):
                o = begin(name)
                for j, w in enumerate(ws):
                    for k in range(kk):
                        if ready and j == 0:
                            ready(k)
                        last = mm(o[:, j * T:(j + 1) * T], w(k), src[:, k, :], start=(k == 0), stop=(k == kk - 1))
                return last

            def token_part(o, w, n, src, t, ready=None):
                for k in range(C):
                    if ready:
                        ready(k)
                    last = mm(o, src[:, k, t * P:(t + 1) * P], w[:, k, 0:n], start=(k == 0), stop=(k == C - 1))
                return last

            def stationary(w, j):
                return lambda k: w[:, k, j * P:(j + 1) * P]

            def chunks_of(prefix):
                return lambda k: drained_of(pe, f"{prefix}{k // 2}")

            pe.wait_ge(consts, 1)
            pe.wait_ge(gmix_loaded, 16)
            end("gmix", nc.tensor.transpose(begin("gmix")[:, 0:C], gmix, ident[0:C, 0:C]))
            pe.wait_ge(xs_ready, 2)
            for n in range(4):
                transpose4(f"tm{n}", xs, n)
            weights("q")
            w = wslot("q", C, 512)
            for n in range(2):
                last = feature_group(f"q{n}", [stationary(w, 2 * n), stationary(w, 2 * n + 1)], hT, ready=chunks_of("tm"))
                end(f"q{n}", last)
            pe.wait_ge(vec_loaded, 16 * 11)
            end("vec", nc.tensor.transpose(begin("vec")[:, 0:P], vrow[:], ident[:]))
            weights("kcvs")
            w = wslot("kcvs", C, 512)
            end("kcvc", feature_group("kcvc", [stationary(w, 0), stationary(w, 1)], hT))
            feature_group("ksvs", [stationary(w, 2)], hT)
            for t in range(TT):
                last = token_part(bank("ksvs")[:, T + t * P:T + t * P + P], w[:, :, 384:512], P, hT, t)
            end("ksvs", last)
            weights("kwg")
            w = wslot("kwg", C, GCOL)
            feature_group("kwvw", [stationary(w, 0)], hT)
            for t in range(TT):
                last = token_part(bank("kwvw")[:, T + t * P:T + t * P + P], w[:, :, P:2 * P], P, hT, t)
            end("kwvw", last)
            o = begin("gn")
            for t in range(TT):
                last = token_part(o[:, t * 24:(t + 1) * 24], w[:, :, 2 * P:2 * P + 24], 24, hT, t)
            end("gn", last)
            o = begin("if")
            for k in range(C):
                for j in range(2):
                    last = mm(o[32 * j:32 * j + HM, j * T:(j + 1) * T], w[:, k, GW + HM * j:GW + HM * j + HM], hT[:, k, :],
                              start=(k == 0), stop=(k == C - 1))
            end("if", last)
            weights("xm")
            w = wslot("xm", C, 512)
            for n in range(2):
                end(f"xm{n}", feature_group(f"xm{n}", [stationary(w, 2 * n), stationary(w, 2 * n + 1)], hT))
            weights("phik")
            weights("phiv")
            pe.wait_ge(blk_ready, 2)
            oo = [begin("cmpA"), begin("cmpB")]
            wk, wv = wslot("phik", CMP_BLOCK, P), wslot("phiv", CMP_BLOCK, P)
            for s in range(CMP_BLOCK):
                for g in range(2):
                    for kind in range(2):
                        a = 32 * (2 * g + kind)
                        last = mm(oo[g][a:a + NCMP, 0:P], blocks[g * DA:(g + 1) * DA, kind, s],
                                  (wk, wv)[kind][g * DA:(g + 1) * DA, s], start=(s == 0), stop=(s == CMP_BLOCK - 1))
                        if s == CMP_BLOCK - 1 and kind == 1:
                            end(("cmpA", "cmpB")[g], last)
            pe.wait_ge(xs_ready, 4)
            for n in range(4):
                transpose4(f"te{n}", mem_tok, n)
            weights("op")
            w = wslot("op", C, 512)
            end("op0", token_part(begin("op0"), w, 512, hT, 0))
            drained_of(pe, "cmpA")
            drained_of(pe, "cmpB")
            end("cmpT", nc.tensor.transpose(begin("cmpT")[:, 0:P], hid_rows, ident[:]))
            end("op1", token_part(begin("op1"), w, 512, hT, 1))
            pe.wait_ge(gelu_done, 1)
            pe.wait_ge(small_loaded, 16 * 5)
            o = begin("cmp2")
            for g in range(2):
                for half in range(2):
                    mm(o[half * DA:(half + 1) * DA, g * CW:g * CW + NCMP], w2[:, 0], gelT[:, g, 0, 0:NCMP],
                       start=True, stop=True)
            for g in range(2):
                last = mm(o[0:NCMP, 2 * CW + g * DA:2 * CW + (g + 1) * DA], gelT[:, g, 1, 0:NCMP], w2[:, 1],
                          start=True, stop=True)
            end("cmp2", last)
            drained_of(pe, "cmp2")
            drained_of(pe, "q0")
            drained_of(pe, "q1")
            for half in range(2):
                name = ("csA", "csB")[half]
                o = begin(name)
                for t in range(TT):
                    for c in range(PAIRS):
                        a = (t * PAIRS + c) * CW
                        last = mm(o[:, a:a + NCMP], qT[half * DA:(half + 1) * DA, c, t * P:(t + 1) * P],
                                  kcT[half * DA:(half + 1) * DA, c // 2, 0:NCMP], start=True, stop=True)
                end(name, last)
            pe.wait_ge(rows_ready, 1)
            o = begin("mt")
            for kind in range(2):
                for t in range(TT):
                    last = nc.tensor.transpose(o[:, (kind * TT + t) * HM:(kind * TT + t + 1) * HM],
                                               rows[:, 5 + 2 * kind, t * P:(t + 1) * P], ident[0:HM, 0:HM])
            end("mt", last)

            def filler(name):
                kind, n = name[:2], int(name[2])
                half = f"{kind}{n // 2}"
                weights(half)
                w = wslot(half, C, 512)
                if kind in ("ga", "gb"):
                    src = hT
                else:
                    src = memT
                    for m in range(4):
                        drained_of(pe, f"te{m}")
                if kind == "vx":
                    last = token_part(begin(name), w, 512, memT, n % 2)
                else:
                    j = 2 * (n % 2)
                    last = feature_group(name, [stationary(w, j), stationary(w, j + 1)], src)
                end(name, last)
            for h in range(HA + 1):
                if h >= 1:
                    m = h - 1
                    pe.wait_ge(s_prob, 2 * m + 2)
                    o = begin(f"ta{m}")
                    for b in range(2):
                        for t in range(TT):
                            last = nc.tensor.transpose(o[:, b * T + t * P:b * T + t * P + P], pr[:, t, b, 0:P], ident[:])
                    end(f"ta{m}", last)
                    o = begin(f"tb{m}")
                    for b in range(2):
                        nc.tensor.transpose(o[:, b * P:(b + 1) * P], pr[:, 1, b, P:T], ident[:])
                    pe.wait_ge(cm_done, 1)
                    for t in range(TT):
                        last = nc.tensor.transpose(o[0:NCMP, T + t * P:T + t * P + P], pcmp[:, t, m, 0:NCMP], ident[:])
                    end(f"tb{m}", last)
                if h < HA:
                    c, half, g = h // 2, h % 2, h // PAIRS
                    drained_of(pe, "ksvs")
                    drained_of(pe, "kwvw")
                    for t in range(TT):
                        o = begin(f"sc{h}_{t}")
                        n = P * (t + 1)
                        for b in range(2):
                            last = mm(o[:, b * n:(b + 1) * n], qT[half * DA:(half + 1) * DA, c, t * P:(t + 1) * P],
                                      kskw[half * DA:(half + 1) * DA, b, g, 0:n], start=True, stop=True)
                        end(f"sc{h}_{t}", last)
                    for name in filler_names(h)[:1]:
                        filler(name)
                if h == 1:
                    pe.wait_ge(wm_loaded, 48)
                    pe.wait_ge(xc_ready, 1)
                    drained_of(pe, "xm0")
                    for t in range(TT):
                        o = begin(f"mv{t}")
                        for m in range(HM):
                            last = mm(o[:, m * DM:(m + 1) * DM], xm[:, m, t * P:(t + 1) * P], wm[:, 2, m],
                                      start=True, stop=True)
                        end(f"mv{t}", last)
                    for m in range(HM):
                        o = begin(f"mq{m}")
                        for k in range(2):
                            last = mm(o[:, k * T:(k + 1) * T], wm[:, k, m], xc[:, m], start=True, stop=True)
                        end(f"mq{m}", last)
                if 3 <= h <= 6:
                    m = h - 3
                    drained_of(pe, f"ms{m}")
                    drained_of(pe, "mv0")
                    drained_of(pe, "mv1")
                    o = begin(f"mn{m}")
                    b = m % 2
                    mm(o[:, 0:DM + 1], dm[:, b, 0, 0:P], mv[:, 0, m, 0:DM + 1], start=True, stop=True)
                    mm(o[:, T:T + DM + 1], dm[:, b, 0, P:T], mv[:, 0, m, 0:DM + 1], start=True, stop=False)
                    last = mm(o[:, T:T + DM + 1], dm[:, b, 1, 0:P], mv[:, 1, m, 0:DM + 1], start=False, stop=True)
                    end(f"mn{m}", last)
                if 2 <= h <= 5:
                    m = h - 2
                    drained_of(pe, f"mq{m}")
                    o = begin(f"mb{m}")
                    end(f"mb{m}", mm(o[:, 0:T], ident[0:HM, m:m + 1].broadcast_to([HM, P]), mrow,
                                     start=True, stop=True))
                    o = begin(f"ms{m}")
                    mm(o[:, 0:T], mqk[:, m, 1, 0:P], mqk[:, m, 0], start=True, stop=True)
                    last = mm(o[:, T:T + P], mqk[:, m, 1, P:T], mqk[:, m, 0, P:T], start=True, stop=True)
                    end(f"ms{m}", last)
                if h == HA:
                    pe.wait_ge(hn_ready, 1)
                    for n in range(2):
                        o = begin(f"ty{n}")
                        for j in range(2):
                            for t in range(TT):
                                last = nc.tensor.transpose(o[:, j * T + t * P:j * T + t * P + P], hs[:, t, 2 * n + j],
                                                           ident[:])
                        end(f"ty{n}", last)
                    for name in filler_names(HA - 1)[1:]:
                        filler(name)
                if h >= 2 and h % 2 == 0:
                    c = h // 2 - 1
                    o = begin(f"pv{c}")
                    g = c // 2
                    for m in (2 * c, 2 * c + 1):
                        drained_of(pe, f"ta{m}")
                        drained_of(pe, f"tb{m}")
                    vg = slice(g * DA, (g + 1) * DA)
                    for b in range(2):
                        for half in range(2):
                            mm(o[half * DA:(half + 1) * DA, 0:T], vsvw[:, b, 0, vg], pT[:, half, 0, b * T:(b + 1) * T],
                               start=(b == 0), stop=False)
                    for b in range(2):
                        for half in range(2):
                            mm(o[half * DA:(half + 1) * DA, P:T], vsvw[:, b, 1, vg],
                               pT[:, half, 1, b * P:(b + 1) * P], start=False, stop=False)
                    for half in range(2):
                        last = mm(o[half * DA:(half + 1) * DA, 0:T], vc[0:NCMP, g],
                                  pT[0:NCMP, half, 1, T:2 * T], start=False, stop=True)
                    end(f"pv{c}", last)
                if h < HA - 1:
                    for name in filler_names(h)[1:]:
                        filler(name)
            weights("ua")
            weights("ub")
            drained_of(pe, "pv3")
            for n in range(4):
                w = wslot("ua", PAIRS, D)
                end(f"ua{n}", feature_group(f"ua{n}", [stationary(w, 2 * n), stationary(w, 2 * n + 1)], yaT, PAIRS))
                if n == 0:
                    drained_of(pe, "ty0")
                    drained_of(pe, "ty1")
                w = wslot("ub", HM, D)
                end(f"ub{n}", feature_group(f"ub{n}", [stationary(w, 2 * n), stationary(w, 2 * n + 1)], ybT, HM))

            def token_group(prefix, piece_name, src, n, t, ready):
                weights(f"{piece_name}{n}")
                name = f"{prefix}{n}_{t}"
                end(name, token_part(begin(name), wslot(f"{piece_name}{n}", C, 512), 512, src, t, ready))

            def project_and_turn(prefix, piece_name, src, turned, ready):
                token_group(prefix, piece_name, src, 0, 0, ready)
                token_group(prefix, piece_name, src, 0, 1, ready)
                token_group(prefix, piece_name, src, 1, 0, ready)
                drained_of(pe, f"{prefix}0_0")
                drained_of(pe, f"{prefix}0_1")
                transpose4(f"{turned}0", x_tok, 0)
                transpose4(f"{turned}1", x_tok, 1)
                token_group(prefix, piece_name, src, 1, 1, ready)
                drained_of(pe, f"{prefix}1_0")
                drained_of(pe, f"{prefix}1_1")
                transpose4(f"{turned}2", x_tok, 2)
                transpose4(f"{turned}3", x_tok, 3)

            project_and_turn("om", "om", sga, "tx", lambda k: pe.wait_ge(merged_ready, k // 2 + 1))

            def cross_query(n):
                weights(f"qx{n // 2}")
                w = wslot(f"qx{n // 2}", C, 512)
                j = 2 * (n % 2)
                end(f"qx{n}", feature_group(f"qx{n}", [stationary(w, j), stationary(w, j + 1)], hT,
                                            ready=chunks_of("tx")))

            def cross_scores(h):
                drained_of(pe, f"qx{h}")
                o = begin(f"sx{h}")
                for t in range(TT):
                    for k in range(2):
                        last = mm(o[:, t * T:(t + 1) * T], qx[:, 2 * h + k, t * P:(t + 1) * P], kx[:, 2 * h + k],
                                  start=(k == 0), stop=(k == 1))
                end(f"sx{h}", last)

            def cross_turn(h):
                pe.wait_ge(cx_prob, h + 1)
                o = begin(f"pt{h}")
                for mt in range(2):
                    for t in range(TT):
                        last = nc.tensor.transpose(o[:, mt * T + t * P:mt * T + t * P + P],
                                                   px[h // 2][:, 2 * (h % 2) + t, mt * P:(mt + 1) * P], ident[:])
                end(f"pt{h}", last)

            def cross_values(h):
                drained_of(pe, f"pt{h}")
                o = begin(f"ox{h}")
                for k in range(2):
                    for mt in range(2):
                        last = mm(o[:, k * T:(k + 1) * T], vx[:, mt, (2 * h + k) * P:(2 * h + k + 1) * P],
                                  pxT[:, h % 2, mt], start=(mt == 0), stop=(mt == 1))
                end(f"ox{h}", last)

            for n in range(4):
                drained_of(pe, f"kx{n}")
                drained_of(pe, f"vx{n}")
            cross_query(0)
            cross_query(1)
            cross_scores(0)
            cross_query(2)
            cross_scores(1)
            cross_query(3)
            cross_scores(2)
            cross_turn(0)
            cross_scores(3)
            for h in range(1, HX):
                cross_turn(h)
                cross_values(h - 1)
            cross_values(HX - 1)
            project_and_turn("ro", "ox", oxT, "tf", chunks_of("ox"))
            pe.wait_ge(wr_loaded, 16)
            o = begin("rt")
            for t in range(TT):
                last = token_part(o[:, t * NE:(t + 1) * NE], wr, NE, hT, t, chunks_of("tf"))
            end("rt", last)
            for t in range(TT):
                for n in range(2):
                    b = YB + 2 * t + n
                    drained_of(pe, [name for name in AT if AT[name][0] == b][-1])
                    mm(ps[:, b, :], ident[:], x_tok[:, t, n * 512:(n + 1) * 512], start=True, stop=False,
                       skip_group_check=True)
            pe.wait_ge(r_gate, 1)
            pe.wait_ge(consts, 2)
            o = begin("slot")
            mm(o[:, 0:NE], strict[:, 0:P], mask[:, 0], start=True, stop=True)
            mm(o[:, NE:2 * NE], strict[:, P:T], mask[:, 0], start=True, stop=False)
            end("slot", mm(o[:, NE:2 * NE], strict[:, 0:P], mask[:, 1], start=False, stop=True))

            def gather(i):
                pe.wait_ge(place_ready, i + 1)
                for c in range(C):
                    for t in range(TT):
                        last = mm(ps[:, XBK, c * SLOTS:(c + 1) * SLOTS], x_tok[:, t, c * P:(c + 1) * P],
                                  place[:, t], start=(t == 0), stop=(t == 1))
                last.then_inc(gathered, 1)

            def scatter():
                for t in range(TT):
                    for n in range(2):
                        half = slice(n * SLOTS, (n + 1) * SLOTS)
                        last = mm(ps[:, YB + 2 * t + n, :], scat[half, t * P:(t + 1) * P], y_slot[half, :],
                                  start=False, stop=False, skip_group_check=True)
                last.then_inc(scattered, 1)

            def halves(bk, stationary_, moving, start, stop):
                for n in range(2):
                    last = mm(ps[n * SLOTS:(n + 1) * SLOTS, bk, :], stationary_, moving(n), start=start, stop=stop,
                              skip_group_check=True)
                return last

            def slots_by_expert():
                o = begin("pos")
                mm(o[0:NE, 0:T], mask[:, 0], strict, start=True, stop=False)
                mm(o[0:NE, P:T], mask[:, 1], strict[:, 0:P], start=False, stop=True)
                for t in range(TT):
                    last = mm(o[0:NE, T + t * P:T + t * P + P], mask[:, t], ident[:], start=True, stop=True)
                end("pos", last)

            def gates_and_counts():
                pe.wait_ge(xg_ready, 1)
                o = begin("cnt")
                for t in range(TT):
                    mm(o[0:NE, t * P:(t + 1) * P], gate[:, t], ident[:], start=True, stop=True)
                for t in range(TT):
                    last = mm(o[0:NE, T:T + 1], mask[:, t], ones[:, 0:1], start=(t == 0), stop=(t == 1))
                end("cnt", last)

            def further_ranks():
                pe.wait_ge(r_ovf, 1)
                o = begin("rank")
                mm(o[0:NE, 0:MORE], strict[0:NE, 0:NE], ovf, start=True, stop=False)
                end("rank", mm(o[0:NE, 0:MORE], ones[0:NE, 0:NE], ovs, start=False, stop=True))

            def further_tables():
                pe.wait_ge(r_sel, 1)
                o = begin("meta")
                mm(o[0:1, 0:16], eidx[0:NE, 0:1], blksel[:, more], start=True, stop=True)
                end("meta", mm(o[0:1, 16:16 + MORE], ones[0:NE, 0:1], ovf, start=True, stop=True))
                o = begin("blk")
                for t in range(TT):
                    mm(o[:, t * 16:(t + 1) * 16], posT[:, t * P:(t + 1) * P], blksel[:, more], start=True, stop=False)
                    mm(o[:, t * 16:(t + 1) * 16], ones[0:NE, 0:P], blkoff[:, more], start=False, stop=True)
                    last = mm(o[:, (2 + t) * 16:(3 + t) * 16], gateT[:, t * P:(t + 1) * P], blksel[:, more],
                              start=True, stop=True)
                end("blk", last)

            def down_biases():
                drained_of(pe, "cnt")
                for t in range(TT):
                    for n in range(2):
                        mm(ps[:, YB + 2 * t + n, :], gateT[:, t * P:(t + 1) * P], bdn_rows[:, n * 512:(n + 1) * 512],
                           start=False, stop=False, skip_group_check=True)

            def piece_rows(j, uses, odd):
                if odd and j < HEADS:
                    pe.wait_ge(odd_loaded[j], uses * 32 + 32)
                    return lambda k, a: odd_slot[j][k][:, a:a + 512]
                s = eslot[EXPERT_PIECES[j]]
                pe.wait_ge(loaded[s], uses * 16 + (16 * dmas[s] + 16))
                w = ring[:, s].rearrange("p (k n) -> p k n", k=2 if j < 4 else 4)
                return lambda k, a: w[:, k, a:a + 512]

            def expert_block(i, heads_used, odd=False):
                if not is_block(i, 0):
                    pe.wait_ge(scat_ready, i)
                pe.wait_ge(cur_ready, i + 1)
                for b in range(2):
                    halves(GBK + b, cur, lambda n: bgu_rows[:, b * D + n * 512:b * D + n * 512 + 512], True, False)
                pe.wait_ge(xg_ready, i + 1)
                for j in range(4):
                    w = piece_rows(j, heads_used if j < HEADS else i, odd)
                    for k in range(2):
                        kk = 2 * j + k
                        for b in range(2):
                            last = halves(GBK + b, xg[:, kk], lambda n: w(k, b * D + n * 512), False, kk == 7)
                    last.then_inc(odd_freed[j] if odd and j < HEADS else freed[eslot[EXPERT_PIECES[j]]], 1)
                    if is_block(i, 0) and j == 0:
                        slots_by_expert()
                        gates_and_counts()
                    elif is_block(i, 0) and j == 1:
                        further_ranks()
                    elif is_block(i, 0) and j == 2:
                        further_tables()
                if is_block(i, 0):
                    down_biases()
                    drained_of(pe, "blk")
                    drained_of(pe, "meta")
                else:
                    pe.wait_ge(yslot_ready, i)
                    scatter()
                pe.wait_ge(h_ready, i + 1)
                for c in range(4):
                    last = nc.tensor.transpose(ps[:, ZBK, c * P:(c + 1) * P], hact[:, c * P:(c + 1) * P], ident[:])
                last.then_inc(ht_done, 1)
                pe.wait_ge(placeg_ready, i + 1)
                for t in range(TT):
                    last = nc.tensor.transpose(ps[:, GBK, t * P:(t + 1) * P], placeg[:, t], ident[:])
                last.then_inc(pt_done, 1)
                gather(i + 1)
                pe.wait_ge(hT_ready, i + 1)
                for j in range(2):
                    w = piece_rows(4 + j, i, odd)
                    for k in range(4):
                        last = halves(ZBK, hactT[:, k, j], lambda n: w(k, n * 512), j == 0 and k == 0,
                                      j == 1 and k == 3)
                    last.then_inc(freed[eslot[EXPERT_PIECES[4 + j]]], 1)

            drained_of(pe, "rt")
            drained_of(pe, "slot")
            gather(0)
            pe.wait_ge(late_loaded, 32)
            expert_block(0, 0)
            expert_block(1, 0, odd=True)
            with pe.Fori(1, NE // 2) as p:
                expert_block(p * 2, p)
                expert_block(p * 2 + 1, p, odd=True)
            nblk = pe.value_load(cnt_i[0:1, 0:1], min_val=NE, max_val=NBLK)
            with pe.If(nblk > NE):
                with pe.Fori(NE, nblk) as i:
                    expert_block(i, i - NE // 2)
            pe.wait_ge(yslot_ready, nblk)
            pe.wait_ge(scat_ready, nblk)
            scatter()

        @block.vector
        def _(dve):
            count = [0]
            V = nc.vector

            def link(ins):
                count[0] += 1
                ins.then_inc(v_chain, 1)
                dve.wait_ge(v_chain, count[0])

            def drain(name, ins):
                ins.then_inc(drained[AT[name][0]], 1)

            def norm(n, src, dst):
                dve.wait_ge(sq_done, 2 * n + 2)
                V.tensor_scalar(msq[:, 2 * n:2 * n + 2], ss[:, 2 * n:2 * n + 2], 1.0 / D, EPS, ALU.mult, ALU.add)\
                    .then_inc(msq_ready, 1)
                dve.wait_ge(std_ready, n + 1)
                link(V.reciprocal(rstd[:, 2 * n:2 * n + 2], std[:, 2 * n:2 * n + 2]))
                for t in range(TT if dst is not None else 0):
                    V.tensor_scalar(dst[:, t], src[:, t], rstd[:, 2 * n + t:2 * n + t + 1], None, ALU.mult)\
                        .then_inc(xs_ready, 1)

            def gained(name, dst, g0, n):
                filled_of(dve, name)
                g = vT[:, g0 + 2 * n:g0 + 2 * n + 2].unsqueeze(2).broadcast_to([P, 2, T])
                drain(name, V.tensor_tensor(dst[:, 2 * n:2 * n + 2],
                                            bank(name).rearrange("p (c t) -> p c t", c=2), g, ALU.mult))

            def col(r):
                return vT[:, r:r + 1]

            dve.wait_ge(consts, 1)
            filled_of(dve, "gmix")
            drain("gmix", V.tensor_copy(vT[:, 0:C], bank("gmix")[:, 0:C]))
            norm(0, x_tok, xs)
            drained_of(dve, "gmix")
            gained("tm1", hT, R_MIX, 1)
            gained("tm3", hT, R_MIX, 3)
            dve.wait_ge(mem_loaded, 32)
            norm(1, mem_tok, mem_tok)
            filled_of(dve, "vec")
            drain("vec", V.tensor_copy(vT[:, C:P], bank("vec")[:, C:P]))
            drained_of(dve, "vec")
            filled_of(dve, "ksvs")
            for half in range(2):
                for g in range(2):
                    V.tensor_copy(kskw[half * DA:(half + 1) * DA, 0, g], bank("ksvs")[g * DA:(g + 1) * DA, 0:T])
            drain("ksvs", V.tensor_copy(vsvw[:, 0], bank("ksvs")[:, T:2 * T].rearrange("p (t e) -> p t e", t=TT)))
            drained_of(dve, "kcvc")
            for kind, r in ((0, R_PEK), (1, R_PEV)):
                sub = kcvc[:, kind].rearrange("p (j s) -> p s j", s=CMP_STRIDE)
                for half in range(2):
                    s0 = half * CMP_STRIDE
                    pe_b = vT[:, r + s0:r + s0 + CMP_STRIDE].unsqueeze(2).broadcast_to([P, CMP_STRIDE, NCMP])
                    last = V.tensor_tensor(blocks[:, kind, s0:s0 + CMP_STRIDE], sub[:, :, half:half + NCMP], pe_b,
                                           ALU.add)
                last.then_inc(blk_ready, 1)
            gflat = gates[:].rearrange("p t h b -> p (t h b)")
            filled_of(dve, "gn")
            drain("gn", V.tensor_copy(gflat, bank("gn")[:, 0:2 * 24]))
            filled_of(dve, "if")
            dve.wait_ge(small_loaded, 16 * 5)
            V.tensor_scalar(rows[:, 0], bank("if")[0:HM, 0:T], bif[0:HM, 0:1], None, ALU.add)
            drain("if", V.tensor_copy(rows[:, 1], bank("if")[32:32 + HM, T:2 * T]))
            drained_of(dve, "if")
            link(V.tensor_scalar(rows[:, 1], rows[:, 1], bif[0:HM, 1:2], None, ALU.add))
            V.scalar_tensor_tensor(out=rows[:, 2], in0=rows[:, 1], scalar=-1.0, in1=rows[:, 1], op0=ALU.mult,
                                   op1=ALU.max).then_inc(fabs_ready, 1)
            filled_of(dve, "xm1")
            drain("xm1", V.tensor_copy(xm[:, 2:4], bank("xm1").rearrange("p (c t) -> p c t", c=2)))
            drained_of(dve, "xm0")
            drained_of(dve, "xm1")
            for h in range(HM):
                last = V.tensor_scalar(conv[:, h], xm[:, h], col(R_WC + 3 * HM + h), col(R_BC + h), ALU.mult, ALU.add)
            for r in range(2, -1, -1):
                link(last)
                s = 3 - r
                for h in range(HM):
                    last = V.scalar_tensor_tensor(out=conv[:, h, s:T], in0=xm[:, h, 0:T - s],
                                                  scalar=col(R_WC + r * HM + h), in1=conv[:, h, s:T],
                                                  op0=ALU.mult, op1=ALU.add)
            last.then_inc(conv_ready, 1)
            dve.wait_ge(gate_e, 1)
            link(V.tensor_scalar(gflat, gflat, 0.5, 0.5, ALU.mult, ALU.add))
            dve.wait_ge(softp_ready, 1)
            link(V.scalar_tensor_tensor(out=rows[:, 1], in0=rows[:, 1], scalar=0.0, in1=rows[:, 3], op0=ALU.min,
                                        op1=ALU.subtract))
            link(V.tensor_tensor_scan(rows[:, 4], ones[0:HM], rows[:, 1], 0.0, ALU.mult, ALU.add))
            link(V.tensor_tensor(rows[:, 5], rows[:, 0], rows[:, 4], ALU.subtract))
            link(V.tensor_tensor_scan(mrow, ones[0:HM], rows[:, 5], 0.0, ALU.mult, ALU.max))
            V.tensor_tensor(rows[:, 7], rows[:, 4], mrow, ALU.add).then_inc(rows_ready, 1)
            dve.wait_ge(silu_e, 1)
            link(V.tensor_scalar(r_xc, r_xc, 0.5, 0.5, ALU.mult, ALU.add))
            V.tensor_tensor(r_xc, r_xc, r_tmp, ALU.mult).then_inc(xc_ready, 1)
            for g in range(2):
                name = ("cmpA", "cmpB")[g]
                filled_of(dve, name)
                for kind in range(2):
                    a = 32 * (2 * g + kind)
                    last = V.tensor_copy(hid_rows[a:a + NCMP], bank(name)[a:a + NCMP, 0:P])
                drain(name, last)
            gained("te1", memT, R_MEM, 1)
            gained("te3", memT, R_MEM, 3)
            filled_of(dve, "cmpT")
            drain("cmpT", V.tensor_copy(hidT, bank("cmpT")[:, 0:P]))
            drained_of(dve, "cmpT")
            link(V.tensor_tensor(hid2, hidT, hidT, ALU.mult))
            link(V.tensor_scalar(hid2, hid2, 0.044715, 1.0, ALU.mult, ALU.add))
            V.tensor_tensor(hid2, hid2, hidT, ALU.mult).then_inc(gelu_in, 1)
            dve.wait_ge(gelu_e, 1)
            link(V.tensor_scalar(hid2, hid2, 0.5, 0.5, ALU.mult, ALU.add))
            V.tensor_tensor(gelT.rearrange("p g k j -> p (g k j)"), hidT, hid2, ALU.mult).then_inc(gelu_done, 1)
            filled_of(dve, "cmp2")
            V.tensor_copy(kcT[:, :, 0:NCMP], bank("cmp2")[:, 0:2 * CW].rearrange("p (g j) -> p g j", g=2)[:, :, 0:NCMP])
            drain("cmp2", V.tensor_copy(vc[0:NCMP], bank("cmp2")[0:NCMP, 2 * CW:2 * CW + P]
                                        .rearrange("p (g d) -> p g d", g=2)))
            for g in range(2):
                name = ("csA", "csB")[g]
                filled_of(dve, name)
                for t in range(TT):
                    s = bank(name)[:, t * PAIRS * CW:(t + 1) * PAIRS * CW].rearrange("p (c j) -> p c j", j=CW)
                    m = rmaskc[:, t, 0:NCMP].unsqueeze(1).broadcast_to([P, PAIRS, NCMP])
                    last = V.scalar_tensor_tensor(out=pcmp[:, t].rearrange("p (c e) j -> p c e j", e=2)[:, :, g, 0:NCMP],
                                                  in0=s[:, :, 0:NCMP], scalar=float(DA) ** -0.5, in1=m,
                                                  op0=ALU.mult, op1=ALU.add)
                drain(name, last)
            drained_of(dve, "csB")
            pflat = pcmp[:].rearrange("p t h j -> p (t h) j")
            valid = pflat[:, :, 0:NCMP]
            link(V.tensor_reduce(cst, valid, AX.X, ALU.max))
            V.tensor_tensor(valid, valid, cst.unsqueeze(2).broadcast_to([P, TT * HA, NCMP]), ALU.subtract)\
                .then_inc(cm_in, 1)
            dve.wait_ge(cm_e, 1)
            link(V.tensor_reduce(cst, valid, AX.X, ALU.add))
            link(V.reciprocal(cst, cst))
            link(V.tensor_tensor(cst.rearrange("p (t h) -> p t h", t=TT), cst.rearrange("p (t h) -> p t h", t=TT),
                                 gates[:, :, :, 0], ALU.mult))
            link(V.tensor_tensor(valid, valid, cst.unsqueeze(2).broadcast_to([P, TT * HA, NCMP]), ALU.mult))
            for t in range(TT):
                last = V.tensor_tensor(pcmp[:, t, :, 0:NCMP], pcmp[:, t, :, 0:NCMP],
                                       mmaskc[:, t, 0:NCMP].unsqueeze(1).broadcast_to([P, HA, NCMP]), ALU.mult)
            last.then_inc(cm_done, 1)
            filled_of(dve, "mt")
            drain("mt", V.tensor_copy(cmcol, bank("mt")[:, 0:16].rearrange("p (k t h) -> p k t h", k=2, t=TT)))
            drained_of(dve, "mt")
            drained_of(dve, "op0")
            drained_of(dve, "op1")
            link(V.tensor_scalar(r_so[:], r_so[:], 0.5, 0.5, ALU.mult, ALU.add))

            def filler(name):
                kind, n = name[:2], int(name[2])
                if kind == "vx":
                    filled_of(dve, name)
                    drain(name, V.tensor_copy(vx[:, n % 2, (n // 2) * 512:(n // 2) * 512 + 512], bank(name)))

            for h in range(HA + 1):
                if h >= 1:
                    m = h - 1
                    filled_of(dve, f"tb{m}")
                    V.tensor_copy(pT[:, m % 2, 1, 0:T], bank(f"tb{m}")[:, 0:T])
                    drain(f"tb{m}", V.tensor_copy(pT[0:NCMP, m % 2, 1, T:2 * T], bank(f"tb{m}")[0:NCMP, T:2 * T]))
                if h < HA:
                    for t in range(TT):
                        name, n = f"sc{h}_{t}", P * (t + 1)
                        filled_of(dve, name)
                        m = causal[:, T - n:T].unsqueeze(1).broadcast_to([P, 2, n])
                        drain(name, V.scalar_tensor_tensor(
                            out=pr[:, t, :, 0:n], in0=bank(name)[:, 0:2 * n].rearrange("p (b n) -> p b n", b=2),
                            scalar=float(DA) ** -0.5, in1=m, op0=ALU.mult, op1=ALU.add))
                        drained_of(dve, name)
                        V.tensor_reduce(nmax[:, 2 * t:2 * t + 2], pr[:, t, :, 0:n], AX.X, ALU.max, negate=True)\
                            .then_inc(s_max, 1)
                    for name in filler_names(h)[:1]:
                        filler(name)
                    for t in range(TT):
                        dve.wait_ge(s_exp, 2 * h + t + 1)
                        link(V.reciprocal(rinv[:, 2 * t:2 * t + 2], rsum[:, 2 * t:2 * t + 2]))
                        V.tensor_tensor(fac[:, 2 * t:2 * t + 2], rinv[:, 2 * t:2 * t + 2], gates[:, t, h, 1:3],
                                        ALU.mult).then_inc(s_fac, 1)
                if h == 1:
                    for t in range(TT):
                        filled_of(dve, f"mv{t}")
                        drain(f"mv{t}", V.tensor_copy(mv[:, t, :, 0:DM], bank(f"mv{t}").rearrange("p (h e) -> p h e", h=HM)))
                if 3 <= h <= 6:
                    m = h - 3
                    name = f"mn{m}"
                    filled_of(dve, name)
                    num = bank(name).rearrange("p (t e) -> p t e", t=TT)
                    link(V.tensor_scalar(den[:, 0:2].unsqueeze(2), num[:, :, DM:DM + 1], -1.0, None, ALU.mult))
                    link(V.tensor_tensor(den[:, 0:2].unsqueeze(2), num[:, :, DM:DM + 1], den[:, 0:2].unsqueeze(2), ALU.max))
                    dve.wait_ge(em_done, 1)
                    link(V.tensor_tensor(den[:, 0:2], den[:, 0:2], emcol[:, :, m], ALU.max))
                    link(V.reciprocal(den[:, 2:4], den[:, 0:2]))
                    for t in range(TT):
                        last = V.scalar_tensor_tensor(out=hs[:, t, m], in0=num[:, t, 0:DM],
                                                      scalar=den[:, 2 + t:3 + t], in1=so[:, t, m * DM:(m + 1) * DM],
                                                      op0=ALU.mult, op1=ALU.mult,
                                                      accum_out=hsum[:, t * HM + m:t * HM + m + 1])
                    drain(name, last)
                if 2 <= h <= 5:
                    m = h - 2
                    name = f"mb{m}"
                    filled_of(dve, name)
                    if m >= 2:
                        filled_of(dve, f"mn{m - 2}")
                    V.tensor_scalar(dm[:, m % 2, 0], bank(name)[:, 0:T], cmcol[:, 0, 0, m:m + 1], 0.0,
                                    ALU.subtract, ALU.max)
                    drain(name, V.tensor_scalar(dm[:, m % 2, 1, 0:P], bank(name)[:, P:T], cmcol[:, 0, 1, m:m + 1],
                                                0.0, ALU.subtract, ALU.max))
                    name = f"ms{m}"
                    filled_of(dve, name)
                    dve.wait_ge(dm_e, m + 1)
                    link(V.tensor_tensor(dm[:, m % 2, :, 0:P], dm[:, m % 2, :, 0:P],
                                         upper[:].unsqueeze(1).broadcast_to([P, 2, P]), ALU.mult))
                    flat = r_dm[:, (m % 2) * 512:(m % 2) * 512 + 384]
                    drain(name, V.tensor_tensor(flat, flat, bank(name)[:, 0:384], ALU.mult))
                if h == 6:
                    for m in range(HM):
                        drained_of(dve, f"mn{m}")
                    link(V.tensor_scalar(hsum, hsum, 1.0 / DM, None, ALU.mult))
                    h3 = hs[:].rearrange("p t h e -> p (t h) e")
                    link(V.tensor_tensor(h3, h3, hsum.unsqueeze(2).broadcast_to([P, TT * HM, DM]), ALU.subtract))
                    sq = r_xm.rearrange("p (h e) -> p h e", e=DM)
                    link(V.tensor_tensor(sq, h3, h3, ALU.mult))
                    link(V.tensor_reduce(lnm, sq, AX.X, ALU.add))
                    V.tensor_scalar(lnm, lnm, 1.0 / DM, EPS, ALU.mult, ALU.add).then_inc(var_ready, 1)
                    for m in range(HM):
                        V.tensor_scalar(ybT[:, m], xc[:, m], col(R_SKIP + m), None, ALU.mult)
                if h == 7:
                    dve.wait_ge(lstd_ready, 1)
                    link(V.reciprocal(hst, hst))
                    V.tensor_tensor(h3, h3, hst.unsqueeze(2).broadcast_to([P, TT * HM, DM]), ALU.mult)\
                        .then_inc(hn_ready, 1)
                if h < HA - 1:
                    for name in filler_names(h)[1:]:
                        filler(name)
            for n in range(2):
                filled_of(dve, f"ty{n}")
                for j in range(2):
                    m = 2 * n + j
                    last = V.scalar_tensor_tensor(out=ybT[:, m], in0=bank(f"ty{n}")[:, j * T:(j + 1) * T],
                                                  scalar=col(R_GAIN + m), in1=ybT[:, m], op0=ALU.mult, op1=ALU.add)
                drain(f"ty{n}", last)
            for name in filler_names(HA - 1)[1:]:
                filler(name)
            for n in range(4):
                for name, g in ((f"ua{n}", sga), (f"ub{n}", sgb)):
                    filled_of(dve, name)
                    drained_of(dve, f"g{name[1]}{n}")
                    drain(name, V.scalar_tensor_tensor(
                        out=g[:, 2 * n:2 * n + 2], in0=g[:, 2 * n:2 * n + 2], scalar=1.0,
                        in1=bank(name).rearrange("p (c t) -> p c t", c=2), op0=ALU.add, op1=ALU.mult))
                drained_of(dve, f"ub{n}")
                V.tensor_tensor(sga[:, 2 * n:2 * n + 2], sga[:, 2 * n:2 * n + 2], sgb[:, 2 * n:2 * n + 2], ALU.add)\
                    .then_inc(merged_ready, 1)

            def residual(prefix, n, t, scale):
                name = f"{prefix}{n}_{t}"
                filled_of(dve, name)
                xv = x_tok[:, t, n * 512:(n + 1) * 512]
                drain(name, V.scalar_tensor_tensor(out=xv, in0=bank(name), scalar=scale, in1=xv, op0=ALU.mult,
                                                   op1=ALU.add))

            def residual_and_turned(prefix, scale, turned, g0):
                for n, t in ((0, 0), (0, 1), (1, 0)):
                    residual(prefix, n, t, scale)
                gained(f"{turned}0", hT, g0, 0)
                gained(f"{turned}1", hT, g0, 1)
                residual(prefix, 1, 1, scale)
                gained(f"{turned}2", hT, g0, 2)
                gained(f"{turned}3", hT, g0, 3)

            dve.wait_ge(x_again, 16)
            residual_and_turned("om", 0.5, "tx", R_X)
            norm(2, None, None)
            link(V.tensor_scalar(rs16, rstd[:, 4:6], float(2 * P) ** -0.5, None, ALU.mult))

            def cross_max(h):
                name = f"sx{h}"
                j = slice(2 * h, 2 * h + 2)
                filled_of(dve, name)
                link(V.tensor_reduce(nmaxx[:, j], bank(name).rearrange("p (t m) -> p t m", t=TT), AX.X, ALU.max,
                                     negate=True))
                V.tensor_tensor(nmaxx[:, j], nmaxx[:, j], rs16, ALU.mult).then_inc(cx_max, 1)

            def cross_inv(h):
                drained_of(dve, f"sx{h}")
                V.reciprocal(rinvx[:, 2 * h:2 * h + 2], rsumx[:, 2 * h:2 * h + 2]).then_inc(cx_inv, 1)

            def cross_turned(h):
                filled_of(dve, f"pt{h}")
                drain(f"pt{h}", V.tensor_copy(pxT[:, h % 2], bank(f"pt{h}").rearrange("p (m t) -> p m t", m=2)))

            cross_max(0)
            cross_inv(0)
            cross_max(1)
            cross_inv(1)
            cross_max(2)
            cross_inv(2)
            cross_turned(0)
            cross_max(3)
            cross_inv(3)
            for h in range(1, HX):
                if h >= 2:
                    filled_of(dve, f"ox{h - 2}")
                cross_turned(h)
            residual_and_turned("ro", 1.0, "tf", R_FFN)
            norm(3, None, None)
            dve.wait_ge(consts, 2)
            filled_of(dve, "rt")
            for t in range(TT):
                last = V.scalar_tensor_tensor(out=lg[:, t], in0=bank("rt")[:, t * NE:(t + 1) * NE],
                                              scalar=rstd[:, 6 + t:7 + t], in1=brow, op0=ALU.mult, op1=ALU.add)
            drain("rt", last)
            drained_of(dve, "rt")
            for t in range(TT):
                last = V.max(top[:, t], lg[:, t])
            link(last)
            V.tensor_scalar(negtop.unsqueeze(2), top[:, :, 0:1], -1.0, None, ALU.mult).then_inc(r_top, 1)
            for t in range(TT):
                V.tensor_scalar(lge[:, t], lg[:, t], top[:, t, 3:4], None, ALU.is_equal)
                last = V.tensor_scalar(gate[:, t], lg[:, t], top[:, t, 3:4], None, ALU.is_gt)
            link(last)
            for t in range(TT):
                V.tensor_tensor_scan(lgm[:, t], ones[:, 0:NE], lge[:, t], 0.0, ALU.mult, ALU.add)
                last = V.tensor_reduce(gsum[:, t:t + 1], gate[:, t], AX.X, ALU.add)
            link(last)
            link(V.tensor_scalar(gsum[:, 0:2], gsum[:, 0:2], -1.0, float(TOPK), ALU.mult, ALU.add))
            for t in range(TT):
                last = V.scalar_tensor_tensor(out=lge[:, t], in0=lgm[:, t], scalar=gsum[:, t:t + 1], in1=lge[:, t],
                                              op0=ALU.is_le, op1=ALU.mult)
            link(last)
            link(V.tensor_tensor(mask, gate, lge, ALU.add))
            dve.wait_ge(r_exp, 1)
            link(V.tensor_tensor(gexp, gexp, mask, ALU.mult))
            link(V.tensor_reduce(gsum[:, 0:2], gexp, AX.X, ALU.add))
            link(V.reciprocal(gsum[:, 2:4], gsum[:, 0:2]))
            V.tensor_tensor(gate, gexp, gsum[:, 2:4].unsqueeze(2).broadcast_to([P, TT, NE]), ALU.mult)\
                .then_inc(r_gate, 1)
            dve.wait_ge(r_gate, 1)
            V.tensor_copy(gate_b[:, :, 0:NE], gate)
            filled_of(dve, "slot")
            own = pos_b[:, :, 0:NE]
            link(V.scalar_tensor_tensor(out=own, in0=bank("slot")[:, 0:2 * NE].rearrange("p (t e) -> p t e", t=TT),
                                        scalar=1024.0, in1=mask, op0=ALU.add, op1=ALU.mult))
            drain("slot", V.tensor_scalar(own, own, -1024.0, None, ALU.add))
            drained_of(dve, "slot")

            def pick_expert(i):
                V.tensor_copy(cur, blksel[:, bass.ds(i, 1)].broadcast_to([NE, SLOTS])).then_inc(cur_ready, 1)

            def find_slots(i):
                for t in range(TT):
                    last = V.tensor_scalar(place[:, t], iota_s[:, 0:SLOTS], pos_b[:, t, bass.ds(i, 1)],
                                           rstd[:, 6 + t:7 + t], ALU.is_equal, ALU.mult)
                last.then_inc(place_ready, 1)

            def take_tokens(i):
                dve.wait_ge(gathered, i + 1)
                V.tensor_tensor(xg, ps[:, XBK, :].rearrange("p (c s) -> p c s", c=C), gain_ffn, ALU.mult)\
                    .then_inc(xg_ready, 1)

            def further_blocks():
                filled_of(dve, "pos")
                link(V.tensor_copy(mT, bank("pos")[0:NE, T:2 * T]))
                link(V.scalar_tensor_tensor(out=posT, in0=bank("pos")[0:NE, 0:T], scalar=1024.0, in1=mT, op0=ALU.add,
                                            op1=ALU.mult))
                drain("pos", V.tensor_scalar(posT, posT, -1024.0, None, ALU.add))
                filled_of(dve, "cnt")
                V.tensor_copy(gateT, bank("cnt")[0:NE, 0:T])
                drain("cnt", V.tensor_copy(cnt, bank("cnt")[0:NE, T:T + 1]))
                drained_of(dve, "cnt")
                for c in range(MORE):
                    last = V.tensor_scalar(ovf[:, c:c + 1], cnt, float(SLOTS * (c + 1)), None, ALU.is_gt)
                link(last)
                link(V.memset(ovs, 0.0))
                link(V.tensor_copy(ovs[:, 1:2], ovf[:, 0:1]))
                V.tensor_tensor(ovs[:, 2:3], ovf[:, 0:1], ovf[:, 1:2], ALU.add).then_inc(r_ovf, 1)
                filled_of(dve, "rank")
                drain("rank", V.tensor_copy(rank, bank("rank")[0:NE, 0:MORE]))
                drained_of(dve, "rank")
                for c in range(MORE):
                    last = V.tensor_scalar(sel3[:, c], idx16[0:NE], rank[:, c:c + 1], ovf[:, c:c + 1], ALU.is_equal, ALU.mult)
                link(last)
                link(V.tensor_tensor(blksel[:, more], sel3[:, 0], sel3[:, 1], ALU.add))
                link(V.tensor_tensor(blksel[:, more], blksel[:, more], sel3[:, 2], ALU.add))
                link(V.tensor_scalar(blkoff[:, more], sel3[:, 0], -float(SLOTS), None, ALU.mult))
                link(V.scalar_tensor_tensor(out=blkoff[:, more], in0=sel3[:, 1], scalar=-float(2 * SLOTS),
                                            in1=blkoff[:, more], op0=ALU.mult, op1=ALU.add))
                V.scalar_tensor_tensor(out=blkoff[:, more], in0=sel3[:, 2], scalar=-float(3 * SLOTS),
                                       in1=blkoff[:, more], op0=ALU.mult, op1=ALU.add).then_inc(r_sel, 1)
                filled_of(dve, "meta")
                link(V.tensor_copy(metas[:, 1:17], bank("meta")[0:1, 0:16]))
                link(V.tensor_reduce(metas[:, 0:1], bank("meta")[0:1, 16:16 + MORE], AX.X, ALU.add))
                link(V.tensor_scalar(metas[:, 0:1], metas[:, 0:1], float(NE), None, ALU.add))
                drain("meta", V.tensor_copy(cnt_i[:, 0:17], metas[:, 0:17]))
                filled_of(dve, "blk")
                V.tensor_copy(pos_b[:, :, more], bank("blk")[:, 0:32].rearrange("p (t b) -> p t b", t=TT))
                drain("blk", V.tensor_copy(gate_b[:, :, more], bank("blk")[:, 32:64].rearrange("p (t b) -> p t b", t=TT)))

            def block_steps(i):
                if not is_block(i, 0):
                    dve.wait_ge(scat_ready, i)
                for t in range(TT):
                    last = V.tensor_scalar(placeg[:, t], iota_s, pos_b[:, t, bass.ds(i, 1)],
                                           gate_b[:, t, bass.ds(i, 1)], ALU.is_equal, ALU.mult)
                last.then_inc(placeg_ready, 1)
                if is_block(i, 0):
                    take_tokens(0)
                find_slots(i + 1)
                if is_block(i, 0):
                    further_blocks()
                dve.wait_ge(freed[eslot["gu3"]], i + 1)
                V.tensor_scalar(gact, ps[:, GBK, :], 7.0, None, ALU.min).then_inc(g_limited, 1)
                V.tensor_scalar(uact, ps[:, UBK, :], -7.0, 7.0, ALU.max, ALU.min).then_inc(g_chain, 1)
                dve.wait_ge(g_limited, i + 1)
                dve.wait_ge(g_chain, i * 2 + 1)
                V.scalar_tensor_tensor(out=uact, in0=uact, scalar=1.0, in1=gact, op0=ALU.add, op1=ALU.mult)\
                    .then_inc(g_chain, 1)
                dve.wait_ge(g_chain, i * 2 + 2)
                dve.wait_ge(sig_done, i + 1)
                V.tensor_tensor(hact, uact, sig, ALU.mult).then_inc(h_ready, 1)
                pick_expert(i + 1)
                dve.wait_ge(ht_done, i + 1)
                V.tensor_copy(hactT.rearrange("p c n s -> p (c n s)"), ps[:, ZBK, :]).then_inc(hT_ready, 1)
                take_tokens(i + 1)

            find_slots(0)
            pick_expert(0)
            block_steps(0)
            nblk = dve.value_load(cnt_i[0:1, 0:1], min_val=NE, max_val=NBLK)
            with dve.Fori(1, nblk) as i:
                block_steps(i)
            dve.wait_ge(fin_sq, 2)
            dve.wait_ge(gfin_loaded, 16)
            V.tensor_scalar(msq[:, 0:2], ss[:, 0:2], 1.0 / D, EPS, ALU.mult, ALU.add).then_inc(fin_v, 1)
            dve.wait_ge(fin_std, 1)
            V.reciprocal(rstd[:, 0:2], std[:, 0:2]).then_inc(fin_v, 1)
            dve.wait_ge(fin_v, 2)
            for t in range(TT):
                V.scalar_tensor_tensor(out=x_tok[:, t], in0=ps[:, YB + 2 * t:YB + 2 * t + 2, :]
                                       .rearrange("p b n -> p (b n)"), scalar=rstd[:, t:t + 1], in1=gfin,
                                       op0=ALU.mult, op1=ALU.mult).then_inc(out_ready, 1)


_INS = ["x", "mem", "g_mix", "w_in", "pe_cmp_k", "pe_cmp_v", "w_phi1_k", "w_phi2_k", "w_phi1_v", "w_phi2_v",
        "w_conv", "b_conv", "w_q_m", "w_k_m", "w_v_m", "b_i", "b_f", "mh_gain", "skip_m", "w_up_a", "w_up_b",
        "w_o_mix", "g_x", "g_mem", "w_q_x", "w_k_x", "w_v_x", "w_o_x", "g_ffn", "w_router", "b_router",
        "w_gu", "b_gu", "w_down", "b_down", "g_final"]


def kernel(**inputs):
    import numpy as _np
    import concourse.bacc as _bacc
    from concourse import mybir as _mybir
    from concourse.bass_utils import run_bass_kernel_spmd as _run

    nc = _bacc.Bacc("TRN2", target_bir_lowering=False, num_devices=1)
    arrays, args = {}, {}
    for name in _INS:
        a = _np.ascontiguousarray(inputs[name])
        arrays[f"in_{name}_dram"] = a
        args[name] = nc.dram_tensor(f"in_{name}_dram", a.shape, _mybir.dt.from_np(a.dtype), kind="ExternalInput").ap()
    out = nc.dram_tensor("out_0_dram", (1, T, D), F32, kind="ExternalOutput").ap()
    program(nc, args, out)
    r = _run(nc, [arrays], core_ids=[0])
    return r.results[0]["out_0_dram"]
```
